# Optimizing a Trainium2 kernel written in Bass

```python
import math
import jax, jax.numpy as jnp
from jax import lax
import numpy as np

D_MODEL = 1024
BATCH = 1
SEQ = 256
DEPTH = 1

N_META = 16
BLOCK_Q = 128
EPS = 1e-6

MLA_HEADS = 8
MLA_Q_RANK = 256
MLA_KV_RANK = 256
MLA_NOPE_DIM = 64
MLA_ROPE_DIM = 32
MLA_V_DIM = 64
MLA_QK_DIM = MLA_NOPE_DIM + MLA_ROPE_DIM
ROPE_THETA = 10000.0

DIFF_HEADS = 4
DIFF_HEAD_DIM = 64
DIFF_V_DIM = 2 * DIFF_HEAD_DIM
DIFF_QK_WIDTH = DIFF_HEADS * 2 * DIFF_HEAD_DIM
DIFF_V_WIDTH = DIFF_HEADS * DIFF_V_DIM

NUM_BUCKETS = 32
MAX_DISTANCE = 128

_S1 = MLA_Q_RANK
_S2 = _S1 + MLA_KV_RANK
_S3 = _S2 + MLA_ROPE_DIM
_S4 = _S3 + DIFF_QK_WIDTH
_S5 = _S4 + DIFF_QK_WIDTH
IN_WIDTH = _S5 + DIFF_V_WIDTH
IN_SPLITS = (_S1, _S2, _S3, _S4, _S5)
MIX_WIDTH = MLA_HEADS * MLA_V_DIM + DIFF_V_WIDTH

PEER_HEADS = 8
PEER_N_KEYS = 128
PEER_N_EXPERTS = PEER_N_KEYS * PEER_N_KEYS
PEER_TOPK = 16
PEER_QUERY_DIM = 256
PEER_SUBKEY_DIM = PEER_QUERY_DIM // 2
PEER_CHUNK = 128


def _rms_norm(x, gain):
    xf = x.astype(jnp.float32)
    y = xf * lax.rsqrt(jnp.mean(xf * xf, axis=-1, keepdims=True) + EPS)
    return (y * gain.astype(jnp.float32)).astype(x.dtype)

def _rope(t, pos):
    half = t.shape[-1] // 2
    inv_freq = ROPE_THETA ** (-jnp.arange(half, dtype=jnp.float32) / half)
    ang = pos.astype(jnp.float32)[:, None] * inv_freq[None, :]
    cos = jnp.cos(ang)[:, None, :].astype(t.dtype)
    sin = jnp.sin(ang)[:, None, :].astype(t.dtype)
    t1, t2 = t[..., :half], t[..., half:]
    return jnp.concatenate([t1 * cos - t2 * sin, t1 * sin + t2 * cos], axis=-1)

def _t5_bucket(dist):
    n = jnp.maximum(dist, 0)
    max_exact = NUM_BUCKETS // 2
    nf = jnp.maximum(n, 1).astype(jnp.float32)
    large = max_exact + (jnp.log(nf / max_exact) / math.log(MAX_DISTANCE / max_exact)
                         * (NUM_BUCKETS - max_exact)).astype(jnp.int32)
    large = jnp.minimum(large, NUM_BUCKETS - 1)
    return jnp.where(n < max_exact, n, large)

def _causal_softmax(logits, q_pos, k_pos):
    mask = k_pos[None, :] <= q_pos[:, None]
    logits = jnp.where(mask, logits.astype(jnp.float32), -1e30)
    return jax.nn.softmax(logits, axis=-1)

def _to_blocks(t):
    b, l = t.shape[0], t.shape[1]
    t = t.reshape((b, l // BLOCK_Q, BLOCK_Q) + t.shape[2:])
    return jnp.moveaxis(t, 1, 0)

def _from_blocks(t):
    t = jnp.moveaxis(t, 0, 1)
    return t.reshape((t.shape[0], t.shape[1] * t.shape[2]) + t.shape[3:])

def _mla(c_q, c_kv, k_rope, q_norm, w_uq, kv_norm, w_ukv, qk_norm_q, qk_norm_k, pos):
    b, l, _ = c_q.shape
    q = (_rms_norm(c_q, q_norm) @ w_uq).reshape(b, l, MLA_HEADS, MLA_QK_DIM)
    kv = (_rms_norm(c_kv, kv_norm) @ w_ukv).reshape(b, l, MLA_HEADS, MLA_NOPE_DIM + MLA_V_DIM)
    k_nope, v = kv[..., :MLA_NOPE_DIM], kv[..., MLA_NOPE_DIM:]
    k_r = jnp.broadcast_to(k_rope[:, :, None, :], (b, l, MLA_HEADS, MLA_ROPE_DIM))
    k = jnp.concatenate([k_nope, k_r], axis=-1)
    q = _rms_norm(q, qk_norm_q)
    k = _rms_norm(k, qk_norm_k)
    q = jnp.concatenate([q[..., :MLA_NOPE_DIM], _rope(q[..., MLA_NOPE_DIM:], pos)], axis=-1)
    k = jnp.concatenate([k[..., :MLA_NOPE_DIM], _rope(k[..., MLA_NOPE_DIM:], pos)], axis=-1)
    scale = MLA_QK_DIM ** -0.5

    def block(args):
        q_start, qb = args
        q_pos = q_start + jnp.arange(BLOCK_Q, dtype=jnp.int32)
        s = jnp.einsum('bqhd,bkhd->bhqk', qb, k) * scale
        p = _causal_softmax(s, q_pos, pos)
        return jnp.einsum('bhqk,bkhd->bqhd', p.astype(v.dtype), v)

    starts = jnp.arange(l // BLOCK_Q, dtype=jnp.int32) * BLOCK_Q
    out = _from_blocks(lax.map(block, (starts, _to_blocks(q))))
    return out.reshape(b, l, MLA_HEADS * MLA_V_DIM)

def _diff_attn(q, k, v, q_norm, k_norm, lam_q1, lam_k1, lam_q2, lam_k2, subln, rel_bias, pos, lambda_init):
    b, l, _ = q.shape
    q = _rms_norm(q.reshape(b, l, DIFF_HEADS, 2, DIFF_HEAD_DIM), q_norm)
    k = _rms_norm(k.reshape(b, l, DIFF_HEADS, 2, DIFF_HEAD_DIM), k_norm)
    v = v.reshape(b, l, DIFF_HEADS, DIFF_V_DIM)
    lam = (jnp.exp(jnp.sum(lam_q1.astype(jnp.float32) * lam_k1.astype(jnp.float32)))
           - jnp.exp(jnp.sum(lam_q2.astype(jnp.float32) * lam_k2.astype(jnp.float32)))
           + lambda_init)
    k1, k2 = k[..., 0, :], k[..., 1, :]
    bias_table = rel_bias.astype(jnp.float32)
    scale = DIFF_HEAD_DIM ** -0.5

    def block(args):
        q_start, qb = args
        q_pos = q_start + jnp.arange(BLOCK_Q, dtype=jnp.int32)
        bias = bias_table[_t5_bucket(q_pos[:, None] - pos[None, :])]
        bias = jnp.transpose(bias, (2, 0, 1))[None]
        s1 = jnp.einsum('bqhd,bkhd->bhqk', qb[..., 0, :], k1).astype(jnp.float32) * scale + bias
        s2 = jnp.einsum('bqhd,bkhd->bhqk', qb[..., 1, :], k2).astype(jnp.float32) * scale + bias
        a = _causal_softmax(s1, q_pos, pos) - lam * _causal_softmax(s2, q_pos, pos)
        return jnp.einsum('bhqk,bkhd->bqhd', a.astype(v.dtype), v)

    starts = jnp.arange(l // BLOCK_Q, dtype=jnp.int32) * BLOCK_Q
    out = _from_blocks(lax.map(block, (starts, _to_blocks(q))))
    out = _rms_norm(out, subln) * (1.0 - lambda_init)
    return out.reshape(b, l, DIFF_V_WIDTH)

def _peer(h, w_query, sub_keys, u, v):
    b, l, d = h.shape
    tokens = h.reshape(b * l // PEER_CHUNK, PEER_CHUNK, d)

    def chunk(xc):
        q = (xc @ w_query).reshape(PEER_CHUNK, PEER_HEADS, 2, PEER_SUBKEY_DIM)
        s = jnp.einsum('chpd,hpnd->chpn', q, sub_keys).astype(jnp.float32)
        s1, i1 = lax.top_k(s[:, :, 0], PEER_TOPK)
        s2, i2 = lax.top_k(s[:, :, 1], PEER_TOPK)
        cand = (s1[..., :, None] + s2[..., None, :]).reshape(PEER_CHUNK, PEER_HEADS, PEER_TOPK * PEER_TOPK)
        best, flat = lax.top_k(cand, PEER_TOPK)
        e1 = jnp.take_along_axis(i1, flat // PEER_TOPK, axis=-1)
        e2 = jnp.take_along_axis(i2, flat % PEER_TOPK, axis=-1)
        experts = e1 * PEER_N_KEYS + e2
        g = jax.nn.softmax(best, axis=-1)
        u_sel = jnp.take(u, experts, axis=0)
        act = jax.nn.gelu(jnp.einsum('cd,chkd->chk', xc, u_sel).astype(jnp.float32), approximate=False)
        v_sel = jnp.take(v, experts, axis=0)
        return jnp.einsum('chk,chkd->cd', (g * act).astype(v.dtype), v_sel)

    return lax.map(chunk, tokens).reshape(b, l, d)

def first_inputs(seed: int = 0) -> dict:
    key = jax.random.key(seed)
    ks = jax.random.split(key, 24)
    f32 = jnp.float32

    def nrm(k, shape, scale):
        return jax.random.normal(k, shape, f32) * scale

    def gain(k, shape):
        return 1.0 + 0.02 * jax.random.normal(k, shape, f32)

    return {
        "x": nrm(ks[0], (BATCH, SEQ, D_MODEL), 1.0),
        "meta_tokens": nrm(ks[1], (N_META, D_MODEL), 1.0),
        "rel_bias": nrm(ks[2], (NUM_BUCKETS, DIFF_HEADS), 0.5),
        "attn_norm": gain(ks[3], (DEPTH, D_MODEL)),
        "w_in": nrm(ks[4], (DEPTH, D_MODEL, IN_WIDTH), D_MODEL ** -0.5),
        "mla_q_norm": gain(ks[5], (DEPTH, MLA_Q_RANK)),
        "mla_w_uq": nrm(ks[6], (DEPTH, MLA_Q_RANK, MLA_HEADS * MLA_QK_DIM), MLA_Q_RANK ** -0.5),
        "mla_kv_norm": gain(ks[7], (DEPTH, MLA_KV_RANK)),
        "mla_w_ukv": nrm(ks[8], (DEPTH, MLA_KV_RANK, MLA_HEADS * (MLA_NOPE_DIM + MLA_V_DIM)), MLA_KV_RANK ** -0.5),
        "mla_qk_norm_q": gain(ks[9], (DEPTH, MLA_QK_DIM)),
        "mla_qk_norm_k": gain(ks[10], (DEPTH, MLA_QK_DIM)),
        "diff_q_norm": gain(ks[11], (DEPTH, DIFF_HEAD_DIM)),
        "diff_k_norm": gain(ks[12], (DEPTH, DIFF_HEAD_DIM)),
        "diff_lambda_q1": nrm(ks[13], (DEPTH, DIFF_HEAD_DIM), 0.1),
        "diff_lambda_k1": nrm(ks[14], (DEPTH, DIFF_HEAD_DIM), 0.1),
        "diff_lambda_q2": nrm(ks[15], (DEPTH, DIFF_HEAD_DIM), 0.1),
        "diff_lambda_k2": nrm(ks[16], (DEPTH, DIFF_HEAD_DIM), 0.1),
        "diff_subln": gain(ks[17], (DEPTH, DIFF_V_DIM)),
        "w_out": nrm(ks[18], (DEPTH, MIX_WIDTH, D_MODEL), MIX_WIDTH ** -0.5),
        "ffn_norm": gain(ks[19], (DEPTH, D_MODEL)),
        "peer_w_query": nrm(ks[20], (DEPTH, D_MODEL, PEER_HEADS * PEER_QUERY_DIM), D_MODEL ** -0.5),
        "peer_sub_keys": nrm(ks[21], (DEPTH, PEER_HEADS, 2, PEER_N_KEYS, PEER_SUBKEY_DIM), PEER_SUBKEY_DIM ** -0.5),
        "peer_u": nrm(ks[22], (DEPTH, PEER_N_EXPERTS, D_MODEL), D_MODEL ** -0.5),
        "peer_v": nrm(ks[23], (DEPTH, PEER_N_EXPERTS, D_MODEL), PEER_HEADS ** -0.5),
    }

def first_block(x, meta_tokens, rel_bias, attn_norm, w_in, mla_q_norm, mla_w_uq, mla_kv_norm, mla_w_ukv,
              mla_qk_norm_q, mla_qk_norm_k, diff_q_norm, diff_k_norm, diff_lambda_q1, diff_lambda_k1,
              diff_lambda_q2, diff_lambda_k2, diff_subln, w_out, ffn_norm, peer_w_query, peer_sub_keys,
              peer_u, peer_v):
    b, s, d = x.shape
    l_real = N_META + s
    l_pad = -(-l_real // BLOCK_Q) * BLOCK_Q
    meta = jnp.broadcast_to(meta_tokens[None].astype(x.dtype), (b, N_META, d))
    h = jnp.concatenate([meta, x, jnp.zeros((b, l_pad - l_real, d), x.dtype)], axis=1)
    pos = jnp.arange(l_pad, dtype=jnp.int32)
    for layer in range(DEPTH):
        lambda_init = 0.8 - 0.6 * math.exp(-0.3 * layer)
        n = _rms_norm(h, attn_norm[layer])
        proj = n @ w_in[layer]
        c_q, c_kv, k_rope, dq, dk, dv = jnp.split(proj, IN_SPLITS, axis=-1)
        y_mla = _mla(c_q, c_kv, k_rope, mla_q_norm[layer], mla_w_uq[layer], mla_kv_norm[layer],
                     mla_w_ukv[layer], mla_qk_norm_q[layer], mla_qk_norm_k[layer], pos)
        y_diff = _diff_attn(dq, dk, dv, diff_q_norm[layer], diff_k_norm[layer], diff_lambda_q1[layer],
                            diff_lambda_k1[layer], diff_lambda_q2[layer], diff_lambda_k2[layer],
                            diff_subln[layer], rel_bias, pos, lambda_init)
        h = h + jnp.concatenate([y_mla, y_diff], axis=-1) @ w_out[layer]
        h = h + _peer(_rms_norm(h, ffn_norm[layer]), peer_w_query[layer], peer_sub_keys[layer],
                      peer_u[layer], peer_v[layer])
    return h[:, N_META:l_real]


MEM_LEN = 256
HEAD_DIM = 64
CONV_CH = D_MODEL // 4
MOBA_WIDTH = D_MODEL // 2
N_MOBA_HEADS = MOBA_WIDTH // HEAD_DIM
GLA_WIDTH = D_MODEL // 4
N_GLA_HEADS = 4
GLA_DV = GLA_WIDTH // N_GLA_HEADS
GLA_DK = GLA_DV // 2
GLA_KEY_WIDTH = N_GLA_HEADS * GLA_DK
GLA_GATE_RANK = 16
GLA_GATE_NORMALIZER = 16.0
GLA_CHUNK = 64
MOBA_BLOCK = 256
MOBA_TOPK = 3
MOBA_QCHUNK = 32
CONV_K = 3
N_XATTN_HEADS = 4
XATTN_WIDTH = N_XATTN_HEADS * HEAD_DIM
D_FF = 2752
IN_SPLITS_2 = (CONV_CH, CONV_CH, CONV_CH,
             MOBA_WIDTH, MOBA_WIDTH, MOBA_WIDTH,
             GLA_KEY_WIDTH, GLA_KEY_WIDTH, GLA_WIDTH, GLA_WIDTH, GLA_GATE_RANK)
IN_PROJ_WIDTH = sum(IN_SPLITS_2)
MIX_WIDTH_2 = CONV_CH + MOBA_WIDTH + GLA_WIDTH


def rmsnorm(x, g):
    xf = x.astype(jnp.float32)
    xf = xf * lax.rsqrt(jnp.mean(xf * xf, axis=-1, keepdims=True) + EPS)
    return xf.astype(x.dtype) * g

def causal_dwconv(u, w, b):
    T = u.shape[1]
    up = jnp.pad(u, ((0, 0), (CONV_K - 1, 0), (0, 0)))
    return sum(up[:, j:j + T] * w[j] for j in range(CONV_K)) + b

def alibi_slopes(n_heads):
    return jnp.asarray(2.0 ** (-8.0 * np.arange(1, n_heads + 1) / n_heads), dtype=jnp.float32)

def moba_attention(q, k, v, slopes):
    Bsz, T, H, hd = q.shape
    nblk = -(-T // MOBA_BLOCK)
    Tp = nblk * MOBA_BLOCK
    pad = ((0, 0), (0, Tp - T), (0, 0), (0, 0))
    q = jnp.pad(q, pad).transpose(0, 2, 1, 3) * (hd ** -0.5)
    k = jnp.pad(k, pad).transpose(0, 2, 1, 3)
    v = jnp.pad(v, pad).transpose(0, 2, 1, 3)
    kb = k.reshape(Bsz, H, nblk, MOBA_BLOCK, hd)
    vb = v.reshape(Bsz, H, nblk, MOBA_BLOCK, hd)
    kmean = jnp.mean(kb.astype(jnp.float32), axis=3)
    gate = jnp.einsum('bhtd,bhnd->bhtn', q.astype(jnp.float32), kmean)
    qblk = jnp.arange(Tp) // MOBA_BLOCK
    past = jnp.arange(nblk)[None, :] < qblk[:, None]
    gate = jnp.where(past, gate, -jnp.inf)
    topk = min(MOBA_TOPK, nblk)
    _, gidx = lax.top_k(gate, topk)
    bi = jnp.arange(Bsz)[:, None, None, None]
    hi = jnp.arange(H)[None, :, None, None]
    sl = slopes[None, :, None, None]

    def chunk(c):
        s0 = c * MOBA_QCHUNK
        qc = lax.dynamic_slice_in_dim(q, s0, MOBA_QCHUNK, axis=2)
        idx = lax.dynamic_slice_in_dim(gidx, s0, MOBA_QCHUNK, axis=2)
        qpos = s0 + jnp.arange(MOBA_QCHUNK)
        valid = jnp.arange(topk)[None, :] < (qpos // MOBA_BLOCK)[:, None]
        ksel = kb[bi, hi, idx]
        vsel = vb[bi, hi, idx]
        kpos_sel = idx[..., None] * MOBA_BLOCK + jnp.arange(MOBA_BLOCK)
        s_sel = jnp.einsum('bhqd,bhqnkd->bhqnk', qc, ksel).astype(jnp.float32)
        s_sel = s_sel - sl[..., None] * (qpos[:, None, None] - kpos_sel).astype(jnp.float32)
        s_sel = jnp.where(valid[None, None, :, :, None], s_sel, -jnp.inf)
        own = s0 // MOBA_BLOCK
        kown = lax.dynamic_slice_in_dim(k, own * MOBA_BLOCK, MOBA_BLOCK, axis=2)
        vown = lax.dynamic_slice_in_dim(v, own * MOBA_BLOCK, MOBA_BLOCK, axis=2)
        kpos_own = own * MOBA_BLOCK + jnp.arange(MOBA_BLOCK)
        rel = (qpos[:, None] - kpos_own[None, :])
        s_own = jnp.einsum('bhqd,bhkd->bhqk', qc, kown).astype(jnp.float32)
        s_own = s_own - sl * rel.astype(jnp.float32)
        s_own = jnp.where(rel >= 0, s_own, -jnp.inf)
        scores = jnp.concatenate(
            [s_sel.reshape(Bsz, H, MOBA_QCHUNK, topk * MOBA_BLOCK), s_own], axis=-1)
        p = jax.nn.softmax(scores, axis=-1).astype(v.dtype)
        p_sel = p[..., :topk * MOBA_BLOCK].reshape(Bsz, H, MOBA_QCHUNK, topk, MOBA_BLOCK)
        p_own = p[..., topk * MOBA_BLOCK:]
        return (jnp.einsum('bhqnk,bhqnkd->bhqd', p_sel, vsel)
                + jnp.einsum('bhqk,bhkd->bhqd', p_own, vown))

    nqc = Tp // MOBA_QCHUNK
    out = lax.map(chunk, jnp.arange(nqc))
    out = out.transpose(1, 0, 3, 2, 4).reshape(Bsz, Tp, H * hd)
    return out[:, :T]

def gla_attention(q, k, v, log_a):
    Bsz, T, H, dk = q.shape
    dv = v.shape[-1]
    n = T // GLA_CHUNK

    def to_chunks(a):
        return a.reshape(Bsz, n, GLA_CHUNK, H, a.shape[-1]).transpose(0, 3, 1, 2, 4)

    q = to_chunks(q) * (dk ** -0.5)
    k = to_chunks(k)
    vc = to_chunks(v)
    b = jnp.cumsum(to_chunks(log_a).astype(jnp.float32), axis=3)
    b_last = b[:, :, :, -1:, :]
    qd = q * jnp.exp(b)
    kd = k * jnp.exp(-b)
    kend = k * jnp.exp(b_last - b)
    causal = jnp.tril(jnp.ones((GLA_CHUNK, GLA_CHUNK), dtype=bool))
    A = jnp.where(causal, jnp.einsum('bhncd,bhnsd->bhncs', qd, kd), 0.0)
    o_intra = jnp.einsum('bhncs,bhnse->bhnce', A, vc)
    U = jnp.einsum('bhnsd,bhnse->bhnde', kend, vc)
    decay = jnp.exp(b_last[:, :, :, 0, :])

    def step(S, xs):
        g, u = xs
        return g[..., None] * S + u, S

    S0 = jnp.zeros((Bsz, H, dk, dv), dtype=U.dtype)
    _, S_prev = lax.scan(step, S0, (decay.transpose(2, 0, 1, 3), U.transpose(2, 0, 1, 3, 4)))
    S_prev = S_prev.transpose(1, 2, 0, 3, 4)
    o_inter = jnp.einsum('bhncd,bhnde->bhnce', qd, S_prev)
    o = (o_intra + o_inter).transpose(0, 2, 3, 1, 4).reshape(Bsz, T, H, dv)
    return o.astype(v.dtype)

def hybrid_mixer(h, w_in, sc_conv_w, sc_conv_b, gla_w_gate, gla_b_gate, gla_norm_g, w_out, slopes):
    Bsz, T, _ = h.shape
    proj = h @ w_in
    points = tuple(int(p) for p in np.cumsum(IN_SPLITS_2)[:-1])
    (c_b, c_c, c_h, m_q, m_k, m_v, g_q, g_k, g_v, g_o, g_lr) = jnp.split(proj, points, axis=-1)
    y_conv = c_b * causal_dwconv(c_c * c_h, sc_conv_w, sc_conv_b)
    hs = lambda a, nh: a.reshape(Bsz, T, nh, -1)
    y_moba = moba_attention(hs(m_q, N_MOBA_HEADS), hs(m_k, N_MOBA_HEADS), hs(m_v, N_MOBA_HEADS), slopes)
    log_a = jax.nn.log_sigmoid((g_lr @ gla_w_gate + gla_b_gate).astype(jnp.float32)) / GLA_GATE_NORMALIZER
    o = gla_attention(hs(g_q, N_GLA_HEADS), hs(g_k, N_GLA_HEADS), hs(g_v, N_GLA_HEADS),
                      hs(log_a, N_GLA_HEADS))
    y_gla = rmsnorm(o, gla_norm_g).reshape(Bsz, T, GLA_WIDTH) * jax.nn.silu(g_o)
    return jnp.concatenate([y_conv, y_moba, y_gla], axis=-1) @ w_out

def memory_cross_attention(h, mem_n, wq, wkv, wo):
    Bsz, T, _ = h.shape
    q = (h @ wq).reshape(Bsz, T, N_XATTN_HEADS, HEAD_DIM)
    k, v = jnp.split(mem_n @ wkv, 2, axis=-1)
    k = k.reshape(Bsz, -1, N_XATTN_HEADS, HEAD_DIM)
    v = v.reshape(Bsz, -1, N_XATTN_HEADS, HEAD_DIM)
    s = jnp.einsum('bthd,bmhd->bhtm', q, k).astype(jnp.float32) * (HEAD_DIM ** -0.5)
    p = jax.nn.softmax(s, axis=-1).astype(v.dtype)
    o = jnp.einsum('bhtm,bmhd->bthd', p, v).reshape(Bsz, T, XATTN_WIDTH)
    return o @ wo

def conv_ffn(h, w_up, conv_w, conv_b, w_down):
    u = causal_dwconv(h @ w_up, conv_w, conv_b)
    a, g = jnp.split(u, 2, axis=-1)
    return (jax.nn.silu(a) * g) @ w_down

def second_inputs(seed: int = 0) -> dict:
    key = jax.random.key(seed)
    ks = jax.random.split(key, 24)
    f32 = jnp.float32

    def w(k, shape, fan_in):
        return jax.random.normal(k, shape, f32) * (fan_in ** -0.5)

    def gain(k, shape):
        return 1.0 + 0.05 * jax.random.normal(k, shape, f32)

    def bias(k, shape):
        return 0.02 * jax.random.normal(k, shape, f32)

    L = DEPTH
    return {
        "x": jax.random.normal(ks[0], (BATCH, SEQ, D_MODEL), f32),
        "mem": jax.random.normal(ks[1], (BATCH, MEM_LEN, D_MODEL), f32),
        "norm_mix_g": gain(ks[2], (L, D_MODEL)),
        "w_in": w(ks[3], (L, D_MODEL, IN_PROJ_WIDTH), D_MODEL),
        "sc_conv_w": w(ks[4], (L, CONV_K, CONV_CH), CONV_K),
        "sc_conv_b": bias(ks[5], (L, CONV_CH)),
        "gla_w_gate": w(ks[6], (L, GLA_GATE_RANK, GLA_KEY_WIDTH), GLA_GATE_RANK),
        "gla_b_gate": bias(ks[7], (L, GLA_KEY_WIDTH)),
        "gla_norm_g": gain(ks[8], (L, GLA_DV)),
        "w_out": w(ks[9], (L, MIX_WIDTH_2, D_MODEL), MIX_WIDTH_2),
        "norm_xattn_g": gain(ks[10], (L, D_MODEL)),
        "norm_mem_g": gain(ks[11], (L, D_MODEL)),
        "xattn_wq": w(ks[12], (L, D_MODEL, XATTN_WIDTH), D_MODEL),
        "xattn_wkv": w(ks[13], (L, D_MODEL, 2 * XATTN_WIDTH), D_MODEL),
        "xattn_wo": w(ks[14], (L, XATTN_WIDTH, D_MODEL), XATTN_WIDTH),
        "norm_ffn_g": gain(ks[15], (L, D_MODEL)),
        "ffn_w_up": w(ks[16], (L, D_MODEL, 2 * D_FF), D_MODEL),
        "ffn_conv_w": w(ks[17], (L, CONV_K, 2 * D_FF), CONV_K),
        "ffn_conv_b": bias(ks[18], (L, 2 * D_FF)),
        "ffn_w_down": w(ks[19], (L, D_FF, D_MODEL), D_FF),
        "final_norm_g": gain(ks[20], (D_MODEL,)),
    }

def second_block(x, mem, norm_mix_g, w_in, sc_conv_w, sc_conv_b, gla_w_gate, gla_b_gate, gla_norm_g,
              w_out, norm_xattn_g, norm_mem_g, xattn_wq, xattn_wkv, xattn_wo, norm_ffn_g,
              ffn_w_up, ffn_conv_w, ffn_conv_b, ffn_w_down, final_norm_g):
    slopes = alibi_slopes(N_MOBA_HEADS)
    for l in range(DEPTH):
        h = rmsnorm(x, norm_mix_g[l])
        x = x + hybrid_mixer(h, w_in[l], sc_conv_w[l], sc_conv_b[l], gla_w_gate[l], gla_b_gate[l],
                             gla_norm_g[l], w_out[l], slopes)
        h = rmsnorm(x, norm_xattn_g[l])
        x = x + memory_cross_attention(h, rmsnorm(mem, norm_mem_g[l]), xattn_wq[l], xattn_wkv[l], xattn_wo[l])
        h = rmsnorm(x, norm_ffn_g[l])
        x = x + conv_ffn(h, ffn_w_up[l], ffn_conv_w[l], ffn_conv_b[l], ffn_w_down[l])
    return rmsnorm(x, final_norm_g)


def setup_inputs(seed=0):
    out = dict(first_inputs(seed))
    for name, value in second_inputs(seed + 1).items():
        if name != "x":
            out[name + "_2"] = value
    return out


def reference(
    x, meta_tokens, rel_bias, attn_norm, w_in, mla_q_norm, mla_w_uq, mla_kv_norm, mla_w_ukv,
    mla_qk_norm_q, mla_qk_norm_k, diff_q_norm, diff_k_norm, diff_lambda_q1, diff_lambda_k1,
    diff_lambda_q2, diff_lambda_k2, diff_subln, w_out, ffn_norm, peer_w_query, peer_sub_keys,
    peer_u, peer_v, mem_2, norm_mix_g_2, w_in_2, sc_conv_w_2, sc_conv_b_2, gla_w_gate_2,
    gla_b_gate_2, gla_norm_g_2, w_out_2, norm_xattn_g_2, norm_mem_g_2, xattn_wq_2, xattn_wkv_2,
    xattn_wo_2, norm_ffn_g_2, ffn_w_up_2, ffn_conv_w_2, ffn_conv_b_2, ffn_w_down_2,
    final_norm_g_2,
):
    x = first_block(
        x, meta_tokens, rel_bias, attn_norm, w_in, mla_q_norm, mla_w_uq, mla_kv_norm, mla_w_ukv,
        mla_qk_norm_q, mla_qk_norm_k, diff_q_norm, diff_k_norm, diff_lambda_q1, diff_lambda_k1,
        diff_lambda_q2, diff_lambda_k2, diff_subln, w_out, ffn_norm, peer_w_query,
        peer_sub_keys, peer_u, peer_v,
    )
    return second_block(
        x, mem_2, norm_mix_g_2, w_in_2, sc_conv_w_2, sc_conv_b_2, gla_w_gate_2, gla_b_gate_2,
        gla_norm_g_2, w_out_2, norm_xattn_g_2, norm_mem_g_2, xattn_wq_2, xattn_wkv_2,
        xattn_wo_2, norm_ffn_g_2, ffn_w_up_2, ffn_conv_w_2, ffn_conv_b_2, ffn_w_down_2,
        final_norm_g_2,
    )


_drawn_inputs = setup_inputs


def setup_inputs(seed=0):
    import zlib

    import numpy as np

    out = dict(_drawn_inputs(seed))
    spreads = {}
    factors = {'mla_q_norm': 5.27,
     'mla_kv_norm': 4.521,
     'mla_qk_norm_q': 5.222,
     'mla_qk_norm_k': 5.171,
     'sc_conv_b_2': 6.914,
     'gla_b_gate_2': 8.0,
     'gla_norm_g_2': 4.787,
     'norm_xattn_g_2': 8.0,
     'norm_mem_g_2': 8.0,
     'ffn_conv_b_2': 27.752,
     'norm_ffn_g_2': 8.0}
    for name, (base, spread) in spreads.items():
        noise = np.random.default_rng([zlib.crc32(name.encode()), seed]).standard_normal(out[name].shape)
        drawn = base * np.exp(spread * noise) if base else spread * noise
        out[name] = __import__('jax').numpy.asarray(drawn.astype(out[name].dtype))
    for name, factor in factors.items():
        out[name] = (out[name] * factor).astype(out[name].dtype)
    return out
```

```python
from contextlib import ExitStack
import math

import numpy as np
import concourse.bass as bass
from concourse import mybir

F32 = mybir.dt.float32
F32R = mybir.dt.float32r
U32 = mybir.dt.uint32
ALU = mybir.AluOpType
ACT = mybir.ActivationFunctionType
AX = mybir.AxisListType

P = 128
D = 1024
KT = D // P
NQ = 256
N_META = 16
NK = NQ + N_META
EPS = 1e-6
NEG = -1e30
RING = 4
QK, NOPE, ROPE, HEADS = 96, 64, 32, 8
DH = 4
LAMBDA_INIT = 0.8 - 0.6 * math.exp(0.0)
BUCKETS, MAX_DIST = 32, 128
FAR = NK - 1
LINE = FAR + NQ + 1
PH, NKEYS, TOPK = 8, 128, 16
MH, GH, GDK, GDV, CHUNK = 8, 4, 32, 64, 64
NCH = NQ // CHUNK
XH = 4
FF = 2752
FT = -(-FF // P)

B_MEM = 0
B_IN = B_MEM + 4
B_OUT = B_IN + 17
B_QUERY = B_OUT + KT
B_PEER = B_QUERY + 2 * PH
B_IN2 = B_PEER + 2 * NKEYS
B_OUT2 = B_IN2 + 25
B_XQ = B_OUT2 + KT
B_XO = B_XQ + 2
B_FFN = B_XO + 2
N_BLOCKS = B_FFN + 3 * FT
assert N_BLOCKS % RING == 0

PARAMS = {}
for _name, _n in (("attn", 8), ("qn", 2), ("kvn", 2), ("qkq", 1), ("qkk", 1), ("dq", 1), ("dk", 1), ("lam", 4),
                  ("subln", 1), ("ffn", 8), ("mix", 8), ("scw", 6), ("scb", 2), ("gate_b", 1), ("gla", 1),
                  ("xattn", 8), ("mem", 8), ("ffn2", 8), ("cw", 6 * FT), ("cb", 2 * FT), ("final", 8)):
    PARAMS[_name] = (sum(n for _, n in PARAMS.values()), _n)
N_PARAMS = sum(n for _, n in PARAMS.values())

CONSTS = {}
for _name, _n in (("ident", 128), ("iota", 128), ("blk64", 128), ("rot", QK), ("cos", NK), ("sin", NK),
                  ("mask", 2 * NK), ("bucket", LINE), ("rel", 2 * NQ), ("gmask", CHUNK), ("gblk", 256)):
    CONSTS[_name] = (sum(n for _, n in CONSTS.values()), _n)
N_CONSTS = sum(n for _, n in CONSTS.values())
N_CONSTS_KEPT = 2 * 128


class At:

    def __init__(self, first, i=0, stride=0):
        self.first, self.i, self.stride = first, i, stride

    def plus(self, k):
        return At(self.first + k, self.i, self.stride)

    def mod(self, m):
        assert self.stride % m == 0
        return self.first % m

    def div(self, m):
        assert self.stride % m == 0
        return self.value(self.first // m, self.stride // m)

    def value(self, first=None, stride=None):
        first = self.first if first is None else first
        stride = self.stride if stride is None else stride
        return first + self.i * stride if stride else first


def build(nc, dram):
    ctx = ExitStack()
    with ctx:
        def sb(name, shape, dt=F32):
            return ctx.enter_context(nc.sbuf_tensor(name, shape, dt))

        sems = {}

        def sem(name):
            if name not in sems:
                sems[name] = ctx.enter_context(nc.semaphore(name))
            return sems[name]

        raw = sb("raw", [P, RING, D])
        w_hi = sb("w_hi", [P, RING, D], F32R)
        w_lo = sb("w_lo", [P, RING, D], F32R)
        x_op = sb("x_op", [P, 2, KT * NK], F32R)
        res = sb("res", [P, KT, NQ])
        par = sb("par", [P, N_PARAMS])
        kept = sb("kept", [P, N_CONSTS_KEPT])
        ones = sb("ones", [P, P])
        eps = sb("eps", [P, 8])
        k_mem = sb("k_mem", [P, 2, NQ])
        v_mem = sb("v_mem", [P, 2, 2 * P])
        route_t = sb("route_t", [P, 3, NQ])
        work = sb("work", [P, 2, 2, 4, P])
        h_op = sb("h_op", [P, 2, 2, NQ], F32R)
        big = sb("big", [P, NKEYS * NQ])

        ps = ctx.enter_context(nc.psum_tensor("ps", [P, 8, 512], F32))

        cursor = [0]

        def area(*shape, rows=P):
            size = int(np.prod(shape))
            a = big[0:rows, cursor[0]:cursor[0] + size]
            cursor[0] += size
            assert cursor[0] <= NKEYS * NQ, cursor[0]
            names = "abcd"[:len(shape)]
            if len(shape) > 1:
                a = a.rearrange(f"p ({' '.join(names)}) -> p {' '.join(names)}", **dict(zip(names, shape)))
            return a

        sq = area(KT * NK)
        xf = area(KT * NK)
        rt = area(NK)
        rb = area(NK)
        acc_sb = area(HEADS * NK)
        scores_sb = area(3, 2, NK)
        probs_t = area(2, 3, NQ)
        row_max = area(3, 2)
        row_sum = area(3, 2)
        row_inv = area(3, 2)
        common = cursor[0]
        cst = area(N_CONSTS - N_CONSTS_KEPT)
        mem_t = res
        v_mem_t = area(2, NQ)
        h_t = area(KT, NK)
        proj = area(17, NK)
        w_uq = area(2, HEADS * QK)
        w_ukv = area(2, HEADS * 128)
        latent = area(2 * NQ + 2 * NK)
        cqn = latent[:, 0:2 * NQ].rearrange("p (a b) -> p a b", a=2)
        ckvn = latent[:, 2 * NQ:].rearrange("p (a b) -> p a b", a=2)
        q_mla = area(HEADS, NQ, rows=QK)
        k_mla = area(HEADS, NK, rows=QK)
        rope_a = acc_sb[0:QK, :].rearrange("p (h n) -> p h n", h=HEADS)
        spare = work[:, :, :, :, :].rearrange("p a b c d -> p (a b c d)")
        v_mla = spare[:, 0:3 * 512].rearrange("p (t n) -> p t n", t=3)
        rel_rep = spare[0:BUCKETS, 3 * 512:4 * 512].rearrange("p (h n) -> p h n", h=DH)
        v_diff = w_uq.rearrange("p a b -> p (a b)").rearrange("p (t n) -> p t n", t=3)
        dqn = latent[:, 0:DH * NQ].rearrange("p (a b) -> p a b", a=DH)
        dkn = area(DH, NK)
        bias = area(DH, 2, NK)
        rel_in = area(DH, rows=BUCKETS)
        line = route_t[:, :, :].rearrange("p a b -> p (a b)")[:, 0:LINE]
        lam = area(16)
        o_diff = proj.rearrange("p a b -> p (a b)")[:, 0:DH * NQ].rearrange("p (a b) -> p a b", a=DH)
        cursor[0] = common
        sub_keys = area(2 * PH, NKEYS)
        q_peer = area(2 * PH, NQ)
        top_v = area(2, 2 * PH, TOPK)
        top_i = area(2, 2 * PH, TOPK)
        top_f = area(2, 2 * PH, TOPK)
        rest = area(2, NKEYS)
        cand = area(2, TOPK * TOPK)
        cand_rest = area(2, TOPK * TOPK)
        best = area(2, PH, TOPK)
        flat = area(2, PH, TOPK)
        ab_u = area(2, 2, PH, TOPK)
        ab_f = area(2, 2, PH, TOPK)
        hit = area(PH, TOPK, TOPK)
        expert = area(2, 2, PH, TOPK)
        soft = area(2, PH, TOPK)
        soft_s = area(2, PH)
        cursor[0] = common
        cst2 = area(N_CONSTS - N_CONSTS_KEPT)
        w_gate = area(P, rows=16)
        proj2 = area(25, NQ)
        conv_u = area(2, NQ)
        conv_y = area(2, NQ)
        v_moba = area(2, 512)
        z = area(NQ)
        z2 = area(NQ)
        log_a = area(NQ)
        csum = area(NQ)
        e_pos = area(NQ)
        e_neg = area(NQ)
        e_end = area(NQ)
        decay = area(NCH)
        qd = area(NQ)
        kd = area(NQ)
        kend_t = area(NCH, P, rows=CHUNK)
        v_gla = area(NCH, 256, rows=CHUNK)
        a_gla = area(GH, NCH, CHUNK, rows=CHUNK)
        state = area(NCH, 256)
        upd = area(NCH, 256)
        o_gla = area(2, NQ)
        y_gla = area(2, NQ)
        silu_o = area(2, NQ)
        q_x = area(2, NQ)
        conv_a = area(2, NQ)
        conv_g = area(2, NQ)
        act_a = area(2, NQ)

        def rows_of(a):
            return a.rearrange("p a b c -> p (a b) c")

        soft_hk, best_hk = rows_of(soft), rows_of(best)
        soft_flat = soft.rearrange("p a b c -> p (a b c)")
        flat_u = flat.rearrange("p a b c -> p (a b c)").bitcast(U32)
        ab_u0, ab_u1 = (ab_u[:, j].rearrange("p a b c -> p (a b c)").bitcast(U32) for j in range(2))
        ab_u_flat = ab_u.rearrange("p a b c d -> p (a b c d)").bitcast(U32)
        ab_f_flat = ab_f.rearrange("p a b c d -> p (a b c d)")
        rb_sub = acc_sb[:, 0:DH * NQ]

        ge = work[:, 0].rearrange("p a b c -> p a (b c)")[:, :, 0:NQ]
        hf = work[:, 1].rearrange("p a b c -> p a (b c)")[:, :, 0:NQ]
        one1, one2 = work[:, 0], work[:, 1]
        G = big[:, :].rearrange("p (t e) -> p t e", e=NKEYS)

        def pcol(name, k=0, rows=P):
            return par[0:rows, PARAMS[name][0] + k:PARAMS[name][0] + k + 1]

        def con(name, rows=P, at=None):
            a, n = CONSTS[name]
            if a < N_CONSTS_KEPT:
                return kept[0:rows, a:a + n]
            return at[0:rows, a - N_CONSTS_KEPT:a - N_CONSTS_KEPT + n]

        ident = con("ident")
        E_MODEL, E_QK, E_64, E_SUB, E_ONE = (eps[:, i:i + 1] for i in range(5))

        def x_k(part, k, T):
            return x_op[:, part, k * T:(k + 1) * T]

        def x_all(part, T):
            return x_op[:, part, 0:KT * T]

        def flat2(a):
            return a.rearrange("p a b -> p (a b)")

        def banks(a, n):
            return ps[:, a:a + n, :].rearrange("p a b -> p (a b)")

        scratch = nc.dram_tensor("bias_lines", (DH, P + 1, LINE), F32, kind="Internal").ap()
        skewed = scratch.rearrange("h p j -> h (p j)")

        M_MEM = 0
        M_IN = M_MEM + 4
        M_OUT = M_IN + 17
        M_QUERY = M_OUT + KT
        M_PEER = M_QUERY + 2 * PH
        M_IN2 = M_PEER
        M_OUT2 = M_IN2 + 25
        M_XQ = M_OUT2 + KT
        M_XO = M_XQ + 2
        M_FFN = M_XO + 2

        R_MEM, R_ATTN, R_PEER, R_MIX, R_XATTN, R_FFN, R_FINAL = range(7)

        units = []
        for h in range(HEADS):
            units.append(dict(kind="mla", head=h, keys=NK, out=h))
        for h in range(DH):
            units.append(dict(kind="diff", head=h, map=0, keys=NK, out=None))
            units.append(dict(kind="diff", head=h, map=1, keys=NK, out=HEADS + h))
        for h in range(MH):
            units.append(dict(kind="moba", head=h, keys=NQ, out=HEADS + DH + h))
        for h in range(XH):
            units.append(dict(kind="xattn", head=h, keys=NQ, out=HEADS + DH + MH + h))
        U_MLA, U_DIFF, U_MOBA, U_X = (0, HEADS, HEADS + 2 * DH, HEADS + 2 * DH + MH)
        U_END = U_X + XH
        n_tail = [sum(1 for u in units[:k] if u["out"] is not None and u["keys"] > NQ) for k in range(U_END + 1)]

        def first_unit(kind):
            return {"mla": U_MLA, "diff": U_DIFF, "moba": U_MOBA, "xattn": U_X}[kind]

        block = ctx.enter_context(nc.Block())

        @block.sync
        def _(sp):
            sp.dma_start(flat2(mem_t[:, :, :]), dram["mem_t"]).then_inc(sem("mem_loaded"), 16)
            sp.dma_start(par[:, :], dram["params"]).then_inc(sem("par_loaded"), 16)

            def load(n):
                sp.dma_start(raw[:, n.mod(RING), :], dram["blocks"][bass.ds(n.value(), 1)].rearrange("a p c -> p (a c)")
                             ).then_inc(sem(f"raw_loaded{n.mod(RING)}"), 16)

            for j in range(RING):
                load(At(j))
            with sp.Fori(1, N_BLOCKS // RING) as i:
                for j in range(RING):
                    sp.wait_ge(sem(f"lo_done{j % 2}"), 2 * i + (j // 2 - 1))
                    load(At(j, i, RING))

        @block.gpsimd
        def _(pool):
            def lo(n):
                pool.wait_ge(sem("hi_done"), n.plus(1).value())
                s = n.mod(RING)
                pool.tensor_tensor(w_lo[:, s, :], raw[:, s, :], w_hi[:, s, :].bitcast(F32), ALU.subtract
                                   ).then_inc(sem("lo_done0"), 1)

            def los(a, b):
                for n in range(a + a % 2, b, 2):
                    lo(At(n))

            pool.memset(ones[:, :], 1.0).then_inc(sem("ones_set"), 1)
            for i, v in enumerate((EPS, QK * EPS, 64 * EPS, EPS / (1 - LAMBDA_INIT) ** 2, 1.0)):
                ins = pool.memset(eps[:, i:i + 1], v)
            ins.then_inc(sem("eps_set"), 1)
            los(B_MEM, B_IN)
            pool.wait_ge(sem("bias_loaded"), 16 * 2 * DH)
            pool.wait_ge(sem("cst_loaded"), 16)
            pool.tensor_tensor(
                bias, bias, con("mask", at=cst).rearrange("p (t k) -> p t k", t=2).unsqueeze(1).to_broadcast([P, DH, 2, NK]),
                ALU.add).then_inc(sem("bias_ready"), 1)
            los(B_IN, B_OUT + 2)
            for which, (x, n) in enumerate(((q_mla, NQ), (k_mla, NK))):
                pool.wait_ge(sem("qk_normed"), which + 1)
                pool.tensor_tensor(rope_a[:, :, 0:n], x,
                                   con("cos", QK, cst)[:, NK - n:NK].unsqueeze(1).to_broadcast([QK, HEADS, n]),
                                   ALU.mult).then_inc(sem("rope_cos"), 1)
            los(B_OUT + 2, B_PEER + 2)
            for c in range(2):
                lo(At(B_PEER + 3 + 2 * c))
            with pool.Fori(0, (NKEYS - 4) // 2) as i:
                for c in range(2):
                    lo(At(B_PEER + 7 + 2 * c, i, 4))
            los(B_PEER + 7 + 2 * (NKEYS - 4), N_BLOCKS)

        @block.scalar
        def _(act):
            def hi(n):
                s = n.mod(RING)
                act.wait_ge(sem(f"raw_loaded{s}"), n.div(RING) * 16 + 16)
                if n.first >= RING:
                    act.wait_ge(sem("block_used"), n.plus(1 - RING).value())
                act.activation(w_hi[:, s, :], raw[:, s, :], ACT.Copy).then_inc(sem("hi_done"), 1)

            ahead = [0]

            def his(upto):
                while ahead[0] < min(upto, N_BLOCKS):
                    hi(At(ahead[0]))
                    ahead[0] += 1

            def evacuate(n, m, dst, rows=P, T=NQ, scale=1.0):
                act.wait_ge(sem("block_used"), n + 1)
                act.activation(dst, ps[0:rows, m % 2, 0:T], ACT.Copy, scale=scale).then_inc(sem("bank_free"), 1)

            def norm(r, src, T):
                act.activation(sq[:, 0:KT * T], src, ACT.Square).then_inc(sem("rms_squares"), 1)
                act.wait_ge(sem("rms_sum"), r + 1)
                act.activation(rt[:, 0:T], ps[:, 2, 0:T], ACT.Sqrt, scale=1.0 / D, bias=E_MODEL).then_inc(sem("rms_root"), 1)

            def norm_hi(r, T, n):
                act.wait_ge(sem("rms_xf"), r + 1)
                if n:
                    act.wait_ge(sem("block_used"), n)
                act.activation(x_all(0, T), xf[:, 0:KT * T], ACT.Copy).then_inc(sem("rms_hi"), 1)

            act.dma_start(kept[:, :], dram["consts"][:, 0:N_CONSTS_KEPT]).then_inc(sem("kept_loaded"), 16)
            act.dma_start(cst, dram["consts"][:, N_CONSTS_KEPT:]).then_inc(sem("cst_loaded"), 16)
            act.dma_start(rel_in, dram["rel_bias"]).then_inc(sem("rel_loaded"), 16)
            act.dma_start(flat2(h_t), dram["h_t"]).then_inc(sem("h_loaded"), 16)
            act.dma_start(flat2(w_uq), dram["w_uq"]).then_inc(sem("wu_loaded"), 16)
            act.dma_start(flat2(w_ukv), dram["w_ukv"]).then_inc(sem("wu_loaded"), 16)
            act.wait_ge(sem("eps_set"), 1)
            act.wait_ge(sem("par_loaded"), 16)
            act.wait_ge(sem("mem_loaded"), 16)
            norm(R_MEM, flat2(mem_t[:, :, :]), NQ)
            his(2)
            for h in range(DH):
                act.wait_ge(sem("line_done"), h + 1)
                if h:
                    act.wait_ge(sem("line_stored"), 16 * h)
                act.activation(line[:, 0:LINE // 2], ps[:, 4, 0:LINE // 2], ACT.Copy)
                act.activation(line[:, LINE // 2:LINE], ps[:, 5, 0:LINE - LINE // 2], ACT.Copy).then_inc(sem("line_ready"), 1)
                act.wait_ge(sem("line_ready"), h + 1)
                act.dma_start(scratch[h, 0:P], line).then_inc(sem("line_stored"), 16)
            norm_hi(R_MEM, NQ, 0)
            his(4)
            for j in range(4):
                evacuate(B_MEM + j, M_MEM + j, k_mem[:, j, :] if j < 2 else v_mem_t[:, j - 2, :])
            act.wait_ge(sem("line_stored"), 16 * DH)
            for h in range(DH):
                for t in range(2):
                    start = FAR - N_META - P * t
                    src = skewed[h, start:start + P * (LINE - 1)].rearrange("(p j) -> p j", j=LINE - 1)[:, 0:NK]
                    act.dma_start(bias[:, h, t, :], src).then_inc(sem("bias_loaded"), 16)
            act.wait_ge(sem("h_loaded"), 16)
            norm(R_ATTN, flat2(h_t), NK)
            act.wait_ge(sem("v_mem_turned"), 1)
            act.activation(flat2(v_mem[:, :, :]), ps[:, 3, :], ACT.Copy).then_inc(sem("v_mem_ready"), 1)
            his(6)
            norm_hi(R_ATTN, NK, B_IN)
            for j in range(17):
                his(B_IN + j + 3)
                evacuate(B_IN + j, M_IN + j, proj[:, j, :], T=NK)
            act.wait_ge(sem("bank_free"), M_OUT)
            lat = ((proj[:, 0:2, N_META:NK], NQ), (proj[:, 2:4, :], NK))
            for w, (src, n) in enumerate(lat):
                act.activation(sq[:, w * 2 * NK:w * 2 * NK + 2 * n].rearrange("p (a b) -> p a b", a=2), src,
                               ACT.Square).then_inc(sem("lat_squares"), 1)
            for w, (src, n) in enumerate(lat):
                act.wait_ge(sem("lat_sum"), w + 1)
                act.activation((rt, rb)[w][:, 0:n], ps[:, 2 + w, 0:n], ACT.Sqrt, scale=1.0 / 256,
                               bias=E_MODEL).then_inc(sem("lat_root"), 1)
            act.wait_ge(sem("q_product"), 1)
            act.activation(flat2(q_mla), banks(4, 4)[0:QK, :], ACT.Copy).then_inc(sem("q_raw"), 1)
            act.wait_ge(sem("q_raw"), 1)
            act.activation(sq[0:QK, 0:HEADS * NQ], flat2(q_mla), ACT.Square).then_inc(sem("qk_squares"), 1)
            for t in range(3):
                rows = min(P, NK - P * t)
                act.wait_ge(sem("v_product"), t + 1)
                act.activation(v_mla[0:rows, t, :], ps[0:rows, 2 + t % 2, :], ACT.Copy).then_inc(sem("v_ready"), 1)
            act.wait_ge(sem("qk_sum"), 1)
            act.activation(xf[0:QK, 0:HEADS * NQ], banks(4, 4)[0:QK, :], ACT.Sqrt, bias=E_QK[0:QK]).then_inc(sem("qk_root"), 1)
            for w in range(2):
                act.wait_ge(sem("k_product"), w + 1)
                act.activation(k_mla[0:NOPE, 4 * w:4 * w + 4, :], ps[0:NOPE, 4:8, 0:NK], ACT.Copy).then_inc(sem("k_raw"), 1)
            act.wait_ge(sem("k_raw"), 3)
            act.wait_ge(sem("qk_sum"), 1)
            act.activation(sq[0:QK, 0:HEADS * NK], flat2(k_mla), ACT.Square).then_inc(sem("qk_squares"), 1)
            act.wait_ge(sem("qk_sum"), 2)
            act.wait_ge(sem("qk_normed"), 1)
            act.activation(xf[0:QK, 0:HEADS * NK], banks(2, 5)[0:QK, 0:HEADS * NK], ACT.Sqrt, scale=1.0 / QK,
                           bias=E_MODEL[0:QK]).then_inc(sem("qk_root"), 1)
            for w, (a, n) in enumerate(((4, NQ), (8, NK))):
                if w:
                    act.wait_ge(sem("d_sum"), w)
                act.activation(sq[:, 0:DH * n].rearrange("p (a b) -> p a b", a=DH), proj[:, a:a + DH, NK - n:NK],
                               ACT.Square).then_inc(sem("d_squares"), 1)
                act.wait_ge(sem("d_sum"), w + 1)
                act.wait_ge(sem("qk_normed"), 2)
                if w:
                    act.wait_ge(sem("d_ready"), w)
                act.activation(xf[:, 0:DH * n], banks(2, 3)[:, 0:DH * n], ACT.Sqrt, scale=1.0 if w == 0 else 1.0 / 64,
                               bias=E_64 if w == 0 else E_MODEL).then_inc(sem("d_root"), 1)
            act.wait_ge(sem("lam_sum"), 1)
            act.activation(lam[:, 4:6], ps[:, 5, 0:2], ACT.Exp).then_inc(sem("lam_exp"), 1)

            def soft(u):
                n = units[u]["keys"]
                act.wait_ge(sem("max_ready"), u + 1)
                for t in range(2):
                    ins = act.activation(scores_sb[:, u % 3, t, 0:n], scores_sb[:, u % 3, t, 0:n], ACT.Exp,
                                         bias=row_max[:, u % 3, t:t + 1], accum_out=row_sum[:, u % 3, t:t + 1])
                ins.then_inc(sem("exp_done"), 1)

            def finish(u):
                o = units[u]["out"]
                if o is None:
                    return
                act.wait_ge(sem("probs_turned"), o + 1)
                act.activation(flat2(probs_t[:, o % 2, 0:2, :]), ps[:, 6, :], ACT.Copy).then_inc(sem("probs_ready"), 1)
                act.wait_ge(sem("out_done"), o + 1)
                kind, h = units[u]["kind"], units[u]["head"]
                if kind == "diff":
                    act.activation(o_diff[:, h, :], ps[:, 7, 0:NQ], ACT.Copy).then_inc(sem("y_hi"), 1)
                else:
                    rows = slice(64 * (h % 2), 64 * (h % 2) + 64)
                    k = h // 2 + (2 if kind == "moba" else 0)
                    act.activation(x_k(0, k, NQ)[rows], ps[rows, 7, 0:NQ], ACT.Copy).then_inc(sem("y_hi"), 1)

            def attention(a, b):
                soft(a)
                for u in range(a, b):
                    if u + 1 < b:
                        soft(u + 1)
                    finish(u)

            attention(U_MLA, U_MOBA)
            act.wait_ge(sem("y_hi"), HEADS + DH)
            act.activation(sq[:, 0:DH * NQ], flat2(o_diff), ACT.Square).then_inc(sem("sub_squares"), 1)
            act.wait_ge(sem("sub_sum"), 1)
            act.activation(rb_sub, banks(2, 2), ACT.Sqrt, scale=1.0 / (P * (1 - LAMBDA_INIT) ** 2),
                           bias=E_SUB).then_inc(sem("sub_root"), 1)
            act.wait_ge(sem("sub_ready"), 1)
            act.activation(x_op[:, 0, 4 * NQ:8 * NQ], xf[:, 0:DH * NQ], ACT.Copy).then_inc(sem("sub_hi"), 1)
            his(B_OUT + 4)
            for j in range(KT):
                act.wait_ge(sem("block_used"), B_OUT + j + 1)
                his(B_OUT + j + 4)
            act.wait_ge(sem("bank_free"), M_QUERY)
            act.dma_start(flat2(sub_keys), dram["sub_keys"]).then_inc(sem("sub_keys_loaded"), 16)
            norm(R_PEER, flat2(res[:, :, :]), NQ)
            norm_hi(R_PEER, NQ, B_QUERY)
            for j in range(2 * PH):
                his(B_QUERY + j + 3)
                evacuate(B_QUERY + j, M_QUERY + j, q_peer[:, j, :])
            his(B_PEER + 2)
            act.wait_ge(sem("soft_in"), 1)
            act.activation(soft_flat, soft_flat, ACT.Exp).then_inc(sem("soft_exp"), 1)
            for w in range(3):
                act.wait_ge(sem("route_turned"), w + 1)
                act.activation(route_t[:, w, :], ps[:, 2 + w, 0:NQ], ACT.Copy).then_inc(sem("route_t_ready"), 1)
            for g in range(2):
                act.wait_ge(sem("g_product"), g + 1)
                act.activation(G[:, 4 * g:4 * g + 4, :].rearrange("p a b -> p (a b)"), ps[:, 2 + g, :],
                               ACT.Copy).then_inc(sem("g_ready"), 1)
            with act.Fori(1, NQ // 8) as i:
                for g in range(2):
                    act.wait_ge(sem("g_product"), 2 * i + (g + 1))
                    act.activation(big[:, bass.ds(1024 * i + 512 * g, 512)], ps[:, 2 + g, :],
                                   ACT.Copy).then_inc(sem("g_ready"), 1)

            def chunk(c):
                act.wait_ge(sem("block_used"), c.plus(0).value(B_PEER + 2 * c.first if c.first else B_PEER + 1, 2 * c.stride))
                if c.first >= 2:
                    act.wait_ge(sem("act_used"), c.plus(-1).value())
                act.activation(ge[:, c.mod(2), :], ps[:, (M_PEER + c.first) % 2, 0:NQ], ACT.Gelu).then_inc(sem("gelu_done"), 1)

            his(B_PEER + 3)
            for c in range(2):
                chunk(At(c))
                hi(At(B_PEER + 3 + 2 * c))
                hi(At(B_PEER + 4 + 2 * c))
            with act.Fori(0, (NKEYS - 4) // 2) as i:
                for c in range(2):
                    chunk(At(2 + c, i, 2))
                    hi(At(B_PEER + 7 + 2 * c, i, 4))
                    hi(At(B_PEER + 8 + 2 * c, i, 4))
            ahead[0] = B_PEER + 7 + 2 * (NKEYS - 4)
            chunk(At(NKEYS - 2))
            his(B_PEER + 2 * NKEYS)
            chunk(At(NKEYS - 1))
            act.wait_ge(sem("acts_ready"), NKEYS)
            act.dma_start(cst2, dram["consts"][:, N_CONSTS_KEPT:]).then_inc(sem("cst2_loaded"), 16)
            act.dma_start(w_gate, dram["w_gate"]).then_inc(sem("cst2_loaded"), 16)

            def collect(n):
                act.wait_ge(sem("block_used"), n)
                act.activation(acc_sb[:, 0:2048], banks(4, 4), ACT.Copy).then_inc(sem("sum_out"), 1)

            collect(B_IN2)
            his(B_IN2 + 2)
            act.wait_ge(sem("res_ready"), 1)
            norm(R_MIX, flat2(res[:, :, :]), NQ)
            norm_hi(R_MIX, NQ, B_IN2)
            for j in range(25):
                his(B_IN2 + j + 3)
                evacuate(B_IN2 + j, M_IN2 + j, proj2[:, j, :], scale=0.125 if 6 <= j < 10 else 1.0)
            act.wait_ge(sem("bank_free"), M_OUT2)
            act.wait_ge(sem("gate_product"), 1)
            act.activation(z, ps[:, 2, 0:NQ], ACT.Identity, bias=pcol("gate_b")).then_inc(sem("gate_z"), 1)
            act.wait_ge(sem("gate_z"), 1)
            act.activation(z2, z, ACT.Abs).then_inc(sem("gate_step"), 1)
            act.wait_ge(sem("gate_step"), 1)
            act.activation(z2, z2, ACT.Exp, scale=-1.0).then_inc(sem("gate_step"), 1)
            act.wait_ge(sem("gate_step"), 2)
            act.activation(z2, z2, ACT.Ln, bias=E_ONE).then_inc(sem("gate_ln"), 1)
            act.wait_ge(sem("csum_ready"), 1)
            act.activation(e_pos, csum, ACT.Exp).then_inc(sem("gla_exp"), 1)
            act.activation(e_neg, csum, ACT.Exp, scale=-1.0).then_inc(sem("gla_exp"), 1)
            for n in range(NCH):
                last = csum[:, CHUNK * n + CHUNK - 1:CHUNK * n + CHUNK]
                act.activation(e_end[:, CHUNK * n:CHUNK * n + CHUNK], csum[:, CHUNK * n:CHUNK * n + CHUNK], ACT.Exp,
                               scale=-1.0, bias=last)
                ins = act.activation(decay[:, n:n + 1], last, ACT.Exp)
            ins.then_inc(sem("gla_exp"), 1)
            act.activation(flat2(silu_o), flat2(proj2[:, 22:24, :]), ACT.Silu).then_inc(sem("silu_ready"), 1)
            act.wait_ge(sem("gla_turned"), 1)
            act.activation(flat2(v_gla), banks(2, 2)[0:CHUNK, :], ACT.Copy).then_inc(sem("gla_v"), 1)
            act.activation(flat2(kend_t), ps[0:CHUNK, 4, :], ACT.Copy).then_inc(sem("gla_v"), 1)
            act.wait_ge(sem("gla_out"), 1)
            act.activation(o_gla, ps[:, 2:4, 0:NQ], ACT.Copy).then_inc(sem("gla_o"), 1)
            act.wait_ge(sem("gla_o"), 1)
            act.activation(sq[:, 0:2 * NQ], flat2(o_gla), ACT.Square).then_inc(sem("gla_squares"), 1)
            act.wait_ge(sem("gla_sum"), 1)
            act.activation(acc_sb[:, 0:512], ps[:, 4, :], ACT.Sqrt, scale=1.0 / GDV, bias=E_MODEL).then_inc(sem("gla_root"), 1)
            act.wait_ge(sem("mix_ready"), 1)
            act.activation(x_op[:, 0, 0:2 * NQ], flat2(conv_y), ACT.Copy).then_inc(sem("mix_hi"), 1)
            act.wait_ge(sem("mix_ready"), 2)
            act.activation(x_op[:, 0, 6 * NQ:8 * NQ], flat2(y_gla), ACT.Copy).then_inc(sem("mix_hi"), 1)
            attention(U_MOBA, U_X)
            for j in range(KT):
                his(B_OUT2 + j + 3)
                act.wait_ge(sem("block_used"), B_OUT2 + j + 1)
            act.wait_ge(sem("bank_free"), M_XQ)
            norm(R_XATTN, flat2(res[:, :, :]), NQ)
            norm_hi(R_XATTN, NQ, B_XQ)
            for j in range(2):
                his(B_XQ + j + 3)
                evacuate(B_XQ + j, M_XQ + j, q_x[:, j, :], scale=0.125)
            attention(U_X, U_END)
            his(B_FFN + 2)
            act.wait_ge(sem("bank_free"), M_FFN)
            norm(R_FFN, flat2(res[:, :, :]), NQ)
            norm_hi(R_FFN, NQ, B_FFN)

            def pvar(name, per, k, p):
                return par[:, bass.ds(p.value(PARAMS[name][0] + k + per * p.first, per * p.stride), 1)]

            def taps(p):
                for half, buf in enumerate((conv_a, conv_g)):
                    done = B_FFN + 1 + half if p.first == 0 else B_FFN + 3 * p.first + half
                    act.wait_ge(sem("block_used"), p.value(done, 3 * p.stride))
                    if half == 0 and p.first >= 2:
                        act.wait_ge(sem("act_used"), p.value(NKEYS + p.first - 1))
                    act.activation(buf[:, p.mod(2), :], ps[:, half, 0:NQ], ACT.Identity, scale=pvar("cw", 6, 3 * half + 2, p),
                                   bias=pvar("cb", 2, half, p)).then_inc(sem("tap_done"), 1)

            def silu(p):
                act.wait_ge(sem("bank_free"), p.value(M_FFN + 2 * p.first + 1, 2 * p.stride))
                act.activation(act_a[:, p.mod(2), :], conv_a[:, p.mod(2), :], ACT.Silu).then_inc(sem("silu_done"), 1)

            def tile(p):
                n = At(B_FFN + 3 * p.first + 3, p.i, 3 * p.stride)
                hi(n)
                taps(p)
                hi(n.plus(1))
                silu(p)
                hi(n.plus(2))

            his(B_FFN + 3)
            tile(At(0))
            with act.Fori(0, (FT - 2) // 4) as i:
                for j in range(4):
                    tile(At(1 + j, i, 4))
            taps(At(FT - 1))
            silu(At(FT - 1))
            collect(N_BLOCKS)
            act.wait_ge(sem("res_ready"), 2)
            norm(R_FINAL, flat2(res[:, :, :]), NQ)
            act.wait_ge(sem("rms_xf"), R_FINAL + 1)
            act.dma_start(dram["out"], xf[:, 0:KT * NQ]).then_inc(sem("out_stored"), 16)
            act.wait_ge(sem("out_stored"), 16)

        @block.vector
        def _(dve):
            steps = [0]

            def step(ins):
                steps[0] += 1
                ins.then_inc(sem("dve_step"), 1)
                dve.wait_ge(sem("dve_step"), steps[0])

            def lo(n):
                dve.wait_ge(sem("hi_done"), n.plus(1).value())
                s = n.mod(RING)
                dve.tensor_tensor(w_lo[:, s, :], raw[:, s, :], w_hi[:, s, :].bitcast(F32), ALU.subtract
                                  ).then_inc(sem("lo_done1"), 1)

            ahead = [1]

            def los(upto):
                while ahead[0] < min(upto, N_BLOCKS):
                    lo(At(ahead[0]))
                    ahead[0] += 2

            def norm(r, src, gain, T, operand=True):
                dve.wait_ge(sem("rms_root"), r + 1)
                step(dve.reciprocal(rb[:, 0:T], rt[:, 0:T]))
                for k in range(KT):
                    ins = dve.scalar_tensor_tensor(out=xf[:, k * T:(k + 1) * T], in0=src[:, k, :], scalar=pcol(gain, k),
                                                   in1=rb[:, 0:T], op0=ALU.mult, op1=ALU.mult)
                ins.then_inc(sem("rms_xf"), 1)
                if operand:
                    dve.wait_ge(sem("rms_hi"), r + 1)
                    dve.tensor_tensor(x_all(1, T), xf[:, 0:KT * T], x_all(0, T).bitcast(F32), ALU.subtract
                                      ).then_inc(sem("rms_x"), 1)

            dve.wait_ge(sem("rel_loaded"), 16)
            dve.tensor_copy(rel_rep, rel_in.unsqueeze(2).to_broadcast([BUCKETS, DH, P])).then_inc(sem("rel_ready"), 1)
            dve.wait_ge(sem("par_loaded"), 16)
            norm(R_MEM, mem_t, "mem", NQ)
            los(4)
            dve.wait_ge(sem("h_loaded"), 16)
            norm(R_ATTN, h_t, "attn", NK)
            l0 = PARAMS["lam"][0]
            dve.tensor_tensor(lam[0:64, 0:2], par[0:64, l0:l0 + 4:2], par[0:64, l0 + 1:l0 + 4:2], ALU.mult
                              ).then_inc(sem("lam_ready"), 1)
            los(B_OUT + 2)
            dve.wait_ge(sem("bank_free"), M_OUT)
            for w, (src, dst, n, gain) in enumerate(((proj[:, 0:2, N_META:NK], cqn, NQ, "qn"), (proj[:, 2:4, :], ckvn, NK, "kvn"))):
                r = (rt, rb)[w][:, 0:n]
                dve.wait_ge(sem("lat_root"), w + 1)
                step(dve.reciprocal(r, r))
                for k in range(2):
                    ins = dve.scalar_tensor_tensor(out=dst[:, k, :], in0=src[:, k, :], scalar=pcol(gain, k), in1=r,
                                                   op0=ALU.mult, op1=ALU.mult)
                ins.then_inc(sem("lat_ready"), 1)
            dve.tensor_copy(k_mla[NOPE:QK], proj[NOPE:QK, 16, :].unsqueeze(1).to_broadcast([ROPE, HEADS, NK])
                            ).then_inc(sem("k_raw"), 1)
            for w, (x, n, gain) in enumerate(((q_mla, NQ, "qkq"), (k_mla, NK, "qkk"))):
                dve.wait_ge(sem("qk_root"), w + 1)
                r = xf[0:QK, 0:HEADS * n]
                step(dve.reciprocal(r, r))
                dve.scalar_tensor_tensor(out=flat2(x), in0=flat2(x), scalar=pcol(gain, rows=QK), in1=r,
                                         op0=ALU.mult, op1=ALU.mult).then_inc(sem("qk_normed"), 1)
                sin = con("sin", QK, cst)[:, NK - n:NK].unsqueeze(1).to_broadcast([QK, HEADS, n])
                dve.wait_ge(sem("qk_turned"), w + 1)
                dve.wait_ge(sem("rope_cos"), w + 1)
                turned = banks(4, 4)[0:QK, :] if w == 0 else banks(2, 5)[0:QK, 0:HEADS * NK]
                step(dve.tensor_tensor(x, turned.rearrange("p (h n) -> p h n", h=HEADS), sin, ALU.mult))
                dve.tensor_tensor(x, x, rope_a[:, :, 0:n], ALU.add).then_inc(sem("qk_ready"), 1)
            for w, (a, dst, n, gain) in enumerate(((4, dqn, NQ, "dq"), (8, dkn, NK, "dk"))):
                dve.wait_ge(sem("d_root"), w + 1)
                r = xf[:, 0:DH * n]
                step(dve.reciprocal(r, r))
                dve.scalar_tensor_tensor(out=dst, in0=proj[:, a:a + DH, NK - n:NK], scalar=pcol(gain),
                                         in1=r.rearrange("p (a b) -> p a b", a=DH), op0=ALU.mult, op1=ALU.mult
                                         ).then_inc(sem("d_ready"), 1)
            for t in range(3):
                rows = min(P, NK - P * t)
                dve.wait_ge(sem("dv_turned"), t + 1)
                dve.tensor_copy(v_diff[0:rows, t, :], ps[0:rows, 6 + t % 2, :]).then_inc(sem("dv_ready"), 1)
            dve.wait_ge(sem("lam_exp"), 1)
            step(dve.tensor_tensor(lam[:, 6:7], lam[:, 5:6], lam[:, 4:5], ALU.subtract))
            step(dve.tensor_scalar(lam[:, 7:8], lam[:, 6:7], -LAMBDA_INIT, None, ALU.add))

            def soft_in(u):
                x = units[u]
                n, b = x["keys"], 2 + 2 * (u % 2)
                s = scores_sb[:, u % 3, :, 0:n]
                src = ps[:, b:b + 2, 0:n]
                dve.wait_ge(sem("scores_done"), u + 1)
                if u >= 3:
                    dve.wait_ge(sem("probs_turned"), sum(1 for v in units[:u - 2] if v["out"] is not None))
                if x["kind"] == "mla":
                    ins = dve.tensor_tensor(s, src, con("mask", at=cst).rearrange("p (t k) -> p t k", t=2), ALU.add)
                elif x["kind"] == "diff":
                    if u == U_DIFF:
                        dve.wait_ge(sem("bias_ready"), 1)
                    ins = dve.tensor_tensor(s, src, bias[:, x["head"]], ALU.add)
                elif x["kind"] == "moba":
                    rel = con("rel", at=cst2).rearrange("p (t k) -> p t k", t=2)
                    ins = dve.scalar_tensor_tensor(out=s, in0=rel, scalar=2.0 ** (-8.0 * (x["head"] + 1) / MH), in1=src,
                                                   op0=ALU.mult, op1=ALU.add)
                else:
                    ins = dve.tensor_copy(s, src)
                ins.then_inc(sem("scores_read"), 1)
                dve.wait_ge(sem("scores_read"), u + 1)
                step(dve.tensor_reduce(row_inv[:, u % 3, :], s, AX.X, ALU.max))
                dve.tensor_scalar(row_max[:, u % 3, :], row_inv[:, u % 3, :], -1.0, None, ALU.mult
                                  ).then_inc(sem("max_ready"), 1)

            def normalise(u):
                x = units[u]
                n, b = x["keys"], u % 3
                dve.wait_ge(sem("exp_done"), u + 1)
                step(dve.reciprocal(row_inv[:, b, :], row_sum[:, b, :]))
                if x["kind"] == "diff" and x["map"] == 1:
                    step(dve.tensor_scalar(row_inv[:, b, :], row_inv[:, b, :], lam[:, 7:8], None, ALU.mult))
                    dve.wait_ge(sem("probs_normed"), u)
                    for t in range(2):
                        ins = dve.scalar_tensor_tensor(out=scores_sb[:, b, t, 0:n], in0=scores_sb[:, b, t, 0:n],
                                                       scalar=row_inv[:, b, t:t + 1], in1=scores_sb[:, (u - 1) % 3, t, 0:n],
                                                       op0=ALU.mult, op1=ALU.add)
                else:
                    for t in range(2):
                        ins = dve.tensor_scalar(scores_sb[:, b, t, 0:n], scores_sb[:, b, t, 0:n],
                                                row_inv[:, b, t:t + 1], None, ALU.mult)
                ins.then_inc(sem("probs_normed"), 1)

            def finish(u):
                x = units[u]
                o = x["out"]
                if o is None:
                    return
                if x["keys"] > NQ:
                    dve.wait_ge(sem("probs_turned"), o + 1)
                    dve.tensor_copy(probs_t[0:N_META, o % 2, 2, :], ps[0:N_META, 7, NQ:2 * NQ]).then_inc(sem("tail_ready"), 1)
                if x["kind"] != "diff":
                    rows = slice(64 * (x["head"] % 2), 64 * (x["head"] % 2) + 64)
                    k = x["head"] // 2 + (2 if x["kind"] == "moba" else 0)
                    dve.wait_ge(sem("y_hi"), o + 1)
                    dve.tensor_tensor(x_k(1, k, NQ)[rows], ps[rows, 7, 0:NQ], x_k(0, k, NQ)[rows].bitcast(F32),
                                      ALU.subtract).then_inc(sem("y_ready"), 1)

            def attention(a, b):
                soft_in(a)
                for u in range(a, b):
                    if u + 1 < b:
                        soft_in(u + 1)
                    normalise(u)
                    finish(u)

            attention(U_MLA, U_MOBA)
            dve.wait_ge(sem("sub_root"), 1)
            step(dve.reciprocal(rb_sub, rb_sub))
            dve.scalar_tensor_tensor(out=xf[:, 0:DH * NQ], in0=flat2(o_diff), scalar=pcol("subln"), in1=rb_sub,
                                     op0=ALU.mult, op1=ALU.mult).then_inc(sem("sub_ready"), 1)
            dve.wait_ge(sem("sub_hi"), 1)
            dve.tensor_tensor(x_op[:, 1, 4 * NQ:8 * NQ], xf[:, 0:DH * NQ], x_op[:, 0, 4 * NQ:8 * NQ].bitcast(F32),
                              ALU.subtract).then_inc(sem("y_ready"), 1)

            def add_residual(n, m, dst, src):
                dve.wait_ge(sem("block_used"), n + 1)
                dve.tensor_tensor(dst, ps[:, m % 2, 0:NQ], src, ALU.add).then_inc(sem("bank_free"), 1)

            for k in range(KT):
                los(B_OUT + k + 3)
                add_residual(B_OUT + k, M_OUT + k, res[:, k, :], h_t[:, k, N_META:NK])
            dve.wait_ge(sem("bank_free"), M_QUERY)
            norm(R_PEER, res, "ffn", NQ)

            def top16(src, rest_, vals, idx):
                for half in range(2):
                    at = slice(8 * half, 8 * half + 8)
                    for t in range(2):
                        ins = dve.max(vals(t)[:, at], src(t) if half == 0 else rest_(t))
                    step(ins)
                    for t in range(2):
                        ins = dve.max_index(idx(t)[:, at].bitcast(U32), vals(t)[:, at], src(t) if half == 0 else rest_(t))
                    if half == 0:
                        for t in range(2):
                            ins = dve.match_replace(rest_(t), vals(t)[:, at], src(t), -3.0e38)
                        step(ins)
                return ins

            for j in range(2 * PH):
                los(B_QUERY + j + 3)
                dve.wait_ge(sem("key_scores"), j + 1)
                top16(lambda t: ps[:, 2 + j % 2, NKEYS * t:NKEYS * (t + 1)], lambda t: rest[:, t, :],
                      lambda t: top_v[:, t, j, :], lambda t: top_i[:, t, j, :]).then_inc(sem("key_scores_read"), 1)
                if j % 2:
                    h = j // 2
                    dve.wait_ge(sem("key_scores_read"), j + 1)
                    for t in range(2):
                        ins = dve.tensor_tensor(cand[:, t, :].rearrange("p (a b) -> p a b", a=TOPK),
                                                top_v[:, t, j - 1, :].unsqueeze(2).to_broadcast([P, TOPK, TOPK]),
                                                top_v[:, t, j, :].unsqueeze(1).to_broadcast([P, TOPK, TOPK]), ALU.add)
                    step(ins)
                    step(top16(lambda t: cand[:, t, :], lambda t: cand_rest[:, t, :],
                               lambda t: best[:, t, h, :], lambda t: flat[:, t, h, :]))
            los(B_PEER + 2)
            dve.tensor_tensor(soft_hk, best_hk, best_hk[:, :, 0:1].to_broadcast([P, 2 * PH, TOPK]), ALU.subtract
                              ).then_inc(sem("soft_in"), 1)
            step(dve.tensor_scalar(ab_u0, flat_u, 4, None, ALU.logical_shift_right))
            step(dve.tensor_scalar(ab_u1, flat_u, 15, None, ALU.bitwise_and))
            step(dve.tensor_copy(ab_f_flat, ab_u_flat))
            step(dve.tensor_copy(top_f.rearrange("p a b c -> p (a b c)"), top_i.rearrange("p a b c -> p (a b c)").bitcast(U32)))
            iota16 = con("iota")[:, 0:TOPK].unsqueeze(1).to_broadcast([P, PH * TOPK, TOPK])
            for half in range(2):
                for t in range(2):
                    hits = hit.rearrange("p a b c -> p (a b) c")
                    step(dve.tensor_tensor(hits, ab_f[:, half, t].rearrange("p a b -> p (a b)").unsqueeze(2).to_broadcast(
                        [P, PH * TOPK, TOPK]), iota16, ALU.is_equal))
                    step(dve.tensor_tensor(hit, hit, top_f[:, t, half:2 * PH:2, :].unsqueeze(2).to_broadcast(
                        [P, PH, TOPK, TOPK]), ALU.mult))
                    ins = dve.tensor_reduce(expert[:, half, t].rearrange("p a b -> p (a b)"), hits, AX.X, ALU.add)
                    step(ins)
            dve.wait_ge(sem("soft_exp"), 1)
            step(dve.tensor_reduce(soft_s.rearrange("p a b -> p (a b)"), soft_hk, AX.X, ALU.add))
            step(dve.reciprocal(soft_s.rearrange("p a b -> p (a b)"), soft_s.rearrange("p a b -> p (a b)")))
            dve.tensor_tensor(soft_hk, soft_hk, soft_s.rearrange("p a b -> p (a b)").unsqueeze(2).to_broadcast(
                [P, 2 * PH, TOPK]), ALU.mult).then_inc(sem("route_ready"), 1)
            dve.wait_ge(sem("route_t_ready"), 3)

            def one_hot(g, j, tok):
                dve.tensor_scalar(one1[:, g, j, :], con("iota"), route_t[:, 0, tok], None, ALU.is_equal)
                return dve.tensor_scalar(one2[:, g, j, :], con("iota"), route_t[:, 1, tok], route_t[:, 2, tok],
                                         ALU.is_equal, ALU.mult)

            for g in range(2):
                for j in range(4):
                    ins = one_hot(g, j, slice(4 * g + j, 4 * g + j + 1))
                ins.then_inc(sem("one_hot_ready"), 1)
            with dve.Fori(1, NQ // 8) as i:
                for g in range(2):
                    dve.wait_ge(sem("g_product"), 2 * i + (g - 1))
                    for j in range(4):
                        ins = one_hot(g, j, bass.ds(8 * i + (4 * g + j), 1))
                    ins.then_inc(sem("one_hot_ready"), 1)

            def chunk(c):
                b = c.mod(2)
                dve.wait_ge(sem("gelu_done"), c.plus(1).value())
                dve.tensor_tensor(hf[:, b, :], ge[:, b, :], G[:, :, bass.ds(c.value(), 1)].rearrange("p t e -> p (t e)"),
                                  ALU.mult).then_inc(sem("act_used"), 1)
                dve.wait_ge(sem("act_used"), c.plus(1).value())
                if c.first >= 2:
                    dve.wait_ge(sem("block_used"), c.value(B_PEER + 2 * (c.first - 2) + 3, 2 * c.stride))
                dve.tensor_copy(h_op[:, b, 0, :], hf[:, b, :]).then_inc(sem("act_hi"), 1)
                dve.wait_ge(sem("act_hi"), c.plus(1).value())
                dve.tensor_tensor(h_op[:, b, 1, :], hf[:, b, :], h_op[:, b, 0, :].bitcast(F32), ALU.subtract
                                  ).then_inc(sem("acts_ready"), 1)

            dve.wait_ge(sem("g_ready"), NQ // 4)
            los(B_PEER + 3)
            for c in range(2):
                chunk(At(c))
                lo(At(B_PEER + 4 + 2 * c))
            with dve.Fori(0, (NKEYS - 4) // 2) as i:
                for c in range(2):
                    chunk(At(2 + c, i, 2))
                    lo(At(B_PEER + 8 + 2 * c, i, 4))
            ahead[0] = B_PEER + 8 + 2 * (NKEYS - 4)
            chunk(At(NKEYS - 2))
            los(B_PEER + 2 * NKEYS)
            chunk(At(NKEYS - 1))

            def add_turned(r):
                dve.wait_ge(sem("sum_turned"), r + 1)
                dve.tensor_tensor(flat2(res[:, :, :]), banks(0, 4), flat2(res[:, :, :]), ALU.add).then_inc(sem("res_ready"), 1)

            los(B_IN2 + 2)
            add_turned(0)
            norm(R_MIX, res, "mix", NQ)
            los(B_OUT2 + 2)
            dve.wait_ge(sem("bank_free"), M_OUT2)
            step(dve.tensor_tensor(flat2(conv_u), flat2(proj2[:, 2:4, :]), flat2(proj2[:, 4:6, :]), ALU.mult))
            for t in range(2):
                w = [pcol("scw", 3 * t + j) for j in range(3)]
                step(dve.tensor_scalar(conv_y[:, t, :], conv_u[:, t, :], w[2], pcol("scb", t), ALU.mult, ALU.add))
                for back in (1, 2):
                    step(dve.scalar_tensor_tensor(out=conv_y[:, t, back:NQ], in0=conv_u[:, t, 0:NQ - back], scalar=w[2 - back],
                                                  in1=conv_y[:, t, back:NQ], op0=ALU.mult, op1=ALU.add))
            dve.tensor_tensor(flat2(conv_y), flat2(conv_y), flat2(proj2[:, 0:2, :]), ALU.mult).then_inc(sem("mix_ready"), 1)
            dve.wait_ge(sem("gate_ln"), 1)
            step(dve.tensor_scalar(z, z, 0.0, None, ALU.min))
            step(dve.tensor_tensor(log_a, z, z2, ALU.subtract))
            step(dve.tensor_scalar(log_a, log_a, 1.0 / 16, None, ALU.mult))
            for n in range(NCH):
                c = slice(CHUNK * n, CHUNK * n + CHUNK)
                ins = dve.tensor_tensor_scan(csum[:, c], ones[:, 0:CHUNK], log_a[:, c], 0.0, ALU.mult, ALU.add)
            ins.then_inc(sem("csum_ready"), 1)
            dve.wait_ge(sem("gla_exp"), 2)
            dve.scalar_tensor_tensor(out=qd, in0=proj2[:, 18, :], scalar=GDK ** -0.5, in1=e_pos, op0=ALU.mult, op1=ALU.mult)
            dve.tensor_tensor(kd, proj2[:, 19, :], e_neg, ALU.mult).then_inc(sem("gla_qk"), 1)
            dve.wait_ge(sem("gla_exp"), 3)
            dve.tensor_tensor(e_end, e_end, proj2[:, 19, :], ALU.mult).then_inc(sem("gla_end"), 1)
            for t in range(2):
                dve.wait_ge(sem("mv_turned"), t + 1)
                dve.tensor_copy(v_moba[:, t, :], ps[:, 6 + t, :]).then_inc(sem("mv_ready"), 1)
            dve.wait_ge(sem("gla_scores"), 1)
            dve.wait_ge(sem("cst2_loaded"), 32)
            dve.tensor_tensor(a_gla.rearrange("p h n c -> p h (n c)").rearrange("p h (n c) -> p h n c", n=NCH),
                              ps[0:CHUNK, 4:8, 0:NQ].rearrange("p h (n c) -> p h n c", n=NCH),
                              con("gmask", CHUNK, cst2).unsqueeze(1).unsqueeze(1).to_broadcast([CHUNK, GH, NCH, CHUNK]),
                              ALU.mult).then_inc(sem("gla_a"), 1)
            step(dve.memset(state[:, 0, :], 0.0))
            for n in range(NCH - 1):
                dve.wait_ge(sem("gla_update"), n + 1)
                step(dve.tensor_tensor(upd[:, n, :], ps[:, n % 2, 0:256], con("gblk", at=cst2), ALU.mult))
                ins = dve.scalar_tensor_tensor(out=state[:, n + 1, :], in0=state[:, n, :], scalar=decay[:, n:n + 1],
                                               in1=upd[:, n, :], op0=ALU.mult, op1=ALU.add)
                ins.then_inc(sem("gla_state"), 1)
                dve.wait_ge(sem("gla_state"), n + 1)
            dve.wait_ge(sem("gla_root"), 1)
            step(dve.reciprocal(acc_sb[:, 0:512], acc_sb[:, 0:512]))
            step(dve.scalar_tensor_tensor(out=flat2(y_gla), in0=flat2(o_gla), scalar=pcol("gla"), in1=acc_sb[:, 0:512],
                                          op0=ALU.mult, op1=ALU.mult))
            dve.wait_ge(sem("silu_ready"), 1)
            dve.tensor_tensor(flat2(y_gla), flat2(y_gla), flat2(silu_o), ALU.mult).then_inc(sem("mix_ready"), 1)
            for w, (src, a) in enumerate(((conv_y, 0), (y_gla, 6))):
                dve.wait_ge(sem("mix_hi"), w + 1)
                dve.tensor_tensor(x_op[:, 1, a * NQ:(a + 2) * NQ], flat2(src), x_op[:, 0, a * NQ:(a + 2) * NQ].bitcast(F32),
                                  ALU.subtract).then_inc(sem("mix_lo"), 1)
            attention(U_MOBA, U_X)
            for k in range(KT):
                los(B_OUT2 + k + 3)
                add_residual(B_OUT2 + k, M_OUT2 + k, res[:, k, :], res[:, k, :])
            dve.wait_ge(sem("bank_free"), M_XQ)
            norm(R_XATTN, res, "xattn", NQ)
            los(B_XQ + 4)
            attention(U_X, U_END)
            for b in range(2):
                dve.wait_ge(sem("block_used"), B_XO + b + 1)
                four = flat2(res[:, 4 * b:4 * b + 4, :])
                dve.tensor_tensor(four, banks(2 * b, 2), four, ALU.add).then_inc(sem("bank_free"), 1)
            los(B_FFN + 2)
            dve.wait_ge(sem("bank_free"), M_FFN)
            norm(R_FFN, res, "ffn2", NQ)

            def conv(p):
                for half, buf in enumerate((conv_a, conv_g)):
                    dve.wait_ge(sem("tap_done"), p.value(2 * p.first + half + 1, 2 * p.stride))
                    for back, done in ((1, "conv_step"), (2, "bank_free")):
                        a = PARAMS["cw"][0] + 3 * half + 2 - back
                        dve.scalar_tensor_tensor(out=buf[:, p.mod(2), back:NQ], in0=ps[:, half, 0:NQ - back],
                                                 scalar=par[:, bass.ds(p.value(a + 6 * p.first, 6 * p.stride), 1)],
                                                 in1=buf[:, p.mod(2), back:NQ], op0=ALU.mult, op1=ALU.add
                                                 ).then_inc(sem(done), 1)
                        if back == 1:
                            dve.wait_ge(sem("conv_step"), p.value(2 * p.first + half + 1, 2 * p.stride))

            def gate(p):
                b = p.mod(2)
                dve.wait_ge(sem("bank_free"), p.value(M_FFN + 2 * p.first + 2, 2 * p.stride))
                dve.wait_ge(sem("silu_done"), p.plus(1).value())
                dve.tensor_tensor(hf[:, b, :], act_a[:, b, :], conv_g[:, b, :], ALU.mult).then_inc(sem("act_used"), 1)
                dve.wait_ge(sem("act_used"), p.value(NKEYS + p.first + 1))
                if p.first >= 2:
                    dve.wait_ge(sem("block_used"), p.value(B_FFN + 3 * (p.first - 2) + 5, 3 * p.stride))
                dve.tensor_copy(h_op[:, b, 0, :], hf[:, b, :]).then_inc(sem("act_hi"), 1)
                dve.wait_ge(sem("act_hi"), p.value(NKEYS + p.first + 1))
                dve.tensor_tensor(h_op[:, b, 1, :], hf[:, b, :], h_op[:, b, 0, :].bitcast(F32), ALU.subtract
                                  ).then_inc(sem("acts_ready"), 1)

            def tile(p):
                n = At(B_FFN + 3 * p.first + 3, p.i, 3 * p.stride)
                if n.mod(2):
                    lo(n)
                conv(p)
                if n.plus(1).mod(2):
                    lo(n.plus(1))
                gate(p)
                if n.plus(2).mod(2):
                    lo(n.plus(2))

            los(B_FFN + 3)
            tile(At(0))
            with dve.Fori(0, (FT - 2) // 4) as i:
                for j in range(4):
                    tile(At(1 + j, i, 4))
            conv(At(FT - 1))
            gate(At(FT - 1))
            add_turned(1)
            norm(R_FINAL, res, "final", NQ, operand=False)

        @block.tensor
        def _(pe):
            def parts(s, wa, wb, k_hi, k_lo):
                return ((w_hi[:, s, wa:wb], k_hi), (w_hi[:, s, wa:wb], k_lo), (w_lo[:, s, wa:wb], k_hi))

            def arrived(n):
                pe.wait_ge(sem(f"lo_done{n.mod(2)}"), n.div(2) + 1)

            def project(n, m_bank, T=NQ, free=None):
                arrived(n)
                if free is not None:
                    pe.wait_ge(*free)
                for k in range(KT):
                    for j, (w, x) in enumerate(parts(n.mod(RING), k * P, k * P + P, x_k(0, k, T), x_k(1, k, T))):
                        mm = pe.matmul(ps[:, m_bank, 0:T], w, x, start=(k == 0 and j == 0), stop=(k == KT - 1 and j == 2))
                mm.then_inc(sem("block_used"), 1)

            def bank_free(m):
                return (sem("bank_free"), m - 1) if m >= 2 else None

            def projections(n, m, count, T=NQ):
                for j in range(count):
                    project(At(n + j), (m + j) % 2, T, bank_free(m + j))

            def norm(r, T):
                pe.wait_ge(sem("rms_squares"), r + 1)
                for k in range(KT):
                    mm = pe.matmul(ps[:, 2, 0:T], ones[:, :], sq[:, k * T:(k + 1) * T], start=(k == 0), stop=(k == KT - 1))
                mm.then_inc(sem("rms_sum"), 1)

            def operand(r):
                pe.wait_ge(sem("rms_x"), r + 1)

            def spread(b, stationary, src, n, rows=P):
                for a in range(0, n, 512):
                    e = min(n, a + 512)
                    mm = pe.matmul(ps[0:rows, b + a // 512, 0:e - a], stationary, src[:, a:e], start=True, stop=True)
                return mm

            pe.wait_ge(sem("ones_set"), 1)
            norm(R_MEM, NQ)
            pe.wait_ge(sem("rel_ready"), 1)
            pe.wait_ge(sem("cst_loaded"), 16)
            for h in range(DH):
                if h:
                    pe.wait_ge(sem("line_ready"), h)
                for a, e, b in ((0, LINE // 2, 4), (LINE // 2, LINE, 5)):
                    mm = pe.matmul(ps[:, b, 0:e - a], rel_rep[:, h, :], con("bucket", BUCKETS, cst)[:, a:e], start=True, stop=True)
                mm.then_inc(sem("line_done"), 1)
            operand(R_MEM)
            projections(B_MEM, M_MEM, 4)
            norm(R_ATTN, NK)
            pe.wait_ge(sem("bank_free"), M_IN)
            pe.wait_ge(sem("kept_loaded"), 16)
            for t in range(2):
                for f in range(2):
                    mm = pe.transpose(ps[:, 3, (2 * t + f) * P:(2 * t + f + 1) * P], v_mem_t[:, f, t * P:t * P + P], ident)
            mm.then_inc(sem("v_mem_turned"), 1)
            operand(R_ATTN)
            projections(B_IN, M_IN, 17, NK)
            for w, n in enumerate((NQ, NK)):
                pe.wait_ge(sem("lat_squares"), w + 1)
                for k in range(2):
                    a = w * 2 * NK + k * n
                    mm = pe.matmul(ps[:, 2 + w, 0:n], ones[:, :], sq[:, a:a + n], start=(k == 0), stop=(k == 1))
                mm.then_inc(sem("lat_sum"), 1)
            pe.wait_ge(sem("wu_loaded"), 32)
            pe.wait_ge(sem("lat_ready"), 1)
            pe.wait_ge(sem("line_ready"), DH)
            for h in range(HEADS):
                for k in range(2):
                    mm = pe.matmul(ps[0:QK, 4 + h // 2, (h % 2) * NQ:(h % 2 + 1) * NQ], w_uq[:, k, QK * h:QK * h + QK],
                                   cqn[:, k, :], start=(k == 0), stop=(k == 1))
            mm.then_inc(sem("q_product"), 1)
            pe.wait_ge(sem("lat_ready"), 2)
            for t in range(3):
                rows = min(P, NK - P * t)
                if t == 2:
                    pe.wait_ge(sem("v_ready"), 1)
                for k in range(2):
                    mm = pe.matmul(ps[0:rows, 2 + t % 2, :], ckvn[:, k, P * t:P * t + rows], w_ukv[:, k, 512:1024],
                                   start=(k == 0), stop=(k == 1))
                mm.then_inc(sem("v_product"), 1)
            pe.wait_ge(sem("qk_squares"), 1)
            spread(4, ones[0:QK, 0:QK], sq[0:QK, :], HEADS * NQ, QK).then_inc(sem("qk_sum"), 1)
            pe.wait_ge(sem("qk_root"), 1)
            for w in range(2):
                if w:
                    pe.wait_ge(sem("k_raw"), 2)
                for h in range(4):
                    for k in range(2):
                        a = NOPE * (4 * w + h)
                        mm = pe.matmul(ps[0:NOPE, 4 + h, 0:NK], w_ukv[:, k, a:a + NOPE], ckvn[:, k, :], start=(k == 0), stop=(k == 1))
                mm.then_inc(sem("k_product"), 1)
            pe.wait_ge(sem("qk_normed"), 1)
            pe.wait_ge(sem("k_raw"), 3)
            spread(4, con("rot", QK, cst), flat2(q_mla), HEADS * NQ, QK).then_inc(sem("qk_turned"), 1)
            pe.wait_ge(sem("qk_squares"), 2)
            pe.wait_ge(sem("v_ready"), 3)
            pe.wait_ge(sem("qk_ready"), 1)
            spread(2, ones[0:QK, 0:QK], sq[0:QK, :], HEADS * NK, QK).then_inc(sem("qk_sum"), 1)
            pe.wait_ge(sem("qk_normed"), 2)
            spread(2, con("rot", QK, cst), flat2(k_mla), HEADS * NK, QK).then_inc(sem("qk_turned"), 1)
            pe.wait_ge(sem("qk_ready"), 2)
            for w, n in enumerate((NQ, NK)):
                pe.wait_ge(sem("d_squares"), w + 1)
                if w:
                    pe.wait_ge(sem("d_root"), w)
                spread(2, con("blk64", at=cst), sq, DH * n).then_inc(sem("d_sum"), 1)
            for t in range(3):
                rows = min(P, NK - P * t)
                if t == 2:
                    pe.wait_ge(sem("dv_ready"), 1)
                for h in range(DH):
                    mm = pe.transpose(ps[0:rows, 6 + t % 2, h * P:h * P + P], proj[:, 12 + h, P * t:P * t + rows], ident)
                mm.then_inc(sem("dv_turned"), 1)
            pe.wait_ge(sem("lam_ready"), 1)
            pe.matmul(ps[:, 5, 0:2], ones[0:64, :], lam[0:64, 0:2], start=True, stop=True).then_inc(sem("lam_sum"), 1)
            pe.wait_ge(sem("d_root"), 2)
            pe.wait_ge(sem("d_ready"), 2)
            pe.wait_ge(sem("dv_ready"), 3)
            pe.wait_ge(sem("lam_exp"), 1)

            def scores(u):
                x = units[u]
                h, n, b = x["head"], x["keys"], 2 + 2 * (u % 2)
                if u >= 2:
                    pe.wait_ge(sem("scores_read"), u - 1)
                for t in range(2):
                    c = slice(P * t, P * t + P)
                    half = slice(64 * (h % 2), 64 * (h % 2) + 64)
                    if x["kind"] == "mla":
                        q, k = q_mla[:, h, c], k_mla[:, h, :]
                    elif x["kind"] == "diff":
                        half = slice(64 * x["map"], 64 * x["map"] + 64)
                        q, k = dqn[half, h, c], dkn[half, h, :]
                    elif x["kind"] == "moba":
                        q, k = proj2[half, 6 + h // 2, c], proj2[half, 10 + h // 2, :]
                    else:
                        q, k = q_x[half, h // 2, c], k_mem[half, h // 2, :]
                    mm = pe.matmul(ps[:, b + t, 0:n], q, k, start=True, stop=True)
                mm.then_inc(sem("scores_done"), 1)

            def weigh(u):
                x = units[u]
                o, h, n = x["out"], x["head"], x["keys"]
                if o is None:
                    return
                pe.wait_ge(sem("probs_normed"), u + 1)
                if o:
                    pe.wait_ge(sem("probs_ready"), o)
                    pe.wait_ge(sem("y_hi"), o)
                for t in range(2):
                    for j in range(2):
                        mm = pe.transpose(ps[:, 6, j * NQ + t * P:j * NQ + t * P + P], scores_sb[:, u % 3, t, j * P:j * P + P], ident)
                    if n > NQ:
                        mm = pe.transpose(ps[0:N_META, 7, NQ + t * P:NQ + t * P + P], scores_sb[:, u % 3, t, NQ:n], ident)
                mm.then_inc(sem("probs_turned"), 1)
                pe.wait_ge(sem("probs_ready"), o + 1)
                if n > NQ:
                    pe.wait_ge(sem("tail_ready"), n_tail[u] + 1)
                if x["kind"] != "diff" and o and units[u - 1]["kind"] != "diff":
                    pe.wait_ge(sem("y_ready"), y_before(u))
                rows = slice(0, P) if x["kind"] == "diff" else slice(64 * (h % 2), 64 * (h % 2) + 64)
                tiles = 3 if n > NQ else 2
                for t in range(tiles):
                    k = min(P, n - P * t)
                    if x["kind"] == "mla":
                        v = v_mla[0:k, t, 64 * h:64 * h + 64]
                    elif x["kind"] == "diff":
                        v = v_diff[0:k, t, P * h:P * h + P]
                    elif x["kind"] == "moba":
                        v = v_moba[0:k, t, 64 * h:64 * h + 64]
                    else:
                        v = v_mem[0:k, t, 64 * h:64 * h + 64]
                    mm = pe.matmul(ps[rows, 7, 0:NQ], v, probs_t[0:k, o % 2, t, :], start=(t == 0), stop=(t == tiles - 1))
                mm.then_inc(sem("out_done"), 1)

            def y_before(u):
                return u if u < U_DIFF else HEADS + 1 + (u - U_MOBA)

            def attention(a, b):
                scores(a)
                for u in range(a, b):
                    if u + 1 < b:
                        scores(u + 1)
                    if u == U_DIFF + 1:
                        pe.wait_ge(sem("y_ready"), HEADS)
                    weigh(u)

            attention(U_MLA, U_MOBA)
            pe.wait_ge(sem("sub_squares"), 1)
            spread(2, ones[:, :], sq, DH * NQ).then_inc(sem("sub_sum"), 1)
            pe.wait_ge(sem("y_ready"), HEADS + 1)
            projections(B_OUT, M_OUT, KT)
            norm(R_PEER, NQ)
            operand(R_PEER)
            pe.wait_ge(sem("sub_keys_loaded"), 16)

            def key_scores(j):
                pe.wait_ge(sem("bank_free"), M_QUERY + j + 1)
                if j >= 2:
                    pe.wait_ge(sem("key_scores_read"), j - 1)
                for t in range(2):
                    mm = pe.matmul(ps[:, 2 + j % 2, NKEYS * t:NKEYS * (t + 1)], q_peer[:, j, P * t:P * t + P], sub_keys[:, j, :],
                                   start=True, stop=True)
                mm.then_inc(sem("key_scores"), 1)

            for j in range(2 * PH):
                project(At(B_QUERY + j), (M_QUERY + j) % 2, NQ, bank_free(M_QUERY + j))
                if j:
                    key_scores(j - 1)
            key_scores(2 * PH - 1)
            pe.wait_ge(sem("route_ready"), 1)
            for w in range(3):
                for t in range(2):
                    src = (expert[:, w, t] if w < 2 else soft[:, t]).rearrange("p a b -> p (a b)")
                    mm = pe.transpose(ps[:, 2 + w, P * t:P * t + P], src, ident)
                mm.then_inc(sem("route_turned"), 1)
            pe.wait_ge(sem("route_t_ready"), 3)

            def g_product(g):
                for j in range(4):
                    mm = pe.matmul(ps[:, 2 + g % 2, P * j:P * j + P], one1[:, g % 2, j, :], one2[:, g % 2, j, :], start=True, stop=True)
                mm.then_inc(sem("g_product"), 1)

            for g in range(2):
                pe.wait_ge(sem("one_hot_ready"), g + 1)
                g_product(g)
            with pe.Fori(1, NQ // 8) as i:
                for g in range(2):
                    pe.wait_ge(sem("one_hot_ready"), 2 * i + (g + 1))
                    pe.wait_ge(sem("g_ready"), 2 * i + (g - 1))
                    g_product(g)

            def expand(n, b, first, last):
                s = n.mod(RING)
                for t in range(2):
                    x_hi, x_lo = (h_op[:, b, j, P * t:P * t + P] for j in range(2))
                    for half in range(2):
                        c = slice(512 * half, 512 * half + 512)
                        for j, (x, w) in enumerate(((x_hi, w_hi), (x_hi, w_lo), (x_lo, w_hi))):
                            mm = pe.matmul(ps[:, 4 + 2 * t + half, :], x, w[:, s, c], start=(first and j == 0),
                                           stop=(last and j == 2), skip_group_check=True)
                return mm

            def chunk(c, first=False):
                n = At(B_PEER + 1 + 2 * c.first, c.i, 2 * c.stride)
                project(n, (M_PEER + c.first + 1) % 2, NQ, (sem("gelu_done"), c.value()) if c.first else None)
                arrived(n.plus(1))
                pe.wait_ge(sem("acts_ready"), c.plus(1).value())
                expand(n.plus(1), c.mod(2), first, False).then_inc(sem("block_used"), 1)

            pe.wait_ge(sem("bank_free"), M_PEER)
            project(At(B_PEER), M_PEER % 2, NQ)
            for c in range(2):
                chunk(At(c), c == 0)
            with pe.Fori(0, (NKEYS - 4) // 2) as i:
                for c in range(2):
                    chunk(At(2 + c, i, 2))
            chunk(At(NKEYS - 2))
            arrived(At(B_PEER + 2 * NKEYS - 1))
            pe.wait_ge(sem("acts_ready"), NKEYS)
            mm = expand(At(B_PEER + 2 * NKEYS - 1), (NKEYS - 1) % 2, False, True)
            mm.then_inc(sem("block_used"), 1)

            def turn_sum(r):
                pe.wait_ge(sem("sum_out"), r + 1)
                for k in range(KT):
                    for t in range(2):
                        a = (k % 2) * NQ + P * t
                        mm = pe.transpose(ps[:, k // 2, a:a + P], acc_sb[:, 1024 * t + P * k:1024 * t + P * k + P], ident)
                mm.then_inc(sem("sum_turned"), 1)

            turn_sum(0)
            norm(R_MIX, NQ)
            operand(R_MIX)
            projections(B_IN2, M_IN2, 25)
            pe.wait_ge(sem("bank_free"), M_OUT2)
            pe.wait_ge(sem("cst2_loaded"), 32)
            pe.matmul(ps[:, 2, 0:NQ], w_gate, proj2[0:16, 24, :], start=True, stop=True).then_inc(sem("gate_product"), 1)
            for t in range(2):
                for f in range(4):
                    mm = pe.transpose(ps[:, 6 + t, f * P:f * P + P], proj2[:, 14 + f, P * t:P * t + P], ident)
                mm.then_inc(sem("mv_turned"), 1)
            pe.wait_ge(sem("gate_z"), 1)
            pe.wait_ge(sem("gla_end"), 1)
            for n in range(NCH):
                c = slice(CHUNK * n, CHUNK * n + CHUNK)
                for f in range(2):
                    pe.transpose(banks(2, 2)[0:CHUNK, n * 256 + f * P:n * 256 + f * P + P], proj2[:, 20 + f, c], ident)
                mm = pe.transpose(ps[0:CHUNK, 4, n * P:n * P + P], e_end[:, c], ident)
            mm.then_inc(sem("gla_turned"), 1)
            pe.wait_ge(sem("gla_v"), 2)
            pe.wait_ge(sem("gla_qk"), 1)
            pe.wait_ge(sem("mv_ready"), 2)
            for h in range(GH):
                r = slice(GDK * h, GDK * h + GDK)
                for n in range(NCH):
                    c = slice(CHUNK * n, CHUNK * n + CHUNK)
                    mm = pe.matmul(ps[0:CHUNK, 4 + h, c], kd[r, c], qd[r, c], start=True, stop=True)
            mm.then_inc(sem("gla_scores"), 1)
            for n in range(NCH - 1):
                if n >= 2:
                    pe.wait_ge(sem("gla_state"), n - 1)
                pe.matmul(ps[:, n % 2, 0:256], kend_t[:, n, :], v_gla[:, n, :], start=True, stop=True
                          ).then_inc(sem("gla_update"), 1)
            pe.wait_ge(sem("gla_a"), 1)
            pe.wait_ge(sem("gla_state"), NCH - 1)
            for f in range(2):
                for n in range(NCH):
                    c = slice(CHUNK * n, CHUNK * n + CHUNK)
                    pe.matmul(ps[:, 2 + f, c], state[:, n, P * f:P * f + P], qd[:, c], start=True, stop=False,
                              skip_group_check=True)
                    for e in range(2):
                        h = 2 * f + e
                        mm = pe.matmul(ps[GDV * e:GDV * e + GDV, 2 + f, c], v_gla[:, n, GDV * h:GDV * h + GDV],
                                       a_gla[:, h, n, :], start=False, stop=True, skip_group_check=True)
            mm.then_inc(sem("gla_out"), 1)
            pe.wait_ge(sem("gla_squares"), 1)
            spread(4, con("blk64", at=cst2), sq, 2 * NQ).then_inc(sem("gla_sum"), 1)
            pe.wait_ge(sem("gla_root"), 1)
            attention(U_MOBA, U_X)
            pe.wait_ge(sem("mix_lo"), 2)
            pe.wait_ge(sem("y_ready"), HEADS + 1 + MH)
            projections(B_OUT2, M_OUT2, KT)
            norm(R_XATTN, NQ)
            operand(R_XATTN)
            projections(B_XQ, M_XQ, 2)
            pe.wait_ge(sem("bank_free"), M_XO)
            pe.wait_ge(sem("v_mem_ready"), 1)
            attention(U_X, U_END)
            pe.wait_ge(sem("y_ready"), HEADS + 1 + MH + XH)
            for b in range(2):
                n = At(B_XO + b)
                arrived(n)
                for f in range(4):
                    for k in range(2):
                        a = (2 * f + k) * P
                        for j, (w, x) in enumerate(parts(n.mod(RING), a, a + P, x_k(0, k, NQ), x_k(1, k, NQ))):
                            mm = pe.matmul(ps[:, 2 * b + f // 2, (f % 2) * NQ:(f % 2 + 1) * NQ], w, x,
                                           start=(k == 0 and j == 0), stop=(k == 1 and j == 2))
                mm.then_inc(sem("block_used"), 1)
            norm(R_FFN, NQ)
            operand(R_FFN)

            def up(p, n):
                for half in range(2):
                    free = (sem("bank_free"), p.value(M_FFN + 2 * p.first - 1 + half, 2 * p.stride)) if p.first else None
                    project(n.plus(half), half, NQ, free)

            def down(p, n, last=False):
                arrived(n)
                pe.wait_ge(sem("acts_ready"), p.value(NKEYS + p.first + 1))
                expand(n, p.mod(2), p.first == 0, last).then_inc(sem("block_used"), 1)

            def tile(p):
                n = At(B_FFN + 2 + 3 * p.first, p.i, 3 * p.stride)
                up(p.plus(1), n)
                down(p, n.plus(2))

            up(At(0), At(B_FFN))
            tile(At(0))
            with pe.Fori(0, (FT - 2) // 4) as i:
                for j in range(4):
                    tile(At(1 + j, i, 4))
            down(At(FT - 1), At(N_BLOCKS - 1), last=True)
            turn_sum(1)
            norm(R_FINAL, NQ)


def constants():
    c = np.zeros((P, N_CONSTS), np.float32)

    def put(name, a):
        c[:a.shape[0], CONSTS[name][0]:CONSTS[name][0] + a.shape[1]] = a

    put("ident", np.eye(P, dtype=np.float32))
    put("blk64", np.kron(np.eye(2), np.ones((64, 64))))
    put("iota", np.tile(np.arange(P), (P, 1)))
    half = ROPE // 2
    rot = np.zeros((QK, QK))
    for j in range(half):
        rot[NOPE + half + j, NOPE + j] = -1.0
        rot[NOPE + j, NOPE + half + j] = 1.0
    put("rot", rot)
    freq = np.float32(10000.0) ** (-np.arange(half, dtype=np.float32) / np.float32(half))
    angle = np.arange(NK, dtype=np.float32)[:, None] * freq[None, :]
    cos, sin = np.ones((QK, NK)), np.zeros((QK, NK))
    for j in range(2):
        cos[NOPE + half * j:NOPE + half * (j + 1)] = np.cos(angle).T
        sin[NOPE + half * j:NOPE + half * (j + 1)] = np.sin(angle).T
    put("cos", cos)
    put("sin", sin)
    p = np.arange(P)[:, None, None]
    t = np.arange(2)[None, :, None]
    d = N_META + P * t + p - np.arange(NK)[None, None, :]
    put("mask", np.where(d >= 0, 0.0, NEG).reshape(P, -1))
    n = np.maximum(FAR - np.arange(LINE), 0)
    exact = BUCKETS // 2
    large = exact + (np.log(np.maximum(n, 1).astype(np.float32) / np.float32(exact))
                     / np.float32(math.log(MAX_DIST / exact)) * np.float32(BUCKETS - exact)).astype(np.int32)
    bucket = np.where(n < exact, n, np.minimum(large, BUCKETS - 1))
    put("bucket", (bucket[None, :] == np.arange(BUCKETS)[:, None]).astype(np.float32))
    d = P * t + p - np.arange(NQ)[None, None, :]
    put("rel", np.where(d >= 0, -d, -1e32).reshape(P, -1))
    put("gmask", (np.arange(CHUNK)[:, None] <= np.arange(CHUNK)[None, :]).astype(np.float32))
    put("gblk", (np.arange(P)[:, None] // GDK == np.arange(256)[None, :] // GDV).astype(np.float32))
    return c


def layout(a):
    def lay(name):
        return np.asarray(a[name], np.float32)

    def tiles(w):
        return w.reshape(KT, P, -1, P).transpose(2, 1, 0, 3).reshape(-1, P, D)

    def pad(w, rows, cols):
        out = np.zeros((rows, cols), np.float32)
        out[:w.shape[0], :w.shape[1]] = w
        return out

    def feature_major(x):
        return np.ascontiguousarray(x.T.reshape(KT, P, -1).transpose(1, 0, 2).reshape(P, -1))

    w_in = lay("w_in")[0]
    rope = np.zeros((D, P), np.float32)
    rope[:, NOPE:QK] = w_in[:, 512:544]
    u = lay("peer_u")[0].reshape(NKEYS, NKEYS, KT, P).transpose(1, 3, 2, 0).reshape(NKEYS, P, D)
    v = lay("peer_v")[0].reshape(NKEYS, NKEYS, D).transpose(1, 0, 2)
    up = lay("ffn_w_up_2")[0]
    up_a, up_g = (tiles(pad(up[:, FF * j:FF * (j + 1)], D, FT * P)) for j in range(2))
    down = pad(lay("ffn_w_down_2")[0], FT * P, D).reshape(FT, P, D)
    wo = lay("xattn_wo_2")[0].reshape(2, P, 2, 4, P).transpose(2, 1, 3, 0, 4).reshape(2, P, D)
    peer = [u[0]] + [w for c in range(NKEYS - 1) for w in (u[c + 1], v[c])] + [v[-1]]
    ffn = [up_a[0], up_g[0]] + [w for t in range(FT - 1) for w in (up_a[t + 1], up_g[t + 1], down[t])] + [down[-1]]
    blocks = np.empty((N_BLOCKS, P, D), np.float32)
    at = 0
    for group in (tiles(lay("xattn_wkv_2")[0]), tiles(np.concatenate([w_in[:, :512], w_in[:, 544:], rope], axis=1)),
                  tiles(lay("w_out")[0]), tiles(lay("peer_w_query")[0]), peer, tiles(pad(lay("w_in_2")[0], D, 25 * P)),
                  tiles(lay("w_out_2")[0]), tiles(lay("xattn_wq_2")[0]), wo, ffn):
        for w in group:
            blocks[at] = w
            at += 1
    assert at == N_BLOCKS

    params = np.zeros((P, N_PARAMS), np.float32)

    def put(name, v, k=0, twice=False):
        v = np.concatenate([v, v]) if twice else v
        n = -(-v.size // P)
        cols = np.zeros(n * P, np.float32)
        cols[:v.size] = v
        params[:, PARAMS[name][0] + k:PARAMS[name][0] + k + n] = cols.reshape(n, P).T

    for name, source in (("attn", "attn_norm"), ("qn", "mla_q_norm"), ("kvn", "mla_kv_norm"), ("qkq", "mla_qk_norm_q"),
                         ("qkk", "mla_qk_norm_k"), ("subln", "diff_subln"), ("ffn", "ffn_norm"), ("mix", "norm_mix_g_2"),
                         ("scb", "sc_conv_b_2"), ("gate_b", "gla_b_gate_2"), ("xattn", "norm_xattn_g_2"),
                         ("mem", "norm_mem_g_2"), ("ffn2", "norm_ffn_g_2")):
        put(name, lay(source)[0])
    put("final", lay("final_norm_g_2"))
    for name, source in (("dq", "diff_q_norm"), ("dk", "diff_k_norm"), ("gla", "gla_norm_g_2")):
        put(name, lay(source)[0], twice=True)
    for k, source in enumerate(("diff_lambda_q1", "diff_lambda_k1", "diff_lambda_q2", "diff_lambda_k2")):
        put("lam", lay(source)[0], k)
    for t in range(2):
        for j in range(3):
            put("scw", lay("sc_conv_w_2")[0, j, P * t:P * t + P], 3 * t + j)
    cw, cb = lay("ffn_conv_w_2")[0], lay("ffn_conv_b_2")[0]
    for half in range(2):
        for t in range(FT):
            f = slice(FF * half + P * t, FF * half + min(P * t + P, FF))
            put("cb", cb[f], 2 * t + half)
            for j in range(3):
                put("cw", cw[j, f], 6 * t + 3 * half + j)

    ukv = lay("mla_w_ukv")[0].reshape(2, P, HEADS, 2, 64).transpose(1, 0, 3, 2, 4).reshape(P, -1)
    return {
        "blocks": blocks,
        "params": params,
        "consts": constants(),
        "h_t": feature_major(np.concatenate([lay("meta_tokens"), lay("x")[0]], axis=0)),
        "mem_t": feature_major(lay("mem_2")[0]),
        "rel_bias": lay("rel_bias"),
        "w_uq": np.ascontiguousarray(lay("mla_w_uq")[0].reshape(2, P, -1).transpose(1, 0, 2).reshape(P, -1)),
        "w_ukv": np.ascontiguousarray(ukv),
        "sub_keys": np.ascontiguousarray(lay("peer_sub_keys")[0].transpose(3, 0, 1, 2).reshape(P, -1)),
        "w_gate": lay("gla_w_gate_2")[0],
    }


def kernel(**inputs):
    import concourse.bacc as bacc
    from concourse.bass_utils import run_bass_kernel_spmd

    nc = bacc.Bacc("TRN2", target_bir_lowering=False, num_devices=1, dynamic_dma_scratch_size=1024)
    arrays = layout(inputs)
    dram = {name: nc.dram_tensor(name, a.shape, F32, kind="ExternalInput").ap() for name, a in arrays.items()}
    dram["out"] = nc.dram_tensor("out", (P, KT * NQ), F32, kind="ExternalOutput").ap()
    build(nc, dram)
    out = run_bass_kernel_spmd(nc, [arrays], core_ids=[0]).results[0]["out"]
    return np.ascontiguousarray(out.reshape(P, KT, NQ).transpose(2, 1, 0).reshape(1, NQ, D))
```

```python
from contextlib import ExitStack
import math

import numpy as np
import concourse.bass as bass
from concourse import mybir

F32 = mybir.dt.float32
F32R = mybir.dt.float32r
U32 = mybir.dt.uint32
ALU = mybir.AluOpType
ACT = mybir.ActivationFunctionType
AX = mybir.AxisListType

P = 128
D = 1024
KT = D // P
NQ = 256
N_META = 16
NK = NQ + N_META
EPS = 1e-6
NEG = -1e30
RING = 4
LOADS_AHEAD = RING + 2
QK, NOPE, ROPE, HEADS = 96, 64, 32, 8
DH = 4
LAMBDA_INIT = 0.8 - 0.6 * math.exp(0.0)
BUCKETS, MAX_DIST = 32, 128
FAR = NK - 1
LINE = FAR + NQ + 1
PH, NKEYS, TOPK = 8, 128, 16
EARLY = 64
SOFT_AT = 5
EARLY_G = 32
MH, GH, GDK, GDV, CHUNK = 8, 4, 32, 64, 64
NCH = NQ // CHUNK
XH = 4
FF = 2752
FT = -(-FF // P)

B_MEM = 0
B_IN = B_MEM + 4
B_OUT = B_IN + 17
B_QUERY = B_OUT + KT
B_EARLY = B_QUERY + 4 * PH
B_BESIDE = B_QUERY + 2 * PH + EARLY - EARLY_G
B_V = B_QUERY + 2 * PH + EARLY
B_PEER = B_V + EARLY
B_IN2 = B_PEER + 2 * (NKEYS - EARLY)
B_OUT2 = B_IN2 + 25
B_XQ = B_OUT2 + KT
B_XO = B_XQ + 2
B_FFN = B_XO + 2
N_BLOCKS = B_FFN + 3 * FT
assert N_BLOCKS % RING == 0

PARAMS = {}
for _name, _n in (("attn", 8), ("qn", 2), ("kvn", 2), ("qkq", 1), ("qkk", 1), ("dq", 1), ("dk", 1), ("lam", 4),
                  ("subln", 1), ("ffn", 8), ("mix", 8), ("scw", 6), ("scb", 2), ("gate_b", 1), ("gla", 1),
                  ("xattn", 8), ("mem", 8), ("ffn2", 8), ("cw", 6 * FT), ("cb", 2 * FT), ("final", 8)):
    PARAMS[_name] = (sum(n for _, n in PARAMS.values()), _n)
N_PARAMS = sum(n for _, n in PARAMS.values())

CONSTS = {}
for _name, _n in (("ident", 128), ("iota", 128), ("blk64", 128), ("rot", QK), ("cos", NK), ("sin", NK),
                  ("mask", 2 * NK), ("bucket", LINE), ("rel", 2 * NQ), ("gmask", CHUNK), ("gblk", 256)):
    CONSTS[_name] = (sum(n for _, n in CONSTS.values()), _n)
N_CONSTS = sum(n for _, n in CONSTS.values())
N_CONSTS_KEPT = 2 * 128


def lo_owner(n):
    return "pool" if B_QUERY <= n < B_V or n % 2 == 0 else "dve"


class At:

    def __init__(self, first, i=0, stride=0):
        self.first, self.i, self.stride = first, i, stride

    def plus(self, k):
        return At(self.first + k, self.i, self.stride)

    def mod(self, m):
        assert self.stride % m == 0
        return self.first % m

    def div(self, m):
        assert self.stride % m == 0
        return self.value(self.first // m, self.stride // m)

    def value(self, first=None, stride=None):
        first = self.first if first is None else first
        stride = self.stride if stride is None else stride
        return first + self.i * stride if stride else first


def build(nc, dram):
    ctx = ExitStack()
    with ctx:
        def sb(name, shape, dt=F32):
            return ctx.enter_context(nc.sbuf_tensor(name, shape, dt))

        sems = {}

        def sem(name):
            if name not in sems:
                sems[name] = ctx.enter_context(nc.semaphore(name))
            return sems[name]

        raw = sb("raw", [P, RING, D])
        w_hi = sb("w_hi", [P, RING, D], F32R)
        w_lo = sb("w_lo", [P, RING, D], F32R)
        x_op = sb("x_op", [P, 2, KT * NK], F32R)
        res = sb("res", [P, KT, NQ])
        par = sb("par", [P, N_PARAMS])
        kept = sb("kept", [P, N_CONSTS_KEPT])
        ones = sb("ones", [P, P])
        eps = sb("eps", [P, 8])
        kv_mem = sb("kv_mem", [P, RING, NQ])
        a_out = kv_mem
        route_t = sb("route_t", [P, 3, NQ])
        work = sb("work", [P, 2, 2, 4, P])
        h_op = sb("h_op", [P, 2, 2, NQ], F32R)
        big = sb("big", [P, NKEYS * NQ])

        ps = ctx.enter_context(nc.psum_tensor("ps", [P, 8, 512], F32))

        cursor = [0]

        def area(*shape, rows=P):
            size = int(np.prod(shape))
            a = big[0:rows, cursor[0]:cursor[0] + size]
            cursor[0] += size
            assert cursor[0] <= NKEYS * NQ, cursor[0]
            names = "abcd"[:len(shape)]
            if len(shape) > 1:
                a = a.rearrange(f"p ({' '.join(names)}) -> p {' '.join(names)}", **dict(zip(names, shape)))
            return a

        sq = area(KT * NK)
        xf = area(KT * NK)
        rt = area(NK)
        rb = area(NK)
        acc_sb = area(HEADS * NK)
        scores_sb = area(3, 2, NK)
        probs_t = area(2, 3, NQ)
        row_max = area(3, 2)
        row_sum = area(3, 2)
        row_inv = area(3, 2)
        common = cursor[0]
        cst = area(N_CONSTS - N_CONSTS_KEPT)
        mem_t = res
        v_mem_t = area(2, NQ)
        h_t = area(KT, NK)
        k_mem = kv_mem[:, 0:2, :]
        v_mem = kv_mem[:, 2:4, :]
        proj = area(17, NK)
        w_uq = area(2, HEADS * QK)
        w_ukv = area(2, HEADS * 128)
        latent = area(2 * NQ + 2 * NK)
        cqn = latent[:, 0:2 * NQ].rearrange("p (a b) -> p a b", a=2)
        ckvn = latent[:, 2 * NQ:].rearrange("p (a b) -> p a b", a=2)
        q_mla = area(HEADS, NQ, rows=QK)
        k_mla = area(HEADS, NK, rows=QK)
        rope_a = acc_sb[0:QK, :].rearrange("p (h n) -> p h n", h=HEADS)
        spare = work[:, :, :, :, :].rearrange("p a b c d -> p (a b c d)")
        v_mla = spare[:, 0:3 * 512].rearrange("p (t n) -> p t n", t=3)
        rel_rep = spare[0:BUCKETS, 3 * 512:4 * 512].rearrange("p (h n) -> p h n", h=DH)
        v_diff = w_uq.rearrange("p a b -> p (a b)").rearrange("p (t n) -> p t n", t=3)
        dqn = latent[:, 0:DH * NQ].rearrange("p (a b) -> p a b", a=DH)
        dkn = area(DH, NK)
        bias = area(DH, 2, NK)
        rel_in = area(DH, rows=BUCKETS)
        line = route_t[:, :, :].rearrange("p a b -> p (a b)")[:, 0:LINE]
        lam = area(16)
        o_diff = proj.rearrange("p a b -> p (a b)")[:, 0:DH * NQ].rearrange("p (a b) -> p a b", a=DH)
        cursor[0] = common
        sub_keys = area(2 * PH, NKEYS)
        q_peer = area(2 * PH, NQ)
        top_v = area(2, 2 * PH, TOPK)
        top_i = area(2, 2 * PH, TOPK)
        top_f = area(2, 2 * PH, TOPK)
        rest = area(2, NKEYS)
        cand = area(2, TOPK * TOPK)
        cand_rest = area(2, TOPK * TOPK)
        best = area(2, PH, TOPK)
        flat = area(2, PH, TOPK)
        ab_u = area(2, 2, PH, TOPK)
        ab_f = area(2, 2, PH, TOPK)
        hit = area(PH, TOPK, TOPK)
        expert = area(2, 2, PH, TOPK)
        soft = area(2, PH, TOPK)
        soft_s = area(2, PH)
        cursor[0] = common
        cst2 = area(N_CONSTS - N_CONSTS_KEPT)
        w_gate = area(P, rows=16)
        proj2 = area(25, NQ)
        conv_u = area(2, NQ)
        conv_y = area(2, NQ)
        v_moba = area(2, 512)
        z = area(NQ)
        z2 = area(NQ)
        log_a = area(NQ)
        csum = area(NQ)
        e_pos = area(NQ)
        e_neg = area(NQ)
        e_end = area(NQ)
        decay = area(NCH)
        qd = area(NQ)
        kd = area(NQ)
        kend_t = area(NCH, P, rows=CHUNK)
        v_gla = area(NCH, 256, rows=CHUNK)
        a_gla = area(GH, NCH, CHUNK, rows=CHUNK)
        state = area(NCH, 256)
        upd = area(NCH, 256)
        o_gla = area(2, NQ)
        y_gla = area(2, NQ)
        silu_o = area(2, NQ)
        q_x = area(2, NQ)
        kv_x = area(4, NQ)
        conv_a, conv_g, act_a = (proj2[:, 2 * j:2 * j + 2, :] for j in range(3))

        def rows_of(a):
            return a.rearrange("p a b c -> p (a b) c")

        soft_hk, best_hk = rows_of(soft), rows_of(best)
        soft_flat = soft.rearrange("p a b c -> p (a b c)")
        flat_u = flat.rearrange("p a b c -> p (a b c)").bitcast(U32)
        ab_u0, ab_u1 = (ab_u[:, j].rearrange("p a b c -> p (a b c)").bitcast(U32) for j in range(2))
        ab_u_flat = ab_u.rearrange("p a b c d -> p (a b c d)").bitcast(U32)
        ab_f_flat = ab_f.rearrange("p a b c d -> p (a b c d)")
        rb_sub = acc_sb[:, 0:DH * NQ]

        ge = work[:, 0].rearrange("p a b c -> p a (b c)")[:, :, 0:NQ]
        hf = work[:, 1].rearrange("p a b c -> p a (b c)")[:, :, 0:NQ]
        a_in = work[:, :].rearrange("p w a b c -> p (w a) (b c)")[:, :, NQ:2 * NQ]
        one1, one2 = work[:, 0], work[:, 1]
        G = big[:, :].rearrange("p (t e) -> p t e", e=NKEYS)

        def pcol(name, k=0, rows=P):
            return par[0:rows, PARAMS[name][0] + k:PARAMS[name][0] + k + 1]

        def con(name, rows=P, at=None):
            a, n = CONSTS[name]
            if a < N_CONSTS_KEPT:
                return kept[0:rows, a:a + n]
            return at[0:rows, a - N_CONSTS_KEPT:a - N_CONSTS_KEPT + n]

        ident = con("ident")
        E_MODEL, E_QK, E_64, E_SUB, E_ONE = (eps[:, i:i + 1] for i in range(5))

        def x_k(part, k, T):
            return x_op[:, part, k * T:(k + 1) * T]

        def x_all(part, T):
            return x_op[:, part, 0:KT * T]

        def flat2(a):
            return a.rearrange("p a b -> p (a b)")

        def banks(a, n):
            return ps[:, a:a + n, :].rearrange("p a b -> p (a b)")

        scratch = nc.dram_tensor("bias_lines", (DH, P + 1, LINE), F32, kind="Internal").ap()
        mem_store = nc.dram_tensor("mem_store", (P, 4 * NQ), F32, kind="Internal").ap()
        early_store = nc.dram_tensor("early_store", (EARLY, P, NQ), F32, kind="Internal").ap()
        skewed = scratch.rearrange("h p j -> h (p j)")

        M_MEM = 0
        M_IN = M_MEM + 4
        M_OUT = M_IN + 17
        M_QUERY = M_OUT + KT
        M_PEER = M_QUERY + 2 * PH + EARLY
        M_IN2 = M_PEER
        M_OUT2 = M_IN2 + 25
        M_XQ = M_OUT2 + KT
        M_XO = M_XQ + 2
        M_FFN = M_XO + 2

        R_MEM, R_ATTN, R_PEER, R_MIX, R_XATTN, R_FFN, R_FINAL = range(7)

        units = []
        for h in range(HEADS):
            units.append(dict(kind="mla", head=h, keys=NK, out=h))
        for h in range(DH):
            units.append(dict(kind="diff", head=h, map=0, keys=NK, out=None))
            units.append(dict(kind="diff", head=h, map=1, keys=NK, out=HEADS + h))
        for h in range(MH):
            units.append(dict(kind="moba", head=h, keys=NQ, out=HEADS + DH + h))
        for h in range(XH):
            units.append(dict(kind="xattn", head=h, keys=NQ, out=HEADS + DH + MH + h))
        U_MLA, U_DIFF, U_MOBA, U_X = (0, HEADS, HEADS + 2 * DH, HEADS + 2 * DH + MH)
        U_END = U_X + XH

        def walk(a, b):
            for i in range(a, b + 2):
                yield (i if i < b else None, i - 1 if a <= i - 1 < b else None, i - 2 if i - 2 >= a else None)

        def rest_taken(n):
            owner = lo_owner(n.first)
            before = sum(lo_owner(k) == owner for k in range(n.first))
            per = sum(lo_owner(n.first + k) == owner for k in range(n.stride))
            return sem(f"lo_{owner}"), n.value(before + 1, per)

        block = ctx.enter_context(nc.Block())

        @block.sync
        def _(sp):
            sp.dma_start(flat2(mem_t[:, :, :]), dram["mem_t"]).then_inc(sem("mem_loaded"), 16)
            sp.dma_start(par[:, :], dram["params"]).then_inc(sem("par_loaded"), 16)

            def load(n):
                sp.dma_start(raw[:, n.mod(RING), :], dram["blocks"][bass.ds(n.value(), 1)].rearrange("a p c -> p (a c)")
                             ).then_inc(sem(f"raw_loaded{n.mod(RING)}"), 16)

            def next_load(n):
                sp.wait_ge(*rest_taken(n.plus(-RING)))
                load(n)

            def early(w):
                return (w // 2 if w % 2 else None) if w < 4 * PH else w - 2 * PH

            def store(c, m):
                sp.wait_ge(sem("bank_free"), m.value())
                sp.dma_start(early_store[bass.ds(c.value(), 1)].rearrange("a p t -> p (a t)"), a_out[:, c.mod(RING), :]
                             ).then_inc(sem(f"early_stored{c.mod(RING)}"), 16)

            for j in range(RING):
                load(At(j))
            with sp.Fori(0, B_QUERY // RING - 1) as i:
                for j in range(RING):
                    next_load(At(RING + j, i, RING))
            for n in range(B_QUERY // RING * RING, B_EARLY + LOADS_AHEAD):
                next_load(At(n))
                w = n - LOADS_AHEAD - B_QUERY
                if w >= 0 and early(w) is not None:
                    store(At(early(w)), At(M_QUERY + w + 1))
            with sp.Fori(0, (EARLY - 2 * PH) // RING - 1) as i:
                for j in range(RING):
                    next_load(At(B_EARLY + LOADS_AHEAD + j, i, RING))
                    store(At(2 * PH + j, i, RING), At(M_QUERY + 4 * PH + j + 1, i, RING))
            for j in range(RING):
                next_load(At(B_V - RING + LOADS_AHEAD + j))
                store(At(EARLY - RING + j), At(M_PEER - RING + j + 1))

            def early_back(c):
                sp.dma_start(a_in[:, c.mod(RING), :], early_store[bass.ds(c.value(), 1)].rearrange("a p t -> p (a t)")
                             ).then_inc(sem(f"early_loaded{c.mod(RING)}"), 16)

            for j in range(RING):
                sp.wait_ge(sem(f"early_stored{j}"), 16 * (EARLY // RING))
            sp.wait_ge(sem("g_ready"), NQ // 4)
            for j in range(RING):
                early_back(At(j))
            with sp.Fori(0, EARLY // RING - 1) as i:
                for j in range(RING):
                    next_load(At(B_V + LOADS_AHEAD + j, i, RING))
                    sp.wait_ge(sem("act_used"), At(j + 1, i, RING).value())
                    early_back(At(RING + j, i, RING))
            begin = B_PEER + LOADS_AHEAD - RING
            left = N_BLOCKS - begin
            with sp.Fori(0, left // RING) as i:
                for j in range(RING):
                    next_load(At(begin + j, i, RING))
            for n in range(N_BLOCKS - left % RING, N_BLOCKS):
                next_load(At(n))

        @block.gpsimd
        def _(pool):
            def lo(n):
                pool.wait_ge(sem("hi_done"), n.plus(1).value())
                s = n.mod(RING)
                pool.tensor_tensor(w_lo[:, s, :], raw[:, s, :], w_hi[:, s, :].bitcast(F32), ALU.subtract
                                   ).then_inc(sem("lo_pool"), 1)

            def los(a, b):
                for n in range(a, b):
                    if lo_owner(n) == "pool":
                        lo(At(n))

            pool.memset(ones[:, :], 1.0).then_inc(sem("ones_set"), 1)
            for i, v in enumerate((EPS, QK * EPS, 64 * EPS, EPS / (1 - LAMBDA_INIT) ** 2, 1.0)):
                ins = pool.memset(eps[:, i:i + 1], v)
            ins.then_inc(sem("eps_set"), 1)
            los(B_MEM, B_IN)
            pool.wait_ge(sem("bias_loaded"), 16 * 2 * DH)
            pool.wait_ge(sem("cst_loaded"), 16)
            pool.tensor_tensor(
                bias, bias, con("mask", at=cst).rearrange("p (t k) -> p t k", t=2).unsqueeze(1).to_broadcast([P, DH, 2, NK]),
                ALU.add).then_inc(sem("bias_ready"), 1)
            los(B_IN, B_OUT + 2)
            for which, (x, n) in enumerate(((q_mla, NQ), (k_mla, NK))):
                pool.wait_ge(sem("qk_normed"), which + 1)
                pool.tensor_tensor(rope_a[:, :, 0:n], x,
                                   con("cos", QK, cst)[:, NK - n:NK].unsqueeze(1).to_broadcast([QK, HEADS, n]),
                                   ALU.mult).then_inc(sem("rope_cos"), 1)
            los(B_OUT + 2, B_QUERY)
            with pool.Fori(0, (B_V - B_QUERY) // RING) as i:
                for j in range(RING):
                    lo(At(B_QUERY + j, i, RING))
            first = B_V + B_V % 2
            rounds = (N_BLOCKS - first) // RING
            with pool.Fori(0, rounds) as i:
                for j in range(0, RING, 2):
                    lo(At(first + j, i, RING))
            los(first + RING * rounds, N_BLOCKS)

        @block.scalar
        def _(act):
            def hi(n):
                s = n.mod(RING)
                act.wait_ge(sem(f"raw_loaded{s}"), n.div(RING) * 16 + 16)
                if n.first >= RING:
                    act.wait_ge(sem("block_used"), n.plus(1 - RING).value())
                act.activation(w_hi[:, s, :], raw[:, s, :], ACT.Copy).then_inc(sem("hi_done"), 1)

            ahead = [0]

            def his(upto):
                while ahead[0] < min(upto, N_BLOCKS):
                    hi(At(ahead[0]))
                    ahead[0] += 1

            def evacuate(n, m, dst, rows=P, T=NQ, scale=1.0):
                act.wait_ge(sem("block_used"), n + 1)
                act.activation(dst, ps[0:rows, m % 2, 0:T], ACT.Copy, scale=scale).then_inc(sem("bank_free"), 1)

            def norm(r, src, T):
                act.activation(sq[:, 0:KT * T], src, ACT.Square).then_inc(sem("rms_squares"), 1)
                act.wait_ge(sem("rms_sum"), r + 1)
                act.activation(rt[:, 0:T], ps[:, 2, 0:T], ACT.Sqrt, scale=1.0 / D, bias=E_MODEL).then_inc(sem("rms_root"), 1)

            def norm_hi(r, T, n):
                act.wait_ge(sem("rms_xf"), r + 1)
                if n:
                    act.wait_ge(sem("block_used"), n)
                act.activation(x_all(0, T), xf[:, 0:KT * T], ACT.Copy).then_inc(sem("rms_hi"), 1)

            act.dma_start(kept[:, :], dram["consts"][:, 0:N_CONSTS_KEPT]).then_inc(sem("kept_loaded"), 16)
            act.dma_start(cst, dram["consts"][:, N_CONSTS_KEPT:]).then_inc(sem("cst_loaded"), 16)
            act.dma_start(rel_in, dram["rel_bias"]).then_inc(sem("rel_loaded"), 16)
            act.dma_start(flat2(h_t), dram["h_t"]).then_inc(sem("h_loaded"), 16)
            act.dma_start(flat2(w_uq), dram["w_uq"]).then_inc(sem("wu_loaded"), 16)
            act.dma_start(flat2(w_ukv), dram["w_ukv"]).then_inc(sem("wu_loaded"), 16)
            act.wait_ge(sem("eps_set"), 1)
            act.wait_ge(sem("par_loaded"), 16)
            act.wait_ge(sem("mem_loaded"), 16)
            norm(R_MEM, flat2(mem_t[:, :, :]), NQ)
            his(2)
            for h in range(DH):
                act.wait_ge(sem("line_done"), h + 1)
                if h:
                    act.wait_ge(sem("line_stored"), 16 * h)
                act.activation(line[:, 0:LINE // 2], ps[:, 4, 0:LINE // 2], ACT.Copy)
                act.activation(line[:, LINE // 2:LINE], ps[:, 5, 0:LINE - LINE // 2], ACT.Copy).then_inc(sem("line_ready"), 1)
                act.wait_ge(sem("line_ready"), h + 1)
                act.dma_start(scratch[h, 0:P], line).then_inc(sem("line_stored"), 16)
            norm_hi(R_MEM, NQ, 0)
            his(4)
            for j in range(4):
                evacuate(B_MEM + j, M_MEM + j, k_mem[:, j, :] if j < 2 else v_mem_t[:, j - 2, :])
            act.wait_ge(sem("line_stored"), 16 * DH)
            for h in range(DH):
                for t in range(2):
                    start = FAR - N_META - P * t
                    src = skewed[h, start:start + P * (LINE - 1)].rearrange("(p j) -> p j", j=LINE - 1)[:, 0:NK]
                    act.dma_start(bias[:, h, t, :], src).then_inc(sem("bias_loaded"), 16)
            act.wait_ge(sem("h_loaded"), 16)
            norm(R_ATTN, flat2(h_t), NK)
            act.wait_ge(sem("v_mem_turned"), 1)
            act.activation(flat2(v_mem), ps[:, 3, :], ACT.Copy).then_inc(sem("v_mem_ready"), 1)
            act.wait_ge(sem("v_mem_ready"), 1)
            act.wait_ge(sem("bank_free"), M_IN)
            act.dma_start(mem_store, flat2(kv_mem[:, :, :])).then_inc(sem("mem_stored"), 16)
            his(6)
            norm_hi(R_ATTN, NK, B_IN)
            for j in range(17):
                his(B_IN + j + 3)
                evacuate(B_IN + j, M_IN + j, proj[:, j, :], T=NK)
            act.wait_ge(sem("bank_free"), M_OUT)
            lat = ((proj[:, 0:2, N_META:NK], NQ), (proj[:, 2:4, :], NK))
            for w, (src, n) in enumerate(lat):
                act.activation(sq[:, w * 2 * NK:w * 2 * NK + 2 * n].rearrange("p (a b) -> p a b", a=2), src,
                               ACT.Square).then_inc(sem("lat_squares"), 1)
            for w, (src, n) in enumerate(lat):
                act.wait_ge(sem("lat_sum"), w + 1)
                act.activation((rt, rb)[w][:, 0:n], ps[:, 2 + w, 0:n], ACT.Sqrt, scale=1.0 / 256,
                               bias=E_MODEL).then_inc(sem("lat_root"), 1)
            act.wait_ge(sem("q_product"), 1)
            act.activation(flat2(q_mla), banks(4, 4)[0:QK, :], ACT.Copy).then_inc(sem("q_raw"), 1)
            act.wait_ge(sem("q_raw"), 1)
            act.activation(sq[0:QK, 0:HEADS * NQ], flat2(q_mla), ACT.Square).then_inc(sem("qk_squares"), 1)
            for t in range(3):
                rows = min(P, NK - P * t)
                act.wait_ge(sem("v_product"), t + 1)
                act.activation(v_mla[0:rows, t, :], ps[0:rows, 2 + t % 2, :], ACT.Copy).then_inc(sem("v_ready"), 1)
            act.wait_ge(sem("qk_sum"), 1)
            act.activation(xf[0:QK, 0:HEADS * NQ], banks(4, 4)[0:QK, :], ACT.Sqrt, bias=E_QK[0:QK]).then_inc(sem("qk_root"), 1)
            for w in range(2):
                act.wait_ge(sem("k_product"), w + 1)
                act.activation(k_mla[0:NOPE, 4 * w:4 * w + 4, :], ps[0:NOPE, 4:8, 0:NK], ACT.Copy).then_inc(sem("k_raw"), 1)
            act.wait_ge(sem("k_raw"), 3)
            act.wait_ge(sem("qk_sum"), 1)
            act.activation(sq[0:QK, 0:HEADS * NK], flat2(k_mla), ACT.Square).then_inc(sem("qk_squares"), 1)
            act.wait_ge(sem("qk_sum"), 2)
            act.wait_ge(sem("qk_normed"), 1)
            act.activation(xf[0:QK, 0:HEADS * NK], banks(2, 5)[0:QK, 0:HEADS * NK], ACT.Sqrt, scale=1.0 / QK,
                           bias=E_MODEL[0:QK]).then_inc(sem("qk_root"), 1)
            for w, (a, n) in enumerate(((4, NQ), (8, NK))):
                if w:
                    act.wait_ge(sem("d_sum"), w)
                act.activation(sq[:, 0:DH * n].rearrange("p (a b) -> p a b", a=DH), proj[:, a:a + DH, NK - n:NK],
                               ACT.Square).then_inc(sem("d_squares"), 1)
                act.wait_ge(sem("d_sum"), w + 1)
                act.wait_ge(sem("qk_normed"), 2)
                if w:
                    act.wait_ge(sem("d_ready"), w)
                act.activation(xf[:, 0:DH * n], banks(2, 3)[:, 0:DH * n], ACT.Sqrt, scale=1.0 if w == 0 else 1.0 / 64,
                               bias=E_64 if w == 0 else E_MODEL).then_inc(sem("d_root"), 1)
            act.wait_ge(sem("lam_sum"), 1)
            act.activation(lam[:, 4:6], ps[:, 5, 0:2], ACT.Exp).then_inc(sem("lam_exp"), 1)

            def soft(u):
                n = units[u]["keys"]
                act.wait_ge(sem("max_ready"), u + 1)
                for t in range(2):
                    ins = act.activation(scores_sb[:, u % 3, t, 0:n], scores_sb[:, u % 3, t, 0:n], ACT.Exp,
                                         bias=row_max[:, u % 3, t:t + 1], accum_out=row_sum[:, u % 3, t:t + 1])
                ins.then_inc(sem("exp_done"), 1)

            def probs_out(u):
                x, o = units[u], units[u]["out"]
                act.wait_ge(sem("probs_turned"), o + 1)
                if x["keys"] > NQ:
                    act.activation(probs_t[0:N_META, o % 2, 2, :], ps[0:N_META, 1, 0:NQ], ACT.Copy)
                act.activation(flat2(probs_t[:, o % 2, 0:2, :]), ps[:, 6, :], ACT.Copy).then_inc(sem("probs_ready"), 1)

            def head_out(u):
                kind, h, o = units[u]["kind"], units[u]["head"], units[u]["out"]
                act.wait_ge(sem("out_done"), o + 1)
                if kind == "diff":
                    dst, src = o_diff[:, h, :], ps[:, 7, 0:NQ]
                else:
                    rows = slice(64 * (h % 2), 64 * (h % 2) + 64)
                    dst, src = x_k(0, h // 2 + (2 if kind == "moba" else 0), NQ)[rows], ps[rows, 7, 0:NQ]
                act.activation(dst, src, ACT.Copy).then_inc(sem("y_hi"), 1)

            def attention(a, b):
                for s, p, o in walk(a, b):
                    if s is not None:
                        soft(s)
                    if o is not None and units[o]["out"] is not None:
                        head_out(o)
                    if p is not None and units[p]["out"] is not None:
                        probs_out(p)

            attention(U_MLA, U_MOBA)
            act.wait_ge(sem("y_hi"), HEADS + DH)
            act.activation(sq[:, 0:DH * NQ], flat2(o_diff), ACT.Square).then_inc(sem("sub_squares"), 1)
            act.wait_ge(sem("sub_sum"), 1)
            act.activation(rb_sub, banks(2, 2), ACT.Sqrt, scale=1.0 / (P * (1 - LAMBDA_INIT) ** 2),
                           bias=E_SUB).then_inc(sem("sub_root"), 1)
            act.wait_ge(sem("sub_ready"), 1)
            act.activation(x_op[:, 0, 4 * NQ:8 * NQ], xf[:, 0:DH * NQ], ACT.Copy).then_inc(sem("sub_hi"), 1)
            his(B_OUT + 4)
            for j in range(KT):
                act.wait_ge(sem("block_used"), B_OUT + j + 1)
                his(B_OUT + j + 4)
            act.wait_ge(sem("bank_free"), M_QUERY)
            act.dma_start(flat2(sub_keys), dram["sub_keys"]).then_inc(sem("sub_keys_loaded"), 16)
            norm(R_PEER, flat2(res[:, :, :]), NQ)
            norm_hi(R_PEER, NQ, B_QUERY)
            act.wait_ge(sem("mem_stored"), 16)

            def early(c, m):
                act.wait_ge(sem("block_used"), m.plus(B_QUERY - M_QUERY + 1).value())
                if c.first >= RING:
                    act.wait_ge(sem(f"early_stored{c.mod(RING)}"), c.div(RING) * 16)
                act.activation(a_out[:, c.mod(RING), :], ps[:, m.mod(2), 0:NQ], ACT.Gelu).then_inc(sem("bank_free"), 1)

            for w in range(4 * PH):
                his(B_QUERY + w + 3)
                if w % 2 == 0:
                    evacuate(B_QUERY + w, M_QUERY + w, q_peer[:, w // 2, :])
                else:
                    early(At(w // 2), At(M_QUERY + w))
            for w in range(4 * PH, B_BESIDE - B_QUERY):
                his(B_QUERY + w + 3)
                early(At(w - 2 * PH), At(M_QUERY + w))
                if w == 4 * PH + SOFT_AT:
                    act.wait_ge(sem("soft_in"), 1)
                    act.activation(soft_flat, soft_flat, ACT.Exp).then_inc(sem("soft_exp"), 1)
            for w in range(3):
                act.wait_ge(sem("route_turned"), w + 1)
                act.activation(route_t[:, w, :], ps[:, 2 + w, 0:NQ], ACT.Copy).then_inc(sem("route_t_ready"), 1)

            def beside(i):
                for j in range(RING):
                    hi(At(B_BESIDE + 2 + j, i, RING))
                    early(At(EARLY - EARLY_G + j, i, RING), At(M_PEER - EARLY_G + j, i, RING))
                    for g in range(2 * j, 2 * j + 2):
                        act.wait_ge(sem("g_product"), At(g + 1, i, 8).value())
                        act.activation(big[:, bass.ds(At(512 * g, i, 4096).value(), 512)], ps[:, 2 + g % 2, :],
                                       ACT.Copy).then_inc(sem("g_ready"), 1)

            his(B_BESIDE + 2)
            beside(0)
            with act.Fori(1, EARLY_G // RING) as i:
                beside(i)
            with act.Fori(0, EARLY // RING) as i:
                for j in range(RING):
                    hi(At(B_V + 2 + j, i, RING))
            ahead[0] = B_PEER + 2

            def chunk(d):
                act.wait_ge(sem("block_used"), d.value(B_PEER + max(2 * d.first, 1), 2 * d.stride))
                act.wait_ge(sem("act_used"), d.plus(EARLY - 1).value())
                act.activation(ge[:, d.mod(2), :], ps[:, d.mod(2), 0:NQ], ACT.Gelu).then_inc(sem("gelu_done"), 1)

            his(B_PEER + 3)
            for d in range(2):
                chunk(At(d))
                hi(At(B_PEER + 3 + 2 * d))
                hi(At(B_PEER + 4 + 2 * d))
            with act.Fori(0, (NKEYS - EARLY - 4) // 2) as i:
                for d in range(2):
                    chunk(At(2 + d, i, 2))
                    hi(At(B_PEER + 7 + 2 * d, i, 4))
                    hi(At(B_PEER + 8 + 2 * d, i, 4))
            ahead[0] = B_IN2 - 1
            chunk(At(NKEYS - EARLY - 2))
            his(B_IN2)
            chunk(At(NKEYS - EARLY - 1))
            act.wait_ge(sem("acts_ready"), NKEYS)
            act.dma_start(cst2, dram["consts"][:, N_CONSTS_KEPT:]).then_inc(sem("cst2_loaded"), 16)
            act.dma_start(w_gate, dram["w_gate"]).then_inc(sem("cst2_loaded"), 16)
            act.dma_start(flat2(kv_x), mem_store).then_inc(sem("kv_back"), 16)

            def collect(n):
                act.wait_ge(sem("block_used"), n)
                act.activation(acc_sb[:, 0:2048], banks(4, 4), ACT.Copy).then_inc(sem("sum_out"), 1)

            collect(B_IN2)
            his(B_IN2 + 2)
            act.wait_ge(sem("res_ready"), 1)
            norm(R_MIX, flat2(res[:, :, :]), NQ)
            norm_hi(R_MIX, NQ, B_IN2)
            for j in range(25):
                his(B_IN2 + j + 3)
                evacuate(B_IN2 + j, M_IN2 + j, proj2[:, j, :], scale=0.125 if 6 <= j < 10 else 1.0)
            act.wait_ge(sem("bank_free"), M_OUT2)
            act.wait_ge(sem("gate_product"), 1)
            act.activation(z, ps[:, 2, 0:NQ], ACT.Identity, bias=pcol("gate_b")).then_inc(sem("gate_z"), 1)
            act.wait_ge(sem("gate_z"), 1)
            act.activation(z2, z, ACT.Abs).then_inc(sem("gate_step"), 1)
            act.wait_ge(sem("gate_step"), 1)
            act.activation(z2, z2, ACT.Exp, scale=-1.0).then_inc(sem("gate_step"), 1)
            act.wait_ge(sem("gate_step"), 2)
            act.activation(z2, z2, ACT.Ln, bias=E_ONE).then_inc(sem("gate_ln"), 1)
            act.wait_ge(sem("csum_ready"), 1)
            act.activation(e_pos, csum, ACT.Exp).then_inc(sem("gla_exp"), 1)
            act.activation(e_neg, csum, ACT.Exp, scale=-1.0).then_inc(sem("gla_exp"), 1)
            for n in range(NCH):
                last = csum[:, CHUNK * n + CHUNK - 1:CHUNK * n + CHUNK]
                act.activation(e_end[:, CHUNK * n:CHUNK * n + CHUNK], csum[:, CHUNK * n:CHUNK * n + CHUNK], ACT.Exp,
                               scale=-1.0, bias=last)
                ins = act.activation(decay[:, n:n + 1], last, ACT.Exp)
            ins.then_inc(sem("gla_exp"), 1)
            act.activation(flat2(silu_o), flat2(proj2[:, 22:24, :]), ACT.Silu).then_inc(sem("silu_ready"), 1)
            act.wait_ge(sem("gla_turned"), 1)
            act.activation(flat2(v_gla), banks(2, 2)[0:CHUNK, :], ACT.Copy).then_inc(sem("gla_v"), 1)
            act.activation(flat2(kend_t), ps[0:CHUNK, 4, :], ACT.Copy).then_inc(sem("gla_v"), 1)
            act.wait_ge(sem("gla_out"), 1)
            act.activation(o_gla, ps[:, 2:4, 0:NQ], ACT.Copy).then_inc(sem("gla_o"), 1)
            act.wait_ge(sem("gla_o"), 1)
            act.activation(sq[:, 0:2 * NQ], flat2(o_gla), ACT.Square).then_inc(sem("gla_squares"), 1)
            act.wait_ge(sem("gla_sum"), 1)
            act.activation(acc_sb[:, 0:512], ps[:, 4, :], ACT.Sqrt, scale=1.0 / GDV, bias=E_MODEL).then_inc(sem("gla_root"), 1)
            act.wait_ge(sem("mix_ready"), 1)
            act.activation(x_op[:, 0, 0:2 * NQ], flat2(conv_y), ACT.Copy).then_inc(sem("mix_hi"), 1)
            act.wait_ge(sem("mix_ready"), 2)
            act.activation(x_op[:, 0, 6 * NQ:8 * NQ], flat2(y_gla), ACT.Copy).then_inc(sem("mix_hi"), 1)
            attention(U_MOBA, U_X)
            for j in range(KT):
                his(B_OUT2 + j + 3)
                act.wait_ge(sem("block_used"), B_OUT2 + j + 1)
            act.wait_ge(sem("bank_free"), M_XQ)
            norm(R_XATTN, flat2(res[:, :, :]), NQ)
            norm_hi(R_XATTN, NQ, B_XQ)
            for j in range(2):
                his(B_XQ + j + 3)
                evacuate(B_XQ + j, M_XQ + j, q_x[:, j, :], scale=0.125)
            attention(U_X, U_END)
            his(B_FFN + 2)
            act.wait_ge(sem("bank_free"), M_FFN)
            norm(R_FFN, flat2(res[:, :, :]), NQ)
            norm_hi(R_FFN, NQ, B_FFN)

            def pvar(name, per, k, p):
                return par[:, bass.ds(p.value(PARAMS[name][0] + k + per * p.first, per * p.stride), 1)]

            def taps(p):
                for half, buf in enumerate((conv_a, conv_g)):
                    done = B_FFN + 1 + half if p.first == 0 else B_FFN + 3 * p.first + half
                    act.wait_ge(sem("block_used"), p.value(done, 3 * p.stride))
                    if half == 0 and p.first >= 2:
                        act.wait_ge(sem("act_used"), p.value(NKEYS + p.first - 1))
                    act.activation(buf[:, p.mod(2), :], ps[:, half, 0:NQ], ACT.Identity, scale=pvar("cw", 6, 3 * half + 2, p),
                                   bias=pvar("cb", 2, half, p)).then_inc(sem("tap_done"), 1)

            def silu(p):
                act.wait_ge(sem("bank_free"), p.value(M_FFN + 2 * p.first + 1, 2 * p.stride))
                act.activation(act_a[:, p.mod(2), :], conv_a[:, p.mod(2), :], ACT.Silu).then_inc(sem("silu_done"), 1)

            def tile(p):
                n = At(B_FFN + 3 * p.first + 3, p.i, 3 * p.stride)
                hi(n)
                taps(p)
                hi(n.plus(1))
                silu(p)
                hi(n.plus(2))

            his(B_FFN + 3)
            tile(At(0))
            with act.Fori(0, (FT - 2) // 4) as i:
                for j in range(4):
                    tile(At(1 + j, i, 4))
            taps(At(FT - 1))
            silu(At(FT - 1))
            collect(N_BLOCKS)
            act.wait_ge(sem("res_ready"), 2)
            norm(R_FINAL, flat2(res[:, :, :]), NQ)
            act.wait_ge(sem("rms_xf"), R_FINAL + 1)
            act.dma_start(dram["out"], xf[:, 0:KT * NQ]).then_inc(sem("out_stored"), 16)
            act.wait_ge(sem("out_stored"), 16)

        @block.vector
        def _(dve):
            steps = [0]

            def step(ins):
                steps[0] += 1
                ins.then_inc(sem("dve_step"), 1)
                dve.wait_ge(sem("dve_step"), steps[0])

            def lo(n):
                dve.wait_ge(sem("hi_done"), n.plus(1).value())
                s = n.mod(RING)
                dve.tensor_tensor(w_lo[:, s, :], raw[:, s, :], w_hi[:, s, :].bitcast(F32), ALU.subtract
                                  ).then_inc(sem("lo_dve"), 1)

            ahead = [0]

            def los(upto):
                while ahead[0] < min(upto, N_BLOCKS):
                    if lo_owner(ahead[0]) == "dve":
                        lo(At(ahead[0]))
                    ahead[0] += 1

            def norm(r, src, gain, T, operand=True):
                dve.wait_ge(sem("rms_root"), r + 1)
                step(dve.reciprocal(rb[:, 0:T], rt[:, 0:T]))
                for k in range(KT):
                    ins = dve.scalar_tensor_tensor(out=xf[:, k * T:(k + 1) * T], in0=src[:, k, :], scalar=pcol(gain, k),
                                                   in1=rb[:, 0:T], op0=ALU.mult, op1=ALU.mult)
                ins.then_inc(sem("rms_xf"), 1)
                if operand:
                    dve.wait_ge(sem("rms_hi"), r + 1)
                    dve.tensor_tensor(x_all(1, T), xf[:, 0:KT * T], x_all(0, T).bitcast(F32), ALU.subtract
                                      ).then_inc(sem("rms_x"), 1)

            dve.wait_ge(sem("rel_loaded"), 16)
            dve.tensor_copy(rel_rep, rel_in.unsqueeze(2).to_broadcast([BUCKETS, DH, P])).then_inc(sem("rel_ready"), 1)
            dve.wait_ge(sem("par_loaded"), 16)
            norm(R_MEM, mem_t, "mem", NQ)
            los(4)
            dve.wait_ge(sem("h_loaded"), 16)
            norm(R_ATTN, h_t, "attn", NK)
            l0 = PARAMS["lam"][0]
            dve.tensor_tensor(lam[0:64, 0:2], par[0:64, l0:l0 + 4:2], par[0:64, l0 + 1:l0 + 4:2], ALU.mult
                              ).then_inc(sem("lam_ready"), 1)
            los(B_OUT + 2)
            dve.wait_ge(sem("bank_free"), M_OUT)
            for w, (src, dst, n, gain) in enumerate(((proj[:, 0:2, N_META:NK], cqn, NQ, "qn"), (proj[:, 2:4, :], ckvn, NK, "kvn"))):
                r = (rt, rb)[w][:, 0:n]
                dve.wait_ge(sem("lat_root"), w + 1)
                step(dve.reciprocal(r, r))
                for k in range(2):
                    ins = dve.scalar_tensor_tensor(out=dst[:, k, :], in0=src[:, k, :], scalar=pcol(gain, k), in1=r,
                                                   op0=ALU.mult, op1=ALU.mult)
                ins.then_inc(sem("lat_ready"), 1)
            dve.tensor_copy(k_mla[NOPE:QK], proj[NOPE:QK, 16, :].unsqueeze(1).to_broadcast([ROPE, HEADS, NK])
                            ).then_inc(sem("k_raw"), 1)
            for w, (x, n, gain) in enumerate(((q_mla, NQ, "qkq"), (k_mla, NK, "qkk"))):
                dve.wait_ge(sem("qk_root"), w + 1)
                r = xf[0:QK, 0:HEADS * n]
                step(dve.reciprocal(r, r))
                dve.scalar_tensor_tensor(out=flat2(x), in0=flat2(x), scalar=pcol(gain, rows=QK), in1=r,
                                         op0=ALU.mult, op1=ALU.mult).then_inc(sem("qk_normed"), 1)
                sin = con("sin", QK, cst)[:, NK - n:NK].unsqueeze(1).to_broadcast([QK, HEADS, n])
                dve.wait_ge(sem("qk_turned"), w + 1)
                dve.wait_ge(sem("rope_cos"), w + 1)
                turned = banks(4, 4)[0:QK, :] if w == 0 else banks(2, 5)[0:QK, 0:HEADS * NK]
                step(dve.tensor_tensor(x, turned.rearrange("p (h n) -> p h n", h=HEADS), sin, ALU.mult))
                dve.tensor_tensor(x, x, rope_a[:, :, 0:n], ALU.add).then_inc(sem("qk_ready"), 1)
            for w, (a, dst, n, gain) in enumerate(((4, dqn, NQ, "dq"), (8, dkn, NK, "dk"))):
                dve.wait_ge(sem("d_root"), w + 1)
                r = xf[:, 0:DH * n]
                step(dve.reciprocal(r, r))
                dve.scalar_tensor_tensor(out=dst, in0=proj[:, a:a + DH, NK - n:NK], scalar=pcol(gain),
                                         in1=r.rearrange("p (a b) -> p a b", a=DH), op0=ALU.mult, op1=ALU.mult
                                         ).then_inc(sem("d_ready"), 1)
            for t in range(3):
                rows = min(P, NK - P * t)
                dve.wait_ge(sem("dv_turned"), t + 1)
                dve.tensor_copy(v_diff[0:rows, t, :], ps[0:rows, 6 + t % 2, :]).then_inc(sem("dv_ready"), 1)
            dve.wait_ge(sem("lam_exp"), 1)
            step(dve.tensor_tensor(lam[:, 6:7], lam[:, 5:6], lam[:, 4:5], ALU.subtract))
            step(dve.tensor_scalar(lam[:, 7:8], lam[:, 6:7], -LAMBDA_INIT, None, ALU.add))

            def soft_in(u):
                x = units[u]
                n, b = x["keys"], 2 + 2 * (u % 2)
                s = scores_sb[:, u % 3, :, 0:n]
                src = ps[:, b:b + 2, 0:n]
                dve.wait_ge(sem("scores_done"), u + 1)
                if u >= 3:
                    dve.wait_ge(sem("probs_turned"), sum(1 for v in units[:u - 2] if v["out"] is not None))
                if x["kind"] == "mla":
                    ins = dve.tensor_tensor(s, src, con("mask", at=cst).rearrange("p (t k) -> p t k", t=2), ALU.add)
                elif x["kind"] == "diff":
                    if u == U_DIFF:
                        dve.wait_ge(sem("bias_ready"), 1)
                    ins = dve.tensor_tensor(s, src, bias[:, x["head"]], ALU.add)
                elif x["kind"] == "moba":
                    rel = con("rel", at=cst2).rearrange("p (t k) -> p t k", t=2)
                    ins = dve.scalar_tensor_tensor(out=s, in0=rel, scalar=2.0 ** (-8.0 * (x["head"] + 1) / MH), in1=src,
                                                   op0=ALU.mult, op1=ALU.add)
                else:
                    ins = dve.tensor_copy(s, src)
                ins.then_inc(sem("scores_read"), 1)
                dve.wait_ge(sem("scores_read"), u + 1)
                step(dve.tensor_reduce(row_inv[:, u % 3, :], s, AX.X, ALU.max))
                dve.tensor_scalar(row_max[:, u % 3, :], row_inv[:, u % 3, :], -1.0, None, ALU.mult
                                  ).then_inc(sem("max_ready"), 1)

            def normalise(u):
                x = units[u]
                n, b = x["keys"], u % 3
                dve.wait_ge(sem("exp_done"), u + 1)
                step(dve.reciprocal(row_inv[:, b, :], row_sum[:, b, :]))
                if x["kind"] == "diff" and x["map"] == 1:
                    step(dve.tensor_scalar(row_inv[:, b, :], row_inv[:, b, :], lam[:, 7:8], None, ALU.mult))
                    dve.wait_ge(sem("probs_normed"), u)
                    for t in range(2):
                        ins = dve.scalar_tensor_tensor(out=scores_sb[:, b, t, 0:n], in0=scores_sb[:, b, t, 0:n],
                                                       scalar=row_inv[:, b, t:t + 1], in1=scores_sb[:, (u - 1) % 3, t, 0:n],
                                                       op0=ALU.mult, op1=ALU.add)
                else:
                    for t in range(2):
                        ins = dve.tensor_scalar(scores_sb[:, b, t, 0:n], scores_sb[:, b, t, 0:n],
                                                row_inv[:, b, t:t + 1], None, ALU.mult)
                ins.then_inc(sem("probs_normed"), 1)

            def finish(u):
                x, o = units[u], units[u]["out"]
                if o is None or x["kind"] == "diff":
                    return
                rows = slice(64 * (x["head"] % 2), 64 * (x["head"] % 2) + 64)
                k = x["head"] // 2 + (2 if x["kind"] == "moba" else 0)
                dve.wait_ge(sem("y_hi"), o + 1)
                dve.tensor_tensor(x_k(1, k, NQ)[rows], ps[rows, 7, 0:NQ], x_k(0, k, NQ)[rows].bitcast(F32),
                                  ALU.subtract).then_inc(sem("y_ready"), 1)

            def attention(a, b):
                for s, p, o in walk(a, b):
                    if s is not None:
                        soft_in(s)
                    if p is not None:
                        normalise(p)
                    if o is not None:
                        finish(o)

            attention(U_MLA, U_MOBA)
            dve.wait_ge(sem("sub_root"), 1)
            step(dve.reciprocal(rb_sub, rb_sub))
            dve.scalar_tensor_tensor(out=xf[:, 0:DH * NQ], in0=flat2(o_diff), scalar=pcol("subln"), in1=rb_sub,
                                     op0=ALU.mult, op1=ALU.mult).then_inc(sem("sub_ready"), 1)
            dve.wait_ge(sem("sub_hi"), 1)
            dve.tensor_tensor(x_op[:, 1, 4 * NQ:8 * NQ], xf[:, 0:DH * NQ], x_op[:, 0, 4 * NQ:8 * NQ].bitcast(F32),
                              ALU.subtract).then_inc(sem("y_ready"), 1)

            def add_residual(n, m, dst, src):
                dve.wait_ge(sem("block_used"), n + 1)
                dve.tensor_tensor(dst, ps[:, m % 2, 0:NQ], src, ALU.add).then_inc(sem("bank_free"), 1)

            for k in range(KT):
                los(min(B_OUT + k + 3, B_QUERY))
                add_residual(B_OUT + k, M_OUT + k, res[:, k, :], h_t[:, k, N_META:NK])
            dve.wait_ge(sem("bank_free"), M_QUERY)
            norm(R_PEER, res, "ffn", NQ)

            def top16(src, rest_, vals, idx):
                for half in range(2):
                    at = slice(8 * half, 8 * half + 8)
                    for t in range(2):
                        ins = dve.max(vals(t)[:, at], src(t) if half == 0 else rest_(t))
                    step(ins)
                    for t in range(2):
                        ins = dve.max_index(idx(t)[:, at].bitcast(U32), vals(t)[:, at], src(t) if half == 0 else rest_(t))
                    if half == 0:
                        for t in range(2):
                            ins = dve.match_replace(rest_(t), vals(t)[:, at], src(t), -3.0e38)
                        step(ins)
                return ins

            for j in range(2 * PH):
                dve.wait_ge(sem("key_scores"), j + 1)
                top16(lambda t: ps[:, 2 + j % 2, NKEYS * t:NKEYS * (t + 1)], lambda t: rest[:, t, :],
                      lambda t: top_v[:, t, j, :], lambda t: top_i[:, t, j, :]).then_inc(sem("key_scores_read"), 1)
                if j % 2:
                    h = j // 2
                    dve.wait_ge(sem("key_scores_read"), j + 1)
                    for t in range(2):
                        ins = dve.tensor_tensor(cand[:, t, :].rearrange("p (a b) -> p a b", a=TOPK),
                                                top_v[:, t, j - 1, :].unsqueeze(2).to_broadcast([P, TOPK, TOPK]),
                                                top_v[:, t, j, :].unsqueeze(1).to_broadcast([P, TOPK, TOPK]), ALU.add)
                    step(ins)
                    step(top16(lambda t: cand[:, t, :], lambda t: cand_rest[:, t, :],
                               lambda t: best[:, t, h, :], lambda t: flat[:, t, h, :]))
            dve.tensor_tensor(soft_hk, best_hk, best_hk[:, :, 0:1].to_broadcast([P, 2 * PH, TOPK]), ALU.subtract
                              ).then_inc(sem("soft_in"), 1)
            step(dve.tensor_scalar(ab_u0, flat_u, 4, None, ALU.logical_shift_right))
            step(dve.tensor_scalar(ab_u1, flat_u, 15, None, ALU.bitwise_and))
            step(dve.tensor_copy(ab_f_flat, ab_u_flat))
            step(dve.tensor_copy(top_f.rearrange("p a b c -> p (a b c)"), top_i.rearrange("p a b c -> p (a b c)").bitcast(U32)))
            iota16 = con("iota")[:, 0:TOPK].unsqueeze(1).to_broadcast([P, PH * TOPK, TOPK])
            for half in range(2):
                for t in range(2):
                    hits = hit.rearrange("p a b c -> p (a b) c")
                    step(dve.tensor_tensor(hits, ab_f[:, half, t].rearrange("p a b -> p (a b)").unsqueeze(2).to_broadcast(
                        [P, PH * TOPK, TOPK]), iota16, ALU.is_equal))
                    step(dve.tensor_tensor(hit, hit, top_f[:, t, half:2 * PH:2, :].unsqueeze(2).to_broadcast(
                        [P, PH, TOPK, TOPK]), ALU.mult))
                    ins = dve.tensor_reduce(expert[:, half, t].rearrange("p a b -> p (a b)"), hits, AX.X, ALU.add)
                    step(ins)
            dve.wait_ge(sem("soft_exp"), 1)
            step(dve.tensor_reduce(soft_s.rearrange("p a b -> p (a b)"), soft_hk, AX.X, ALU.add))
            step(dve.reciprocal(soft_s.rearrange("p a b -> p (a b)"), soft_s.rearrange("p a b -> p (a b)")))
            dve.tensor_tensor(soft_hk, soft_hk, soft_s.rearrange("p a b -> p (a b)").unsqueeze(2).to_broadcast(
                [P, 2 * PH, TOPK]), ALU.mult).then_inc(sem("route_ready"), 1)
            dve.wait_ge(sem("route_t_ready"), 3)

            def one_hot(g, j, tok):
                dve.tensor_scalar(one1[:, g, j, :], con("iota"), route_t[:, 0, tok], None, ALU.is_equal)
                return dve.tensor_scalar(one2[:, g, j, :], con("iota"), route_t[:, 1, tok], route_t[:, 2, tok],
                                         ALU.is_equal, ALU.mult)

            for g in range(2):
                for j in range(4):
                    ins = one_hot(g, j, slice(4 * g + j, 4 * g + j + 1))
                ins.then_inc(sem("one_hot_ready"), 1)
            with dve.Fori(1, NQ // 8) as i:
                for g in range(2):
                    dve.wait_ge(sem("g_product"), 2 * i + (g - 1))
                    for j in range(4):
                        ins = one_hot(g, j, bass.ds(8 * i + (4 * g + j), 1))
                    ins.then_inc(sem("one_hot_ready"), 1)

            def split(c, a):
                b = c.mod(2)
                dve.tensor_tensor(hf[:, b, :], a, G[:, :, bass.ds(c.value(), 1)].rearrange("p t e -> p (t e)"),
                                  ALU.mult).then_inc(sem("act_used"), 1)
                dve.wait_ge(sem("act_used"), c.plus(1).value())
                if c.first >= 2:
                    n = B_V + c.first - 1 if c.first < EARLY + 2 else B_PEER + 2 * (c.first - EARLY) - 1
                    dve.wait_ge(sem("block_used"), c.value(n, c.stride if c.first < EARLY else 2 * c.stride))
                dve.tensor_copy(h_op[:, b, 0, :], hf[:, b, :]).then_inc(sem("act_hi"), 1)
                dve.wait_ge(sem("act_hi"), c.plus(1).value())
                dve.tensor_tensor(h_op[:, b, 1, :], hf[:, b, :], h_op[:, b, 0, :].bitcast(F32), ALU.subtract
                                  ).then_inc(sem("acts_ready"), 1)

            def early(c):
                dve.wait_ge(sem(f"early_loaded{c.mod(RING)}"), c.div(RING) * 16 + 16)
                split(c, a_in[:, c.mod(RING), :])
                n = At(B_V + 2 + c.first, c.i, c.stride)
                if lo_owner(n.first) == "dve":
                    lo(n)

            def chunk(d):
                dve.wait_ge(sem("gelu_done"), d.plus(1).value())
                split(d.plus(EARLY), ge[:, d.mod(2), :])

            dve.wait_ge(sem("g_ready"), NQ // 4)
            los(B_V + 2)
            for c in range(RING):
                early(At(c))
            with dve.Fori(0, EARLY // RING - 1) as i:
                for j in range(RING):
                    early(At(RING + j, i, RING))
            ahead[0] = B_PEER + 2
            los(B_PEER + 3)
            for d in range(2):
                chunk(At(d))
                lo(At(B_PEER + 4 + 2 * d))
            with dve.Fori(0, (NKEYS - EARLY - 4) // 2) as i:
                for d in range(2):
                    chunk(At(2 + d, i, 2))
                    lo(At(B_PEER + 8 + 2 * d, i, 4))
            ahead[0] = B_IN2 - 1
            chunk(At(NKEYS - EARLY - 2))
            los(B_IN2)
            chunk(At(NKEYS - EARLY - 1))

            def add_turned(r):
                dve.wait_ge(sem("sum_turned"), r + 1)
                dve.tensor_tensor(flat2(res[:, :, :]), banks(0, 4), flat2(res[:, :, :]), ALU.add).then_inc(sem("res_ready"), 1)

            los(B_IN2 + 2)
            add_turned(0)
            norm(R_MIX, res, "mix", NQ)
            los(B_OUT2 + 2)
            dve.wait_ge(sem("bank_free"), M_OUT2)
            step(dve.tensor_tensor(flat2(conv_u), flat2(proj2[:, 2:4, :]), flat2(proj2[:, 4:6, :]), ALU.mult))
            for t in range(2):
                w = [pcol("scw", 3 * t + j) for j in range(3)]
                step(dve.tensor_scalar(conv_y[:, t, :], conv_u[:, t, :], w[2], pcol("scb", t), ALU.mult, ALU.add))
                for back in (1, 2):
                    step(dve.scalar_tensor_tensor(out=conv_y[:, t, back:NQ], in0=conv_u[:, t, 0:NQ - back], scalar=w[2 - back],
                                                  in1=conv_y[:, t, back:NQ], op0=ALU.mult, op1=ALU.add))
            dve.tensor_tensor(flat2(conv_y), flat2(conv_y), flat2(proj2[:, 0:2, :]), ALU.mult).then_inc(sem("mix_ready"), 1)
            dve.wait_ge(sem("gate_ln"), 1)
            step(dve.tensor_scalar(z, z, 0.0, None, ALU.min))
            step(dve.tensor_tensor(log_a, z, z2, ALU.subtract))
            step(dve.tensor_scalar(log_a, log_a, 1.0 / 16, None, ALU.mult))
            for n in range(NCH):
                c = slice(CHUNK * n, CHUNK * n + CHUNK)
                ins = dve.tensor_tensor_scan(csum[:, c], ones[:, 0:CHUNK], log_a[:, c], 0.0, ALU.mult, ALU.add)
            ins.then_inc(sem("csum_ready"), 1)
            dve.wait_ge(sem("gla_exp"), 2)
            dve.scalar_tensor_tensor(out=qd, in0=proj2[:, 18, :], scalar=GDK ** -0.5, in1=e_pos, op0=ALU.mult, op1=ALU.mult)
            dve.tensor_tensor(kd, proj2[:, 19, :], e_neg, ALU.mult).then_inc(sem("gla_qk"), 1)
            dve.wait_ge(sem("gla_exp"), 3)
            dve.tensor_tensor(e_end, e_end, proj2[:, 19, :], ALU.mult).then_inc(sem("gla_end"), 1)
            for t in range(2):
                dve.wait_ge(sem("mv_turned"), t + 1)
                dve.tensor_copy(v_moba[:, t, :], ps[:, 6 + t, :]).then_inc(sem("mv_ready"), 1)
            dve.wait_ge(sem("gla_scores"), 1)
            dve.wait_ge(sem("cst2_loaded"), 32)
            dve.tensor_tensor(a_gla.rearrange("p h n c -> p h (n c)").rearrange("p h (n c) -> p h n c", n=NCH),
                              ps[0:CHUNK, 4:8, 0:NQ].rearrange("p h (n c) -> p h n c", n=NCH),
                              con("gmask", CHUNK, cst2).unsqueeze(1).unsqueeze(1).to_broadcast([CHUNK, GH, NCH, CHUNK]),
                              ALU.mult).then_inc(sem("gla_a"), 1)
            step(dve.memset(state[:, 0, :], 0.0))
            for n in range(NCH - 1):
                dve.wait_ge(sem("gla_update"), n + 1)
                step(dve.tensor_tensor(upd[:, n, :], ps[:, n % 2, 0:256], con("gblk", at=cst2), ALU.mult))
                ins = dve.scalar_tensor_tensor(out=state[:, n + 1, :], in0=state[:, n, :], scalar=decay[:, n:n + 1],
                                               in1=upd[:, n, :], op0=ALU.mult, op1=ALU.add)
                ins.then_inc(sem("gla_state"), 1)
                dve.wait_ge(sem("gla_state"), n + 1)
            dve.wait_ge(sem("gla_root"), 1)
            step(dve.reciprocal(acc_sb[:, 0:512], acc_sb[:, 0:512]))
            step(dve.scalar_tensor_tensor(out=flat2(y_gla), in0=flat2(o_gla), scalar=pcol("gla"), in1=acc_sb[:, 0:512],
                                          op0=ALU.mult, op1=ALU.mult))
            dve.wait_ge(sem("silu_ready"), 1)
            dve.tensor_tensor(flat2(y_gla), flat2(y_gla), flat2(silu_o), ALU.mult).then_inc(sem("mix_ready"), 1)
            for w, (src, a) in enumerate(((conv_y, 0), (y_gla, 6))):
                dve.wait_ge(sem("mix_hi"), w + 1)
                dve.tensor_tensor(x_op[:, 1, a * NQ:(a + 2) * NQ], flat2(src), x_op[:, 0, a * NQ:(a + 2) * NQ].bitcast(F32),
                                  ALU.subtract).then_inc(sem("mix_lo"), 1)
            attention(U_MOBA, U_X)
            for k in range(KT):
                los(B_OUT2 + k + 3)
                add_residual(B_OUT2 + k, M_OUT2 + k, res[:, k, :], res[:, k, :])
            dve.wait_ge(sem("bank_free"), M_XQ)
            norm(R_XATTN, res, "xattn", NQ)
            los(B_XQ + 4)
            attention(U_X, U_END)
            for b in range(2):
                dve.wait_ge(sem("block_used"), B_XO + b + 1)
                four = flat2(res[:, 4 * b:4 * b + 4, :])
                dve.tensor_tensor(four, banks(2 * b, 2), four, ALU.add).then_inc(sem("bank_free"), 1)
            los(B_FFN + 2)
            dve.wait_ge(sem("bank_free"), M_FFN)
            norm(R_FFN, res, "ffn2", NQ)

            def conv(p):
                for half, buf in enumerate((conv_a, conv_g)):
                    dve.wait_ge(sem("tap_done"), p.value(2 * p.first + half + 1, 2 * p.stride))
                    for back, done in ((1, "conv_step"), (2, "bank_free")):
                        a = PARAMS["cw"][0] + 3 * half + 2 - back
                        dve.scalar_tensor_tensor(out=buf[:, p.mod(2), back:NQ], in0=ps[:, half, 0:NQ - back],
                                                 scalar=par[:, bass.ds(p.value(a + 6 * p.first, 6 * p.stride), 1)],
                                                 in1=buf[:, p.mod(2), back:NQ], op0=ALU.mult, op1=ALU.add
                                                 ).then_inc(sem(done), 1)
                        if back == 1:
                            dve.wait_ge(sem("conv_step"), p.value(2 * p.first + half + 1, 2 * p.stride))

            def gate(p):
                b = p.mod(2)
                dve.wait_ge(sem("bank_free"), p.value(M_FFN + 2 * p.first + 2, 2 * p.stride))
                dve.wait_ge(sem("silu_done"), p.plus(1).value())
                dve.tensor_tensor(hf[:, b, :], act_a[:, b, :], conv_g[:, b, :], ALU.mult).then_inc(sem("act_used"), 1)
                dve.wait_ge(sem("act_used"), p.value(NKEYS + p.first + 1))
                if p.first >= 2:
                    dve.wait_ge(sem("block_used"), p.value(B_FFN + 3 * (p.first - 2) + 5, 3 * p.stride))
                dve.tensor_copy(h_op[:, b, 0, :], hf[:, b, :]).then_inc(sem("act_hi"), 1)
                dve.wait_ge(sem("act_hi"), p.value(NKEYS + p.first + 1))
                dve.tensor_tensor(h_op[:, b, 1, :], hf[:, b, :], h_op[:, b, 0, :].bitcast(F32), ALU.subtract
                                  ).then_inc(sem("acts_ready"), 1)

            def tile(p):
                n = At(B_FFN + 3 * p.first + 3, p.i, 3 * p.stride)
                if n.mod(2):
                    lo(n)
                conv(p)
                if n.plus(1).mod(2):
                    lo(n.plus(1))
                gate(p)
                if n.plus(2).mod(2):
                    lo(n.plus(2))

            los(B_FFN + 3)
            tile(At(0))
            with dve.Fori(0, (FT - 2) // 4) as i:
                for j in range(4):
                    tile(At(1 + j, i, 4))
            conv(At(FT - 1))
            gate(At(FT - 1))
            add_turned(1)
            norm(R_FINAL, res, "final", NQ, operand=False)

        @block.tensor
        def _(pe):
            def parts(s, wa, wb, k_hi, k_lo):
                return ((w_hi[:, s, wa:wb], k_hi), (w_hi[:, s, wa:wb], k_lo), (w_lo[:, s, wa:wb], k_hi))

            def arrived(n):
                pe.wait_ge(*rest_taken(n))

            def project(n, m_bank, T=NQ, free=None):
                arrived(n)
                if free is not None:
                    pe.wait_ge(*free)
                for k in range(KT):
                    for j, (w, x) in enumerate(parts(n.mod(RING), k * P, k * P + P, x_k(0, k, T), x_k(1, k, T))):
                        mm = pe.matmul(ps[:, m_bank, 0:T], w, x, start=(k == 0 and j == 0), stop=(k == KT - 1 and j == 2))
                mm.then_inc(sem("block_used"), 1)

            def bank_free(m):
                return (sem("bank_free"), m - 1) if m >= 2 else None

            def projections(n, m, count, T=NQ):
                for j in range(count):
                    project(At(n + j), (m + j) % 2, T, bank_free(m + j))

            def norm(r, T):
                pe.wait_ge(sem("rms_squares"), r + 1)
                for k in range(KT):
                    mm = pe.matmul(ps[:, 2, 0:T], ones[:, :], sq[:, k * T:(k + 1) * T], start=(k == 0), stop=(k == KT - 1))
                mm.then_inc(sem("rms_sum"), 1)

            def operand(r):
                pe.wait_ge(sem("rms_x"), r + 1)

            def spread(b, stationary, src, n, rows=P):
                for a in range(0, n, 512):
                    e = min(n, a + 512)
                    mm = pe.matmul(ps[0:rows, b + a // 512, 0:e - a], stationary, src[:, a:e], start=True, stop=True)
                return mm

            pe.wait_ge(sem("ones_set"), 1)
            norm(R_MEM, NQ)
            pe.wait_ge(sem("rel_ready"), 1)
            pe.wait_ge(sem("cst_loaded"), 16)
            for h in range(DH):
                if h:
                    pe.wait_ge(sem("line_ready"), h)
                for a, e, b in ((0, LINE // 2, 4), (LINE // 2, LINE, 5)):
                    mm = pe.matmul(ps[:, b, 0:e - a], rel_rep[:, h, :], con("bucket", BUCKETS, cst)[:, a:e], start=True, stop=True)
                mm.then_inc(sem("line_done"), 1)
            operand(R_MEM)
            projections(B_MEM, M_MEM, 4)
            norm(R_ATTN, NK)
            pe.wait_ge(sem("bank_free"), M_IN)
            pe.wait_ge(sem("kept_loaded"), 16)
            for t in range(2):
                for f in range(2):
                    mm = pe.transpose(ps[:, 3, (2 * t + f) * P:(2 * t + f + 1) * P], v_mem_t[:, f, t * P:t * P + P], ident)
            mm.then_inc(sem("v_mem_turned"), 1)
            operand(R_ATTN)
            projections(B_IN, M_IN, 17, NK)
            for w, n in enumerate((NQ, NK)):
                pe.wait_ge(sem("lat_squares"), w + 1)
                for k in range(2):
                    a = w * 2 * NK + k * n
                    mm = pe.matmul(ps[:, 2 + w, 0:n], ones[:, :], sq[:, a:a + n], start=(k == 0), stop=(k == 1))
                mm.then_inc(sem("lat_sum"), 1)
            pe.wait_ge(sem("wu_loaded"), 32)
            pe.wait_ge(sem("lat_ready"), 1)
            pe.wait_ge(sem("line_ready"), DH)
            for h in range(HEADS):
                for k in range(2):
                    mm = pe.matmul(ps[0:QK, 4 + h // 2, (h % 2) * NQ:(h % 2 + 1) * NQ], w_uq[:, k, QK * h:QK * h + QK],
                                   cqn[:, k, :], start=(k == 0), stop=(k == 1))
            mm.then_inc(sem("q_product"), 1)
            pe.wait_ge(sem("lat_ready"), 2)
            for t in range(3):
                rows = min(P, NK - P * t)
                if t == 2:
                    pe.wait_ge(sem("v_ready"), 1)
                for k in range(2):
                    mm = pe.matmul(ps[0:rows, 2 + t % 2, :], ckvn[:, k, P * t:P * t + rows], w_ukv[:, k, 512:1024],
                                   start=(k == 0), stop=(k == 1))
                mm.then_inc(sem("v_product"), 1)
            pe.wait_ge(sem("qk_squares"), 1)
            spread(4, ones[0:QK, 0:QK], sq[0:QK, :], HEADS * NQ, QK).then_inc(sem("qk_sum"), 1)
            pe.wait_ge(sem("qk_root"), 1)
            for w in range(2):
                if w:
                    pe.wait_ge(sem("k_raw"), 2)
                for h in range(4):
                    for k in range(2):
                        a = NOPE * (4 * w + h)
                        mm = pe.matmul(ps[0:NOPE, 4 + h, 0:NK], w_ukv[:, k, a:a + NOPE], ckvn[:, k, :], start=(k == 0), stop=(k == 1))
                mm.then_inc(sem("k_product"), 1)
            pe.wait_ge(sem("qk_normed"), 1)
            pe.wait_ge(sem("k_raw"), 3)
            spread(4, con("rot", QK, cst), flat2(q_mla), HEADS * NQ, QK).then_inc(sem("qk_turned"), 1)
            pe.wait_ge(sem("qk_squares"), 2)
            pe.wait_ge(sem("v_ready"), 3)
            pe.wait_ge(sem("qk_ready"), 1)
            spread(2, ones[0:QK, 0:QK], sq[0:QK, :], HEADS * NK, QK).then_inc(sem("qk_sum"), 1)
            pe.wait_ge(sem("qk_normed"), 2)
            spread(2, con("rot", QK, cst), flat2(k_mla), HEADS * NK, QK).then_inc(sem("qk_turned"), 1)
            pe.wait_ge(sem("qk_ready"), 2)
            for w, n in enumerate((NQ, NK)):
                pe.wait_ge(sem("d_squares"), w + 1)
                if w:
                    pe.wait_ge(sem("d_root"), w)
                spread(2, con("blk64", at=cst), sq, DH * n).then_inc(sem("d_sum"), 1)
            for t in range(3):
                rows = min(P, NK - P * t)
                if t == 2:
                    pe.wait_ge(sem("dv_ready"), 1)
                for h in range(DH):
                    mm = pe.transpose(ps[0:rows, 6 + t % 2, h * P:h * P + P], proj[:, 12 + h, P * t:P * t + rows], ident)
                mm.then_inc(sem("dv_turned"), 1)
            pe.wait_ge(sem("lam_ready"), 1)
            pe.matmul(ps[:, 5, 0:2], ones[0:64, :], lam[0:64, 0:2], start=True, stop=True).then_inc(sem("lam_sum"), 1)
            pe.wait_ge(sem("d_root"), 2)
            pe.wait_ge(sem("d_ready"), 2)
            pe.wait_ge(sem("dv_ready"), 3)
            pe.wait_ge(sem("lam_exp"), 1)

            def scores(u):
                x = units[u]
                h, n, b = x["head"], x["keys"], 2 + 2 * (u % 2)
                if u >= 2:
                    pe.wait_ge(sem("scores_read"), u - 1)
                for t in range(2):
                    c = slice(P * t, P * t + P)
                    half = slice(64 * (h % 2), 64 * (h % 2) + 64)
                    if x["kind"] == "mla":
                        q, k = q_mla[:, h, c], k_mla[:, h, :]
                    elif x["kind"] == "diff":
                        half = slice(64 * x["map"], 64 * x["map"] + 64)
                        q, k = dqn[half, h, c], dkn[half, h, :]
                    elif x["kind"] == "moba":
                        q, k = proj2[half, 6 + h // 2, c], proj2[half, 10 + h // 2, :]
                    else:
                        q, k = q_x[half, h // 2, c], kv_x[half, h // 2, :]
                    mm = pe.matmul(ps[:, b + t, 0:n], q, k, start=True, stop=True)
                mm.then_inc(sem("scores_done"), 1)

            def turn(u):
                o, n = units[u]["out"], units[u]["keys"]
                if o is None:
                    return
                pe.wait_ge(sem("probs_normed"), u + 1)
                if o:
                    pe.wait_ge(sem("probs_ready"), o)
                for t in range(2):
                    for j in range(2):
                        mm = pe.transpose(ps[:, 6, j * NQ + t * P:j * NQ + t * P + P], scores_sb[:, u % 3, t, j * P:j * P + P], ident)
                    if n > NQ:
                        mm = pe.transpose(ps[0:N_META, 1, t * P:t * P + P], scores_sb[:, u % 3, t, NQ:n], ident)
                mm.then_inc(sem("probs_turned"), 1)

            def weigh(u):
                x = units[u]
                o, h, n = x["out"], x["head"], x["keys"]
                if o is None:
                    return
                pe.wait_ge(sem("probs_ready"), o + 1)
                if o:
                    pe.wait_ge(sem("y_hi"), o)
                    pe.wait_ge(sem("y_ready"), min(o, HEADS) if o <= HEADS + DH else HEADS + 1 + u - U_MOBA)
                rows = slice(0, P) if x["kind"] == "diff" else slice(64 * (h % 2), 64 * (h % 2) + 64)
                tiles = 3 if n > NQ else 2
                for t in range(tiles):
                    k = min(P, n - P * t)
                    if x["kind"] == "mla":
                        v = v_mla[0:k, t, 64 * h:64 * h + 64]
                    elif x["kind"] == "diff":
                        v = v_diff[0:k, t, P * h:P * h + P]
                    elif x["kind"] == "moba":
                        v = v_moba[0:k, t, 64 * h:64 * h + 64]
                    else:
                        v = kv_x[0:k, 2 + t, 64 * h:64 * h + 64]
                    mm = pe.matmul(ps[rows, 7, 0:NQ], v, probs_t[0:k, o % 2, t, :], start=(t == 0), stop=(t == tiles - 1))
                mm.then_inc(sem("out_done"), 1)

            def attention(a, b):
                for s, p, o in walk(a, b):
                    if s is not None:
                        scores(s)
                    if o is not None:
                        weigh(o)
                    if p is not None:
                        turn(p)

            attention(U_MLA, U_MOBA)
            pe.wait_ge(sem("sub_squares"), 1)
            spread(2, ones[:, :], sq, DH * NQ).then_inc(sem("sub_sum"), 1)
            pe.wait_ge(sem("y_ready"), HEADS + 1)
            projections(B_OUT, M_OUT, KT)
            norm(R_PEER, NQ)
            operand(R_PEER)
            pe.wait_ge(sem("sub_keys_loaded"), 16)

            def key_scores(j):
                pe.wait_ge(sem("bank_free"), M_QUERY + 2 * j + 1)
                if j >= 2:
                    pe.wait_ge(sem("key_scores_read"), j - 1)
                for t in range(2):
                    mm = pe.matmul(ps[:, 2 + j % 2, NKEYS * t:NKEYS * (t + 1)], q_peer[:, j, P * t:P * t + P], sub_keys[:, j, :],
                                   start=True, stop=True)
                mm.then_inc(sem("key_scores"), 1)

            for j in range(2 * PH):
                for w in range(2 * j, 2 * j + 2):
                    projections(B_QUERY + w, M_QUERY + w, 1)
                key_scores(j)
            projections(B_EARLY, M_QUERY + 4 * PH, B_BESIDE - B_EARLY)
            pe.wait_ge(sem("route_ready"), 1)
            for w in range(3):
                for t in range(2):
                    src = (expert[:, w, t] if w < 2 else soft[:, t]).rearrange("p a b -> p (a b)")
                    mm = pe.transpose(ps[:, 2 + w, P * t:P * t + P], src, ident)
                mm.then_inc(sem("route_turned"), 1)
            pe.wait_ge(sem("route_t_ready"), 3)

            def beside(i, first=False):
                for j in range(RING):
                    m = At(M_PEER - EARLY_G + j, i, RING)
                    project(At(B_BESIDE + j, i, RING), m.mod(2), NQ, (sem("bank_free"), m.plus(-1).value()))
                    for g in range(2 * j, 2 * j + 2):
                        pe.wait_ge(sem("one_hot_ready"), At(g + 1, i, 8).value())
                        if not first or g >= 2:
                            pe.wait_ge(sem("g_ready"), At(g - 1, i, 8).value())
                        for k in range(4):
                            mm = pe.matmul(ps[:, 2 + g % 2, P * k:P * k + P], one1[:, g % 2, k, :], one2[:, g % 2, k, :],
                                           start=True, stop=True)
                        mm.then_inc(sem("g_product"), 1)

            beside(0, True)
            with pe.Fori(1, EARLY_G // RING) as i:
                beside(i)

            def expand(n, b, first, last):
                s = n.mod(RING)
                for t in range(2):
                    x_hi, x_lo = (h_op[:, b, j, P * t:P * t + P] for j in range(2))
                    for half in range(2):
                        c = slice(512 * half, 512 * half + 512)
                        for j, (x, w) in enumerate(((x_hi, w_hi), (x_hi, w_lo), (x_lo, w_hi))):
                            mm = pe.matmul(ps[:, 4 + 2 * t + half, :], x, w[:, s, c], start=(first and j == 0),
                                           stop=(last and j == 2), skip_group_check=True)
                return mm

            def early(c):
                n = At(B_V + c.first, c.i, c.stride)
                arrived(n)
                pe.wait_ge(sem("acts_ready"), c.plus(1).value())
                expand(n, c.mod(2), c.first == 0, False).then_inc(sem("block_used"), 1)

            def chunk(d):
                n = At(B_PEER + 1 + 2 * d.first, d.i, 2 * d.stride)
                project(n, (d.first + 1) % 2, NQ, (sem("gelu_done"), d.value()) if d.first else None)
                arrived(n.plus(1))
                pe.wait_ge(sem("acts_ready"), d.plus(EARLY + 1).value())
                expand(n.plus(1), d.mod(2), False, False).then_inc(sem("block_used"), 1)

            for c in range(RING):
                early(At(c))
            with pe.Fori(0, EARLY // RING - 1) as i:
                for j in range(RING):
                    early(At(RING + j, i, RING))
            pe.wait_ge(sem("bank_free"), M_PEER)
            project(At(B_PEER), 0, NQ)
            for d in range(2):
                chunk(At(d))
            with pe.Fori(0, (NKEYS - EARLY - 4) // 2) as i:
                for d in range(2):
                    chunk(At(2 + d, i, 2))
            chunk(At(NKEYS - EARLY - 2))
            arrived(At(B_IN2 - 1))
            pe.wait_ge(sem("acts_ready"), NKEYS)
            expand(At(B_IN2 - 1), (NKEYS - 1) % 2, False, True).then_inc(sem("block_used"), 1)

            def turn_sum(r):
                pe.wait_ge(sem("sum_out"), r + 1)
                for k in range(KT):
                    for t in range(2):
                        a = (k % 2) * NQ + P * t
                        mm = pe.transpose(ps[:, k // 2, a:a + P], acc_sb[:, 1024 * t + P * k:1024 * t + P * k + P], ident)
                mm.then_inc(sem("sum_turned"), 1)

            turn_sum(0)
            norm(R_MIX, NQ)
            operand(R_MIX)
            projections(B_IN2, M_IN2, 25)
            pe.wait_ge(sem("bank_free"), M_OUT2)
            pe.wait_ge(sem("cst2_loaded"), 32)
            pe.matmul(ps[:, 2, 0:NQ], w_gate, proj2[0:16, 24, :], start=True, stop=True).then_inc(sem("gate_product"), 1)
            for t in range(2):
                for f in range(4):
                    mm = pe.transpose(ps[:, 6 + t, f * P:f * P + P], proj2[:, 14 + f, P * t:P * t + P], ident)
                mm.then_inc(sem("mv_turned"), 1)
            pe.wait_ge(sem("gate_z"), 1)
            pe.wait_ge(sem("gla_end"), 1)
            for n in range(NCH):
                c = slice(CHUNK * n, CHUNK * n + CHUNK)
                for f in range(2):
                    pe.transpose(banks(2, 2)[0:CHUNK, n * 256 + f * P:n * 256 + f * P + P], proj2[:, 20 + f, c], ident)
                mm = pe.transpose(ps[0:CHUNK, 4, n * P:n * P + P], e_end[:, c], ident)
            mm.then_inc(sem("gla_turned"), 1)
            pe.wait_ge(sem("gla_v"), 2)
            pe.wait_ge(sem("gla_qk"), 1)
            pe.wait_ge(sem("mv_ready"), 2)
            for h in range(GH):
                r = slice(GDK * h, GDK * h + GDK)
                for n in range(NCH):
                    c = slice(CHUNK * n, CHUNK * n + CHUNK)
                    mm = pe.matmul(ps[0:CHUNK, 4 + h, c], kd[r, c], qd[r, c], start=True, stop=True)
            mm.then_inc(sem("gla_scores"), 1)
            for n in range(NCH - 1):
                if n >= 2:
                    pe.wait_ge(sem("gla_state"), n - 1)
                pe.matmul(ps[:, n % 2, 0:256], kend_t[:, n, :], v_gla[:, n, :], start=True, stop=True
                          ).then_inc(sem("gla_update"), 1)
            pe.wait_ge(sem("gla_a"), 1)
            pe.wait_ge(sem("gla_state"), NCH - 1)
            for f in range(2):
                for n in range(NCH):
                    c = slice(CHUNK * n, CHUNK * n + CHUNK)
                    pe.matmul(ps[:, 2 + f, c], state[:, n, P * f:P * f + P], qd[:, c], start=True, stop=False,
                              skip_group_check=True)
                    for e in range(2):
                        h = 2 * f + e
                        mm = pe.matmul(ps[GDV * e:GDV * e + GDV, 2 + f, c], v_gla[:, n, GDV * h:GDV * h + GDV],
                                       a_gla[:, h, n, :], start=False, stop=True, skip_group_check=True)
            mm.then_inc(sem("gla_out"), 1)
            pe.wait_ge(sem("gla_squares"), 1)
            spread(4, con("blk64", at=cst2), sq, 2 * NQ).then_inc(sem("gla_sum"), 1)
            pe.wait_ge(sem("gla_root"), 1)
            attention(U_MOBA, U_X)
            pe.wait_ge(sem("mix_lo"), 2)
            pe.wait_ge(sem("y_ready"), HEADS + 1 + MH)
            projections(B_OUT2, M_OUT2, KT)
            norm(R_XATTN, NQ)
            operand(R_XATTN)
            projections(B_XQ, M_XQ, 2)
            pe.wait_ge(sem("bank_free"), M_XO)
            pe.wait_ge(sem("kv_back"), 16)
            attention(U_X, U_END)
            pe.wait_ge(sem("y_ready"), HEADS + 1 + MH + XH)
            for b in range(2):
                n = At(B_XO + b)
                arrived(n)
                for f in range(4):
                    for k in range(2):
                        a = (2 * f + k) * P
                        for j, (w, x) in enumerate(parts(n.mod(RING), a, a + P, x_k(0, k, NQ), x_k(1, k, NQ))):
                            mm = pe.matmul(ps[:, 2 * b + f // 2, (f % 2) * NQ:(f % 2 + 1) * NQ], w, x,
                                           start=(k == 0 and j == 0), stop=(k == 1 and j == 2))
                mm.then_inc(sem("block_used"), 1)
            norm(R_FFN, NQ)
            operand(R_FFN)

            def up(p, n):
                for half in range(2):
                    free = (sem("bank_free"), p.value(M_FFN + 2 * p.first - 1 + half, 2 * p.stride)) if p.first else None
                    project(n.plus(half), half, NQ, free)

            def down(p, n, last=False):
                arrived(n)
                pe.wait_ge(sem("acts_ready"), p.value(NKEYS + p.first + 1))
                expand(n, p.mod(2), p.first == 0, last).then_inc(sem("block_used"), 1)

            def tile(p):
                n = At(B_FFN + 2 + 3 * p.first, p.i, 3 * p.stride)
                up(p.plus(1), n)
                down(p, n.plus(2))

            up(At(0), At(B_FFN))
            tile(At(0))
            with pe.Fori(0, (FT - 2) // 4) as i:
                for j in range(4):
                    tile(At(1 + j, i, 4))
            down(At(FT - 1), At(N_BLOCKS - 1), last=True)
            turn_sum(1)
            norm(R_FINAL, NQ)


def constants():
    c = np.zeros((P, N_CONSTS), np.float32)

    def put(name, a):
        c[:a.shape[0], CONSTS[name][0]:CONSTS[name][0] + a.shape[1]] = a

    put("ident", np.eye(P, dtype=np.float32))
    put("blk64", np.kron(np.eye(2), np.ones((64, 64))))
    put("iota", np.tile(np.arange(P), (P, 1)))
    half = ROPE // 2
    rot = np.zeros((QK, QK))
    for j in range(half):
        rot[NOPE + half + j, NOPE + j] = -1.0
        rot[NOPE + j, NOPE + half + j] = 1.0
    put("rot", rot)
    freq = np.float32(10000.0) ** (-np.arange(half, dtype=np.float32) / np.float32(half))
    angle = np.arange(NK, dtype=np.float32)[:, None] * freq[None, :]
    cos, sin = np.ones((QK, NK)), np.zeros((QK, NK))
    for j in range(2):
        cos[NOPE + half * j:NOPE + half * (j + 1)] = np.cos(angle).T
        sin[NOPE + half * j:NOPE + half * (j + 1)] = np.sin(angle).T
    put("cos", cos)
    put("sin", sin)
    p = np.arange(P)[:, None, None]
    t = np.arange(2)[None, :, None]
    d = N_META + P * t + p - np.arange(NK)[None, None, :]
    put("mask", np.where(d >= 0, 0.0, NEG).reshape(P, -1))
    n = np.maximum(FAR - np.arange(LINE), 0)
    exact = BUCKETS // 2
    large = exact + (np.log(np.maximum(n, 1).astype(np.float32) / np.float32(exact))
                     / np.float32(math.log(MAX_DIST / exact)) * np.float32(BUCKETS - exact)).astype(np.int32)
    bucket = np.where(n < exact, n, np.minimum(large, BUCKETS - 1))
    put("bucket", (bucket[None, :] == np.arange(BUCKETS)[:, None]).astype(np.float32))
    d = P * t + p - np.arange(NQ)[None, None, :]
    put("rel", np.where(d >= 0, -d, -1e32).reshape(P, -1))
    put("gmask", (np.arange(CHUNK)[:, None] <= np.arange(CHUNK)[None, :]).astype(np.float32))
    put("gblk", (np.arange(P)[:, None] // GDK == np.arange(256)[None, :] // GDV).astype(np.float32))
    return c


def layout(a):
    def lay(name):
        return np.asarray(a[name], np.float32)

    def tiles(w):
        return w.reshape(KT, P, -1, P).transpose(2, 1, 0, 3).reshape(-1, P, D)

    def pad(w, rows, cols):
        out = np.zeros((rows, cols), np.float32)
        out[:w.shape[0], :w.shape[1]] = w
        return out

    def feature_major(x):
        return np.ascontiguousarray(x.T.reshape(KT, P, -1).transpose(1, 0, 2).reshape(P, -1))

    w_in = lay("w_in")[0]
    rope = np.zeros((D, P), np.float32)
    rope[:, NOPE:QK] = w_in[:, 512:544]
    u = lay("peer_u")[0].reshape(NKEYS, NKEYS, KT, P).transpose(1, 3, 2, 0).reshape(NKEYS, P, D)
    v = lay("peer_v")[0].reshape(NKEYS, NKEYS, D).transpose(1, 0, 2)
    up = lay("ffn_w_up_2")[0]
    up_a, up_g = (tiles(pad(up[:, FF * j:FF * (j + 1)], D, FT * P)) for j in range(2))
    down = pad(lay("ffn_w_down_2")[0], FT * P, D).reshape(FT, P, D)
    wo = lay("xattn_wo_2")[0].reshape(2, P, 2, 4, P).transpose(2, 1, 3, 0, 4).reshape(2, P, D)
    query = tiles(lay("peer_w_query")[0])
    early = [w for j in range(2 * PH) for w in (query[j], u[j])] + list(u[2 * PH:EARLY]) + list(v[:EARLY])
    peer = [u[EARLY]] + [w for c in range(EARLY, NKEYS - 1) for w in (u[c + 1], v[c])] + [v[-1]]
    ffn = [up_a[0], up_g[0]] + [w for t in range(FT - 1) for w in (up_a[t + 1], up_g[t + 1], down[t])] + [down[-1]]
    blocks = np.empty((N_BLOCKS, P, D), np.float32)
    at = 0
    for group in (tiles(lay("xattn_wkv_2")[0]), tiles(np.concatenate([w_in[:, :512], w_in[:, 544:], rope], axis=1)),
                  tiles(lay("w_out")[0]), early, peer, tiles(pad(lay("w_in_2")[0], D, 25 * P)),
                  tiles(lay("w_out_2")[0]), tiles(lay("xattn_wq_2")[0]), wo, ffn):
        for w in group:
            blocks[at] = w
            at += 1
    assert at == N_BLOCKS

    params = np.zeros((P, N_PARAMS), np.float32)

    def put(name, v, k=0, twice=False):
        v = np.concatenate([v, v]) if twice else v
        n = -(-v.size // P)
        cols = np.zeros(n * P, np.float32)
        cols[:v.size] = v
        params[:, PARAMS[name][0] + k:PARAMS[name][0] + k + n] = cols.reshape(n, P).T

    for name, source in (("attn", "attn_norm"), ("qn", "mla_q_norm"), ("kvn", "mla_kv_norm"), ("qkq", "mla_qk_norm_q"),
                         ("qkk", "mla_qk_norm_k"), ("subln", "diff_subln"), ("ffn", "ffn_norm"), ("mix", "norm_mix_g_2"),
                         ("scb", "sc_conv_b_2"), ("gate_b", "gla_b_gate_2"), ("xattn", "norm_xattn_g_2"),
                         ("mem", "norm_mem_g_2"), ("ffn2", "norm_ffn_g_2")):
        put(name, lay(source)[0])
    put("final", lay("final_norm_g_2"))
    for name, source in (("dq", "diff_q_norm"), ("dk", "diff_k_norm"), ("gla", "gla_norm_g_2")):
        put(name, lay(source)[0], twice=True)
    for k, source in enumerate(("diff_lambda_q1", "diff_lambda_k1", "diff_lambda_q2", "diff_lambda_k2")):
        put("lam", lay(source)[0], k)
    for t in range(2):
        for j in range(3):
            put("scw", lay("sc_conv_w_2")[0, j, P * t:P * t + P], 3 * t + j)
    cw, cb = lay("ffn_conv_w_2")[0], lay("ffn_conv_b_2")[0]
    for half in range(2):
        for t in range(FT):
            f = slice(FF * half + P * t, FF * half + min(P * t + P, FF))
            put("cb", cb[f], 2 * t + half)
            for j in range(3):
                put("cw", cw[j, f], 6 * t + 3 * half + j)

    ukv = lay("mla_w_ukv")[0].reshape(2, P, HEADS, 2, 64).transpose(1, 0, 3, 2, 4).reshape(P, -1)
    return {
        "blocks": blocks,
        "params": params,
        "consts": constants(),
        "h_t": feature_major(np.concatenate([lay("meta_tokens"), lay("x")[0]], axis=0)),
        "mem_t": feature_major(lay("mem_2")[0]),
        "rel_bias": lay("rel_bias"),
        "w_uq": np.ascontiguousarray(lay("mla_w_uq")[0].reshape(2, P, -1).transpose(1, 0, 2).reshape(P, -1)),
        "w_ukv": np.ascontiguousarray(ukv),
        "sub_keys": np.ascontiguousarray(lay("peer_sub_keys")[0].transpose(3, 0, 1, 2).reshape(P, -1)),
        "w_gate": lay("gla_w_gate_2")[0],
    }


def kernel(**inputs):
    import concourse.bacc as bacc
    from concourse.bass_utils import run_bass_kernel_spmd

    nc = bacc.Bacc("TRN2", target_bir_lowering=False, num_devices=1, dynamic_dma_scratch_size=1024)
    arrays = layout(inputs)
    dram = {name: nc.dram_tensor(name, a.shape, F32, kind="ExternalInput").ap() for name, a in arrays.items()}
    dram["out"] = nc.dram_tensor("out", (P, KT * NQ), F32, kind="ExternalOutput").ap()
    build(nc, dram)
    out = run_bass_kernel_spmd(nc, [arrays], core_ids=[0]).results[0]["out"]
    return np.ascontiguousarray(out.reshape(P, KT, NQ).transpose(2, 1, 0).reshape(1, NQ, D))
```

```python
from contextlib import ExitStack
import math

import numpy as np
import concourse.bass as bass
from concourse import mybir

F32 = mybir.dt.float32
F32R = mybir.dt.float32r
U32 = mybir.dt.uint32
ALU = mybir.AluOpType
ACT = mybir.ActivationFunctionType
AX = mybir.AxisListType

P = 128
D = 1024
KT = D // P
NQ = 256
N_META = 16
NK = NQ + N_META
EPS = 1e-6
NEG = -1e30
RING = 4
LOADS_AHEAD = RING + 2
QK, NOPE, ROPE, HEADS = 96, 64, 32, 8
DH = 4
LAMBDA_INIT = 0.8 - 0.6 * math.exp(0.0)
BUCKETS, MAX_DIST = 32, 128
FAR = NK - 1
LINE = FAR + NQ + 1
PH, NKEYS, TOPK = 8, 128, 16
EARLY = 64
SOFT_AT = 5
EARLY_G = 32
MH, GH, GDK, GDV, CHUNK = 8, 4, 32, 64, 64
NCH = NQ // CHUNK
XH = 4
FF = 2752
FT = -(-FF // P)

B_IN = 0
B_MEM = B_IN + 17
B_OUT = B_MEM + 4
B_QUERY = B_OUT + KT
B_EARLY = B_QUERY + 4 * PH
B_BESIDE = B_QUERY + 2 * PH + EARLY - EARLY_G
B_V = B_QUERY + 2 * PH + EARLY
B_PEER = B_V + EARLY
B_IN2 = B_PEER + 2 * (NKEYS - EARLY)
B_OUT2 = B_IN2 + 25
B_XQ = B_OUT2 + KT
B_XO = B_XQ + 2
B_FFN = B_XO + 2
N_BLOCKS = B_FFN + 3 * FT
assert N_BLOCKS % RING == 0

IN2_ORDER = [24, 18, 19, 20, 21, 22, 23, 14, 15, 16, 17, 0, 1, 2, 3, 4, 5, 6, 10, 7, 11, 8, 12, 9, 13]

PARAMS = {}
for _name, _n in (("attn", 8), ("qn", 2), ("kvn", 2), ("qkq", 1), ("qkk", 1), ("dq", 1), ("dk", 1), ("lam", 4),
                  ("subln", 1), ("ffn", 8), ("mix", 8), ("scw", 6), ("scb", 2), ("gate_b", 1), ("gla", 1),
                  ("xattn", 8), ("mem", 8), ("ffn2", 8), ("cw", 6 * FT), ("cb", 2 * FT), ("final", 8)):
    PARAMS[_name] = (sum(n for _, n in PARAMS.values()), _n)
N_PARAMS = sum(n for _, n in PARAMS.values())

CONSTS = {}
for _name, _n in (("ident", 128), ("iota", 128), ("blk64", 128), ("rot", QK), ("cos", NK), ("sin", NK),
                  ("mask", 2 * NK), ("bucket", LINE), ("rel", 2 * NQ), ("gmask", CHUNK), ("gblk", 256)):
    CONSTS[_name] = (sum(n for _, n in CONSTS.values()), _n)
N_CONSTS = sum(n for _, n in CONSTS.values())
N_CONSTS_KEPT = 2 * 128


def taken(n):
    return n + 1 if n < B_MEM else n + 1 - (B_OUT - B_MEM)


def lo_owner(n):
    if B_MEM <= n < B_OUT:
        return None
    return "pool" if B_QUERY <= n <= B_V or n % 2 == 0 else "dve"


class At:

    def __init__(self, first, i=0, stride=0):
        self.first, self.i, self.stride = first, i, stride

    def plus(self, k):
        return At(self.first + k, self.i, self.stride)

    def mod(self, m):
        assert self.stride % m == 0
        return self.first % m

    def div(self, m):
        assert self.stride % m == 0
        return self.value(self.first // m, self.stride // m)

    def value(self, first=None, stride=None):
        first = self.first if first is None else first
        stride = self.stride if stride is None else stride
        return first + self.i * stride if stride else first


def build(nc, dram):
    ctx = ExitStack()
    with ctx:
        def sb(name, shape, dt=F32):
            return ctx.enter_context(nc.sbuf_tensor(name, shape, dt))

        sems = {}

        def sem(name):
            if name not in sems:
                sems[name] = ctx.enter_context(nc.semaphore(name))
            return sems[name]

        raw = sb("raw", [P, RING, D])
        w_hi = sb("w_hi", [P, RING, D], F32R)
        w_lo = sb("w_lo", [P, RING, D], F32R)
        x_op = sb("x_op", [P, 2, KT * NK], F32R)
        res = sb("res", [P, KT, NQ])
        par = sb("par", [P, N_PARAMS])
        kept = sb("kept", [P, N_CONSTS_KEPT])
        ones = sb("ones", [P, P])
        eps = sb("eps", [P, 8])
        kv_mem = sb("kv_mem", [P, RING, NQ])
        a_out = kv_mem
        route_t = sb("route_t", [P, 3, NQ])
        work = sb("work", [P, 2, 2, 4, P])
        h_op = sb("h_op", [P, 2, 2, NQ], F32R)
        big = sb("big", [P, NKEYS * NQ])

        ps = ctx.enter_context(nc.psum_tensor("ps", [P, 8, 512], F32))

        cursor = [0]

        def area(*shape, rows=P):
            size = int(np.prod(shape))
            a = big[0:rows, cursor[0]:cursor[0] + size]
            cursor[0] += size
            assert cursor[0] <= NKEYS * NQ, cursor[0]
            names = "abcd"[:len(shape)]
            if len(shape) > 1:
                a = a.rearrange(f"p ({' '.join(names)}) -> p {' '.join(names)}", **dict(zip(names, shape)))
            return a

        sq = area(KT * NK)
        xf = area(KT * NK)
        rt = area(NK)
        rb = area(NK)
        acc_sb = area(HEADS * NK)
        sq_begin = cursor[0]
        scores_sb = area(3, 2, NK)
        probs_t = area(2, 3, NQ)
        row_max = area(3, 2)
        row_sum = area(3, 2)
        row_inv = area(3, 2)
        common = cursor[0]
        cst = area(N_CONSTS - N_CONSTS_KEPT)
        mem_t = res
        h_t = area(KT, NK)
        k_mem = kv_mem[:, 0:2, :]
        v_mem = kv_mem[:, 2:4, :]
        proj = area(9, NK)
        w_uq = area(2, HEADS * QK)
        w_ukv = area(2, HEADS * 128)
        latent = area(2 * NQ + 2 * NK)
        cqn = latent[:, 0:2 * NQ].rearrange("p (a b) -> p a b", a=2)
        ckvn = latent[:, 2 * NQ:].rearrange("p (a b) -> p a b", a=2)
        q_mla = area(HEADS, NQ, rows=QK)
        k_mla = area(HEADS, NK, rows=QK)
        rope_a = acc_sb[0:QK, :].rearrange("p (h n) -> p h n", h=HEADS)
        spare = work[:, :, :, :, :].rearrange("p a b c d -> p (a b c d)")
        v_mla = spare[:, 0:3 * 512].rearrange("p (t n) -> p t n", t=3)
        rel_rep = spare[0:BUCKETS, 3 * 512:4 * 512].rearrange("p (h n) -> p h n", h=DH)
        v_diff = w_uq.rearrange("p a b -> p (a b)").rearrange("p (t n) -> p t n", t=3)
        v_mem_t = w_ukv[:, 0, 0:2 * NQ].rearrange("p (a b) -> p a b", a=2)
        dqn = area(DH, NQ)
        dkn = area(DH, NK)
        rope_k = proj[NOPE:QK, 4, :]
        rope_kc = latent[NOPE:QK, 2 * NQ - NK:2 * NQ]
        head_of = area(HEADS * QK, rows=HEADS)
        map_of = area(2 * DH * 64, rows=2 * DH)
        one_in = area(15)
        two_in = area(14)
        pair_in = area(14)
        rq = area(2, 2, 8)
        rk = area(2, NK, rows=8)
        mem_rt, mem_rb = acc_sb[:, 0:NQ], acc_sb[:, NQ:2 * NQ]
        lat_sq = xf[:, 0:2 * NQ + 2 * NK]
        d_sq = big[:, sq_begin:sq_begin + DH * (NQ + NK) + NK]
        dq_sq = d_sq[:, 0:DH * NQ].rearrange("p (a b) -> p a b", a=DH)
        dk_sq = d_sq[:, DH * NQ:DH * (NQ + NK)].rearrange("p (a b) -> p a b", a=DH)
        rope_sq = d_sq[NOPE:QK, DH * (NQ + NK):]
        bias = area(DH, 2, NK)
        rel_in = area(DH, rows=BUCKETS)
        line = route_t[:, :, :].rearrange("p a b -> p (a b)")[:, 0:LINE]
        lam = area(16)
        o_diff = proj.rearrange("p a b -> p (a b)")[:, 0:DH * NQ].rearrange("p (a b) -> p a b", a=DH)
        cursor[0] = common
        sub_keys = area(2 * PH, NKEYS)
        q_peer = area(2 * PH, NQ)
        top_v = area(2, 2 * PH, TOPK)
        top_i = area(2, 2 * PH, TOPK)
        top_f = area(2, 2 * PH, TOPK)
        rest = area(2, NKEYS)
        cand = area(2, TOPK * TOPK)
        cand_rest = area(2, TOPK * TOPK)
        best = area(2, PH, TOPK)
        flat = area(2, PH, TOPK)
        ab_u = area(2, 2, PH, TOPK)
        ab_f = area(2, 2, PH, TOPK)
        hit = area(PH, TOPK, TOPK)
        expert = area(2, 2, PH, TOPK)
        soft = area(2, PH, TOPK)
        soft_s = area(2, PH)
        cursor[0] = common
        cst2 = area(N_CONSTS - N_CONSTS_KEPT)
        w_gate = area(P, rows=16)
        proj2 = area(25, NQ)
        conv_u = area(2, NQ)
        conv_y = area(2, NQ)
        v_moba = area(2, 512)
        z = area(NQ)
        z2 = area(NQ)
        log_a = area(NQ)
        csum = area(NQ)
        e_pos = area(NQ)
        e_neg = area(NQ)
        e_end = area(NQ)
        decay = area(NCH)
        qd = area(NQ)
        kd = area(NQ)
        kend_t = area(NCH, P, rows=CHUNK)
        v_gla = area(NCH, 256, rows=CHUNK)
        a_gla = area(GH, NCH, CHUNK, rows=CHUNK)
        state = area(NCH, 256)
        upd = area(NCH, 256)
        o_gla = area(2, NQ)
        y_gla = area(2, NQ)
        silu_o = area(2, NQ)
        q_x = area(2, NQ)
        kv_x = area(4, NQ)
        up_out = proj2[:, 6:10, :].rearrange("p (h b) n -> p h b n", h=2)
        conv_a, conv_g, act_a = (proj2[:, 2 * j:2 * j + 2, :] for j in range(3))

        def rows_of(a):
            return a.rearrange("p a b c -> p (a b) c")

        soft_hk, best_hk = rows_of(soft), rows_of(best)
        soft_flat = soft.rearrange("p a b c -> p (a b c)")
        flat_u = flat.rearrange("p a b c -> p (a b c)").bitcast(U32)
        ab_u0, ab_u1 = (ab_u[:, j].rearrange("p a b c -> p (a b c)").bitcast(U32) for j in range(2))
        ab_u_flat = ab_u.rearrange("p a b c d -> p (a b c d)").bitcast(U32)
        ab_f_flat = ab_f.rearrange("p a b c d -> p (a b c d)")
        sub_r = rk[:, 0, 0:NQ]

        ge = work[:, 0].rearrange("p a b c -> p a (b c)")[:, :, 0:NQ]
        hf = work[:, 1].rearrange("p a b c -> p a (b c)")[:, :, 0:NQ]
        a_in = work[:, :].rearrange("p w a b c -> p (w a) (b c)")[:, :, NQ:2 * NQ]
        one1, one2 = work[:, 0], work[:, 1]
        G = big[:, :].rearrange("p (t e) -> p t e", e=NKEYS)

        def pcol(name, k=0, rows=P):
            return par[0:rows, PARAMS[name][0] + k:PARAMS[name][0] + k + 1]

        def con(name, rows=P, at=None):
            a, n = CONSTS[name]
            if a < N_CONSTS_KEPT:
                return kept[0:rows, a:a + n]
            return at[0:rows, a - N_CONSTS_KEPT:a - N_CONSTS_KEPT + n]

        ident = con("ident")
        E_MODEL, E_QK, E_64, E_SUB, E_ONE = (eps[:, i:i + 1] for i in range(5))

        def x_k(part, k, T):
            return x_op[:, part, k * T:(k + 1) * T]

        def x_all(part, T):
            return x_op[:, part, 0:KT * T]

        def flat2(a):
            return a.rearrange("p a b -> p (a b)")

        def banks(a, n):
            return ps[:, a:a + n, :].rearrange("p a b -> p (a b)")

        scratch = nc.dram_tensor("bias_lines", (DH, P + 1, LINE), F32, kind="Internal").ap()
        mem_store = nc.dram_tensor("mem_store", (P, 4 * NQ), F32, kind="Internal").ap()
        early_store = nc.dram_tensor("early_store", (EARLY, P, NQ), F32, kind="Internal").ap()
        skewed = scratch.rearrange("h p j -> h (p j)")

        M_IN = 0
        M_OUT = M_IN + 17
        M_QUERY = M_OUT + KT
        M_PEER = M_QUERY + 2 * PH + EARLY
        M_IN2 = M_PEER
        M_OUT2 = M_IN2 + 25
        M_XQ = M_OUT2 + KT
        M_XO = M_XQ + 2
        M_FFN = M_XO + 2

        R_ATTN, R_MEM, R_PEER, R_MIX, R_XATTN, R_FFN, R_FINAL = range(7)

        DEFERRED = (R_MIX, R_XATTN, R_FFN)

        def normed(r):
            return KT * sum(i not in DEFERRED for i in range(r))

        def operands(r):
            return r + 1 if r < R_MEM else r

        units = []
        for h in range(HEADS):
            units.append(dict(kind="mla", head=h, keys=NK, out=h))
        for h in range(DH):
            units.append(dict(kind="diff", head=h, map=0, keys=NK, out=None))
            units.append(dict(kind="diff", head=h, map=1, keys=NK, out=HEADS + h))
        for h in range(MH):
            units.append(dict(kind="moba", head=h, keys=NQ, out=HEADS + DH + h))
        for h in range(XH):
            units.append(dict(kind="xattn", head=h, keys=NQ, out=HEADS + DH + MH + h))
        U_MLA, U_DIFF, U_MOBA, U_X = (0, HEADS, HEADS + 2 * DH, HEADS + 2 * DH + MH)
        U_END = U_X + XH

        MEMORY_AT = [2, 5, 9]
        OUT_HI_AT = {8: 1, 11: 2, 14: 3}
        OUT_LO_AT = 12

        def out_tile(kind, h):
            return h // 2 + dict(mla=0, moba=2, xattn=KT - 2)[kind]

        def memory_bank(j):
            return 0 if j < 3 else 6

        def out_bank(o):
            return 7 if o % 2 == 0 else 1

        def outputs_read(o):
            return min(o - 1, HEADS) if o <= HEADS + DH else o - 1

        def walk(a, b):
            for i in range(a, b + 2):
                yield (i if i < b else None, i - 1 if a <= i - 1 < b else None, i - 2 if i - 2 >= a else None)

        def rest_taken(n):
            owner = lo_owner(n.first)
            before = sum(lo_owner(k) == owner for k in range(n.first))
            per = sum(lo_owner(n.first + k) == owner for k in range(n.stride))
            return sem(f"lo_{owner}"), n.value(before + 1, per)

        block = ctx.enter_context(nc.Block())

        @block.sync
        def _(sp):
            sp.dma_start(par[:, :], dram["params"]).then_inc(sem("par_loaded"), 16)
            sp.wait_ge(sem("h_loaded2"), 16)

            def load(n):
                sp.dma_start(raw[:, n.mod(RING), :], dram["blocks"][bass.ds(n.value(), 1)].rearrange("a p c -> p (a c)")
                             ).then_inc(sem(f"raw_loaded{n.mod(RING)}"), 16)

            def next_load(n):
                if B_MEM <= n.first - RING < B_OUT:
                    sp.wait_ge(sem("block_used"), n.first - RING + 1)
                else:
                    sp.wait_ge(*rest_taken(n.plus(-RING)))
                load(n)

            def early(w):
                return (w // 2 if w % 2 else None) if w < 4 * PH else w - 2 * PH

            def store(c, m):
                sp.wait_ge(sem("bank_free"), m.value())
                sp.dma_start(early_store[bass.ds(c.value(), 1)].rearrange("a p t -> p (a t)"), a_out[:, c.mod(RING), :]
                             ).then_inc(sem(f"early_stored{c.mod(RING)}"), 16)

            for j in range(RING):
                load(At(j))
            sp.dma_start(flat2(mem_t[:, :, :]), dram["mem_t"]).then_inc(sem("mem_loaded"), 16)
            for n in range(RING, B_EARLY + LOADS_AHEAD):
                next_load(At(n))
                w = n - LOADS_AHEAD - B_QUERY
                if w >= 0 and early(w) is not None:
                    store(At(early(w)), At(M_QUERY + w + 1))
            with sp.Fori(0, (EARLY - 2 * PH) // RING - 2) as i:
                for j in range(RING):
                    next_load(At(B_EARLY + LOADS_AHEAD + j, i, RING))
                    store(At(2 * PH + j, i, RING), At(M_QUERY + 4 * PH + j + 1, i, RING))
            for j in range(RING):
                next_load(At(B_V - 2 * RING + LOADS_AHEAD + j))
                store(At(EARLY - 2 * RING + j), At(M_PEER - 2 * RING + j + 1))
            for n in range(B_V - RING + LOADS_AHEAD, B_V + RING + 2):
                next_load(At(n))

            def early_back(v):
                c = v.plus(-RING)
                sp.dma_start(a_in[:, v.mod(RING), :], early_store[bass.ds(c.value(), 1)].rearrange("a p t -> p (a t)")
                             ).then_inc(sem(f"early_loaded{v.mod(RING)}"), 16)

            for j in range(RING):
                sp.wait_ge(sem(f"early_stored{j}"), 16 * (EARLY // RING - 1))
            sp.wait_ge(sem("g_ready"), NQ // 4)
            for v in range(RING, 2 * RING):
                early_back(At(v))
                if v >= RING + 2:
                    next_load(At(B_V + v))
            for v in range(2 * RING, 2 * RING + 2):
                next_load(At(B_V + v))
            with sp.Fori(0, EARLY // RING - 2) as i:
                for j in range(RING):
                    next_load(At(B_V + RING + LOADS_AHEAD + j, i, RING))
                    sp.wait_ge(sem("act_used"), At(RING + j + 1, i, RING).value())
                    early_back(At(2 * RING + j, i, RING))
            begin = B_PEER + LOADS_AHEAD - RING
            left = N_BLOCKS - begin
            with sp.Fori(0, left // RING) as i:
                for j in range(RING):
                    next_load(At(begin + j, i, RING))
            for n in range(N_BLOCKS - left % RING, N_BLOCKS):
                next_load(At(n))

        @block.gpsimd
        def _(pool):
            def lo(n):
                pool.wait_ge(sem("hi_done"), n.value(taken(n.first)))
                s = n.mod(RING)
                pool.tensor_tensor(w_lo[:, s, :], raw[:, s, :], w_hi[:, s, :].bitcast(F32), ALU.subtract
                                   ).then_inc(sem("lo_pool"), 1)

            def los(a, b):
                for n in range(a, b):
                    if lo_owner(n) == "pool":
                        lo(At(n))

            def norm_lo(r, T):
                for k in range(1, KT, 2):
                    pool.wait_ge(sem("rms_hi"), KT * (operands(r) - 1) + k + 1)
                    pool.tensor_tensor(x_k(1, k, T), xf[:, k * T:(k + 1) * T], x_k(0, k, T).bitcast(F32), ALU.subtract
                                       ).then_inc(sem("x_odd"), 1)

            def add_squares(r, n):
                for k in range(1, KT - 1):
                    los(pool_at[0], n + k + 3)
                    pool_at[0] = max(pool_at[0], n + k + 3)
                    pool.wait_ge(sem("rms_squares"), KT * r + k + 1)
                    if squares_added[0]:
                        pool.wait_ge(sem("squares_added"), squares_added[0])
                    pool.tensor_tensor(sq[:, 0:NQ], sq[:, 0:NQ], sq[:, k * NQ:(k + 1) * NQ], ALU.add
                                       ).then_inc(sem("squares_added"), 1)
                    squares_added[0] += 1

            pool_at, squares_added = [0], [0]

            def normalise(a, b):
                for u in range(a, b):
                    x, n = units[u], units[u]["keys"]
                    if x["kind"] == "diff" and x["map"] == 1:
                        continue
                    s = scores_sb[:, u % 3, :, 0:n]
                    pool.wait_ge(sem("row_inverse"), u + 1)
                    pool.tensor_tensor(s, s, row_inv[:, u % 3, :].unsqueeze(2).to_broadcast([P, 2, n]), ALU.mult
                                       ).then_inc(sem("probs_normed"), 1)

            pool.memset(ones[:, :], 1.0).then_inc(sem("ones_set"), 1)
            for i, v in enumerate((EPS, QK * EPS, 64 * EPS, EPS / (1 - LAMBDA_INIT) ** 2, 1.0)):
                ins = pool.memset(eps[:, i:i + 1], v)
            ins.then_inc(sem("eps_set"), 1)
            pool.memset(one_in, 0.0)
            pool.memset(pair_in, 0.0)
            pool.memset(two_in, 0.0).then_inc(sem("windows_zero"), 1)
            los(B_IN, B_IN + 1)
            norm_lo(R_ATTN, NK)
            los(B_IN + 1, B_IN + 9)
            pool.wait_ge(sem("cst_loaded"), 16)
            pool.wait_ge(sem("rms_xf"), KT * (R_MEM + 1))
            pool.wait_ge(sem("q_raw"), 1)
            pool.tensor_tensor(rope_a[:, :, 0:NQ], q_mla,
                               con("cos", QK, cst)[:, N_META:NK].unsqueeze(1).to_broadcast([QK, HEADS, NQ]),
                               ALU.mult).then_inc(sem("rope_cos"), 1)
            los(B_IN + 9, B_MEM)
            pool.wait_ge(sem("bias_loaded"), 16 * 2 * DH)
            pool.tensor_tensor(
                bias, bias, con("mask", at=cst).rearrange("p (t k) -> p t k", t=2).unsqueeze(1).to_broadcast([P, DH, 2, NK]),
                ALU.add).then_inc(sem("bias_ready"), 1)
            normalise(U_MLA, U_MOBA)
            pool_at[0] = B_OUT
            add_squares(R_PEER, B_OUT)
            los(pool_at[0], B_QUERY + 2)
            norm_lo(R_PEER, NQ)
            los(B_QUERY + 2, B_QUERY + RING)
            with pool.Fori(1, (B_V - B_QUERY) // RING) as i:
                for j in range(RING):
                    lo(At(B_QUERY + j, i, RING))
            def even(first, end):
                first += first % 2
                rounds = (end - first) // RING
                with pool.Fori(0, rounds) as i:
                    for j in range(0, RING, 2):
                        lo(At(first + j, i, RING))
                los(first + RING * rounds, end)

            lo(At(B_V))
            even(B_V + 1, B_IN2 + 2)
            even(B_IN2 + 2, B_OUT2 + 2)
            normalise(U_MOBA, U_X)
            pool_at[0] = B_OUT2 + 2
            add_squares(R_XATTN, B_OUT2)
            los(pool_at[0], B_FFN + 2)
            normalise(U_X, U_END)
            even(B_FFN + 2, N_BLOCKS)

        @block.scalar
        def _(act):
            def hi(n):
                s = n.mod(RING)
                act.wait_ge(sem(f"raw_loaded{s}"), n.div(RING) * 16 + 16)
                if n.first >= RING:
                    act.wait_ge(sem("block_used"), n.plus(1 - RING).value())
                act.activation(w_hi[:, s, :], raw[:, s, :], ACT.Copy).then_inc(sem("hi_done"), 1)

            ahead = [0]

            def his(upto):
                while ahead[0] < min(upto, N_BLOCKS):
                    if lo_owner(ahead[0]):
                        hi(At(ahead[0]))
                    ahead[0] += 1

            def evacuate(n, m, dst, rows=P, T=NQ, scale=1.0):
                act.wait_ge(sem("block_used"), n + 1)
                act.activation(dst, ps[0:rows, m % 2, 0:T], ACT.Copy, scale=scale).then_inc(sem("bank_free"), 1)

            def squares(src, k, T, n=1):
                act.activation(sq[:, k * T:(k + n) * T], src, ACT.Square).then_inc(sem("rms_squares"), n)

            def root(r, T, bank=2):
                act.wait_ge(sem("rms_sum"), r + 1)
                act.activation(rt[:, 0:T], ps[:, bank, 0:T], ACT.Sqrt, scale=1.0 / D, bias=E_MODEL).then_inc(sem("rms_root"), 1)

            def norm_hi(r, T, n):
                if n:
                    act.wait_ge(sem("block_used"), n)
                for k in range(KT):
                    act.wait_ge(sem("rms_xf"), normed(r) + k + 1)
                    act.activation(x_k(0, k, T), xf[:, k * T:(k + 1) * T], ACT.Copy).then_inc(sem("rms_hi"), 1)

            def gained_hi(r, gain, tiles):
                for k in tiles:
                    act.activation(x_k(0, k, NQ), res[:, k, :], ACT.Copy, scale=pcol(gain, k)).then_inc(sem("rms_hi"), 1)

            for c in range(4):
                at = slice(2 * c * NK, 2 * (c + 1) * NK)
                act.dma_start(flat2(h_t)[:, at], dram["h_t"][:, at]).then_inc(sem(f"h_loaded{c}"), 16)
            act.dma_start(kept[:, :], dram["consts"][:, 0:N_CONSTS_KEPT]).then_inc(sem("kept_loaded"), 16)
            act.dma_start(rel_in, dram["rel_bias"]).then_inc(sem("rel_loaded"), 16)
            act.wait_ge(sem("eps_set"), 1)
            act.activation(eps[:, 5:6], eps[:, 4:5], ACT.Sqrt)
            act.wait_ge(sem("par_loaded"), 16)
            for c in range(4):
                act.wait_ge(sem(f"h_loaded{c}"), 16)
                squares(flat2(h_t)[:, 2 * c * NK:2 * (c + 1) * NK], 2 * c, NK, 2)
            root(R_ATTN, NK)
            his(2)
            act.dma_start(cst, dram["consts"][:, N_CONSTS_KEPT:]).then_inc(sem("cst_loaded"), 16)
            act.dma_start(flat2(w_uq), dram["w_uq"]).then_inc(sem("wu_loaded"), 16)
            act.dma_start(flat2(w_ukv), dram["w_ukv"]).then_inc(sem("wu_loaded"), 16)
            norm_hi(R_ATTN, NK, 0)

            def line_out(h):
                act.wait_ge(sem("line_done"), h + 1)
                if h:
                    act.wait_ge(sem("line_stored"), 16 * h)
                act.activation(line[:, 0:LINE // 2], ps[:, 4, 0:LINE // 2], ACT.Copy)
                act.activation(line[:, LINE // 2:LINE], ps[:, 5, 0:LINE - LINE // 2], ACT.Copy).then_inc(sem("line_ready"), 1)
                act.wait_ge(sem("line_ready"), h + 1)
                act.dma_start(scratch[h, 0:P], line).then_inc(sem("line_stored"), 16)

            def evacuate_in(j):
                his(B_IN + j + 3)
                act.wait_ge(sem("block_used"), B_IN + j + 1)
                b = ps[:, (M_IN + j) % 2]
                if j == 4:
                    act.activation(rope_sq, b[NOPE:QK, 0:NK], ACT.Square)
                    ins = act.activation(rope_k, b[NOPE:QK, 0:NK], ACT.Copy, scale=pcol("qkk")[NOPE:QK])
                elif 5 <= j < 9:
                    act.activation(dq_sq[:, j - 5, :], b[:, N_META:NK], ACT.Square)
                    ins = act.activation(dqn[:, j - 5, :], b[:, N_META:NK], ACT.Copy, scale=pcol("dq"))
                elif 9 <= j < 13:
                    act.activation(dk_sq[:, j - 9, :], b[:, 0:NK], ACT.Square)
                    ins = act.activation(dkn[:, j - 9, :], b[:, 0:NK], ACT.Copy, scale=pcol("dk"))
                else:
                    ins = act.activation(proj[:, j if j < 4 else j - 8, :], b[:, 0:NK], ACT.Copy)
                ins.then_inc(sem("bank_free"), 1)

            def lat_squares(w):
                src, n = ((proj[:, 0:2, N_META:NK], NQ), (proj[:, 2:4, :], NK))[w]
                act.wait_ge(sem("bank_free"), M_IN + 2 * w + 2)
                act.activation(lat_sq[:, w * 2 * NQ:w * 2 * NQ + 2 * n].rearrange("p (a b) -> p a b", a=2), src,
                               ACT.Square).then_inc(sem("lat_squares"), 1)

            def lat_root(w):
                n = (NQ, NK)[w]
                act.wait_ge(sem("lat_sum"), w + 1)
                act.activation((rt, rb)[w][:, 0:n], ps[:, 2 + w, 0:n], ACT.Sqrt, scale=1.0 / 256,
                               bias=E_MODEL).then_inc(sem("lat_root"), 1)

            def v_out(t):
                rows = min(P, NK - P * t)
                act.wait_ge(sem("v_product"), t + 1)
                act.activation(v_mla[0:rows, t, :], ps[0:rows, 2 + t % 2, :], ACT.Copy).then_inc(sem("v_ready"), 1)

            def k_out(w):
                act.wait_ge(sem("k_product"), w + 1)
                act.activation(sq[0:NOPE, 4 * w * NK:4 * (w + 1) * NK].rearrange("p (h n) -> p h n", h=4),
                               ps[0:NOPE, 4:8, 0:NK], ACT.Square)
                act.activation(k_mla[0:NOPE, 4 * w:4 * w + 4, :], ps[0:NOPE, 4:8, 0:NK], ACT.Copy,
                               scale=pcol("qkk")[0:NOPE]).then_inc(sem("k_raw"), 1)

            act.wait_ge(sem("mem_loaded"), 16)
            squares(flat2(mem_t[:, :, :]), 0, NQ, KT)
            act.wait_ge(sem("x_even"), KT // 2)
            act.wait_ge(sem("x_odd"), KT // 2)
            evacuate_in(0)
            line_out(0)
            evacuate_in(1)
            lat_squares(0)
            line_out(1)
            act.wait_ge(sem("rms_sum"), R_MEM + 1)
            act.activation(mem_rt, ps[:, 3, 0:NQ], ACT.Sqrt, scale=1.0 / D, bias=E_MODEL).then_inc(sem("rms_root"), 1)
            evacuate_in(2)
            lat_root(0)
            line_out(2)
            evacuate_in(3)
            lat_squares(1)
            line_out(3)
            evacuate_in(4)
            lat_root(1)
            evacuate_in(5)
            act.wait_ge(sem("q_product"), 1)
            act.activation(flat2(q_mla), banks(4, 4)[0:QK, :], ACT.Copy, scale=pcol("qkq", rows=QK)).then_inc(sem("q_raw"), 1)
            act.activation(xf[0:QK, 0:HEADS * NQ], banks(4, 4)[0:QK, :], ACT.Square).then_inc(sem("q_squares"), 1)
            evacuate_in(6)
            act.wait_ge(sem("line_stored"), 16 * DH)
            for h in range(DH):
                for t in range(2):
                    start = FAR - N_META - P * t
                    src = skewed[h, start:start + P * (LINE - 1)].rearrange("(p j) -> p j", j=LINE - 1)[:, 0:NK]
                    act.dma_start(bias[:, h, t, :], src).then_inc(sem("bias_loaded"), 16)
            evacuate_in(7)
            v_out(0)
            v_out(1)
            evacuate_in(8)
            v_out(2)
            evacuate_in(9)
            k_out(0)
            evacuate_in(10)
            k_out(1)
            evacuate_in(11)
            act.wait_ge(sem("k_sum"), 1)
            act.activation(rk[:, 0, :], ps[0:8, 3, 0:NK], ACT.Sqrt, scale=1.0 / QK, bias=E_MODEL[0:8]).then_inc(sem("k_root"), 1)
            evacuate_in(12)
            act.wait_ge(sem("q_sum"), 1)
            for w, e in enumerate((E_QK, E_64)):
                ins = act.activation(rq[:, w].rearrange("p t h -> p (t h)"), ps[:, 2, 16 * w:16 * w + 16], ACT.Sqrt, bias=e)
            ins.then_inc(sem("q_root"), 1)
            evacuate_in(13)
            act.wait_ge(sem("k_sum"), 2)
            act.activation(rk[:, 1, :], ps[0:8, 3, 0:NK], ACT.Sqrt, scale=1.0 / 64, bias=E_MODEL[0:8]).then_inc(sem("k_root"), 1)
            evacuate_in(14)
            evacuate_in(15)
            act.wait_ge(sem("lam_sum"), 1)
            act.activation(lam[:, 4:6], ps[:, 2, 0:2], ACT.Exp).then_inc(sem("lam_exp"), 1)
            evacuate_in(16)

            def memory_out(j):
                if j < 4:
                    act.wait_ge(sem("block_used"), B_MEM + j + 1)
                    act.activation(k_mem[:, j, :] if j < 2 else v_mem_t[:, j - 2, :], ps[:, memory_bank(j), 0:NQ], ACT.Copy
                                   ).then_inc(sem("memory_out"), 1)
                else:
                    act.wait_ge(sem("v_mem_turned"), 1)
                    act.activation(flat2(v_mem), ps[:, memory_bank(j), :], ACT.Copy).then_inc(sem("v_mem_ready"), 1)
                    act.wait_ge(sem("v_mem_ready"), 1)
                    act.wait_ge(sem("memory_out"), 4)
                    act.dma_start(mem_store, flat2(kv_mem[:, :, :])).then_inc(sem("mem_stored"), 16)

            def soft(u):
                n = units[u]["keys"]
                act.wait_ge(sem("max_ready"), u + 1)
                kind, h = units[u]["kind"], units[u]["head"]
                for t in range(2):
                    s = scores_sb[:, u % 3, t, 0:n]
                    src = ps[:, 2 + 2 * (u % 2) + t, 0:n] if kind == "xattn" else s
                    ins = act.activation(s, src, ACT.Exp, scale=rq[:, 0, t, h:h + 1] if kind == "mla" else 1.0,
                                         bias=row_max[:, u % 3, t:t + 1], accum_out=row_sum[:, u % 3, t:t + 1])
                ins.then_inc(sem("exp_done"), 1)

            def probs_out(u):
                x, o = units[u], units[u]["out"]
                act.wait_ge(sem("probs_turned"), o + 1)
                if x["keys"] > NQ:
                    act.activation(probs_t[0:N_META, o % 2, 2, :], ps[0:N_META, out_bank(o), NQ:2 * NQ], ACT.Copy)
                act.activation(flat2(probs_t[:, o % 2, 0:2, :]), ps[:, 6, :], ACT.Copy).then_inc(sem("probs_ready"), 1)

            def head_out(u):
                kind, h, o = units[u]["kind"], units[u]["head"], units[u]["out"]
                act.wait_ge(sem("out_done"), o + 1)
                if kind == "diff":
                    act.activation(sq[:, h * NQ:(h + 1) * NQ], ps[:, out_bank(o), 0:NQ], ACT.Square).then_inc(sem("sub_squares"), 1)
                    dst, src = o_diff[:, h, :], ps[:, out_bank(o), 0:NQ]
                else:
                    rows = slice(64 * (h % 2), 64 * (h % 2) + 64)
                    dst, src = x_k(0, out_tile(kind, h), NQ)[rows], ps[rows, out_bank(o), 0:NQ]
                act.activation(dst, src, ACT.Copy).then_inc(sem("y_hi"), 1)

            def attention(a, b, begun=False):
                for s, p, o in walk(a, b):
                    if s is not None and not (begun and s == a):
                        soft(s)
                    if o is not None and units[o]["out"] is not None:
                        head_out(o)
                    if p is not None and units[p]["out"] is not None:
                        probs_out(p)
                    if s in MEMORY_AT:
                        memory_out(MEMORY_AT.index(s))
                    if s in OUT_HI_AT:
                        his(B_OUT + OUT_HI_AT[s])

            attention(U_MLA, U_MOBA)
            act.wait_ge(sem("sub_sum"), 1)
            act.activation(sub_r, ps[0:8, 0, 0:NQ], ACT.Sqrt, scale=1.0 / (P * (1 - LAMBDA_INIT) ** 2),
                           bias=E_SUB[0:8]).then_inc(sem("sub_root"), 1)
            memory_out(3)
            for h in range(DH):
                act.wait_ge(sem("sub_ready"), h + 1)
                act.activation(x_k(0, 4 + h, NQ), xf[:, h * NQ:(h + 1) * NQ], ACT.Copy).then_inc(sem("sub_hi"), 1)
            his(B_OUT + 4)
            for j in range(KT):
                his(B_OUT + j + 4)
                act.wait_ge(sem("bank_free"), M_OUT + j + 1)
                squares(res[:, j, :], j, NQ)
            act.dma_start(flat2(sub_keys), dram["sub_keys"]).then_inc(sem("sub_keys_loaded"), 16)
            root(R_PEER, NQ)
            norm_hi(R_PEER, NQ, B_QUERY)
            memory_out(4)
            act.wait_ge(sem("mem_stored"), 16)

            def early(c, m):
                act.wait_ge(sem("block_used"), m.plus(B_QUERY - M_QUERY + 1).value())
                if c.first >= RING:
                    act.wait_ge(sem(f"early_stored{c.mod(RING)}"), c.div(RING) * 16)
                act.activation(a_out[:, c.mod(RING), :], ps[:, m.mod(2), 0:NQ], ACT.Gelu).then_inc(sem("bank_free"), 1)

            for w in range(4 * PH):
                his(B_QUERY + w + 3)
                if w % 2 == 0:
                    evacuate(B_QUERY + w, M_QUERY + w, q_peer[:, w // 2, :])
                else:
                    early(At(w // 2), At(M_QUERY + w))
            for w in range(4 * PH, B_BESIDE - B_QUERY):
                his(B_QUERY + w + 3)
                if w == B_BESIDE - B_QUERY - 1:
                    for r in range(3):
                        act.wait_ge(sem("route_turned"), r + 1)
                        act.activation(route_t[:, r, :], ps[:, 2 + r, 0:NQ], ACT.Copy).then_inc(sem("route_t_ready"), 1)
                early(At(w - 2 * PH), At(M_QUERY + w))
                if w == 4 * PH + SOFT_AT:
                    act.wait_ge(sem("soft_in"), 1)
                    act.activation(soft_flat, soft_flat, ACT.Exp).then_inc(sem("soft_exp"), 1)

            def beside(i):
                for j in range(RING):
                    for g in range(2 * j, 2 * j + 2):
                        act.wait_ge(sem("g_product"), At(g + 1, i, 8).value())
                        act.activation(big[:, bass.ds(At(512 * g, i, 4096).value(), 512)], ps[:, 2 + g % 2, :],
                                       ACT.Copy).then_inc(sem("g_ready"), 1)
                    hi(At(B_BESIDE + 3 + j, i, RING))
                    early(At(EARLY - EARLY_G + j, i, RING), At(M_PEER - EARLY_G + j, i, RING))

            his(B_BESIDE + 3)
            beside(0)
            with act.Fori(1, EARLY_G // RING) as i:
                beside(i)
            with act.Fori(0, EARLY // RING) as i:
                for j in range(RING):
                    hi(At(B_V + 3 + j, i, RING))
            ahead[0] = B_PEER + 3

            def chunk(d):
                act.wait_ge(sem("block_used"), d.value(B_PEER + max(2 * d.first, 1), 2 * d.stride))
                act.wait_ge(sem("act_used"), d.plus(EARLY - 1).value())
                act.activation(ge[:, d.mod(2), :], ps[:, d.mod(2), 0:NQ], ACT.Gelu).then_inc(sem("gelu_done"), 1)

            his(B_PEER + 3)
            for d in range(2):
                chunk(At(d))
                hi(At(B_PEER + 3 + 2 * d))
                hi(At(B_PEER + 4 + 2 * d))
            with act.Fori(0, (NKEYS - EARLY - 4) // 2) as i:
                for d in range(2):
                    chunk(At(2 + d, i, 2))
                    hi(At(B_PEER + 7 + 2 * d, i, 4))
                    hi(At(B_PEER + 8 + 2 * d, i, 4))
            ahead[0] = B_IN2 - 1
            chunk(At(NKEYS - EARLY - 2))
            his(B_IN2)
            chunk(At(NKEYS - EARLY - 1))
            act.wait_ge(sem("acts_ready"), NKEYS)
            act.dma_start(cst2, dram["consts"][:, N_CONSTS_KEPT:]).then_inc(sem("cst2_loaded"), 16)
            act.dma_start(w_gate, dram["w_gate"]).then_inc(sem("cst2_loaded"), 16)
            act.dma_start(flat2(kv_x), mem_store).then_inc(sem("kv_back"), 16)

            def residual_squares(r):
                for b in range(4):
                    act.wait_ge(sem("res_ready"), 4 * r + b + 1)
                    squares(flat2(res[:, 2 * b:2 * b + 2, :]), 2 * b, NQ, 2)

            his(B_IN2 + 2)
            act.wait_ge(sem("block_used"), B_IN2 - 2)
            for b in range(4):
                act.wait_ge(sem("res_ready"), b + 1)
                gained_hi(R_MIX, "mix", range(2 * b, 2 * b + 2))
            residual_squares(0)
            root(R_MIX, NQ)
            his(B_IN2 + 4)
            act.wait_ge(sem("gate_product"), 1)
            act.activation(z, ps[:, 2, 0:NQ], ACT.Identity, bias=pcol("gate_b")).then_inc(sem("gate_z"), 1)
            act.wait_ge(sem("gate_z"), 1)
            act.activation(z2, z, ACT.Abs).then_inc(sem("gate_step"), 1)
            act.wait_ge(sem("gate_step"), 1)
            act.activation(z2, z2, ACT.Exp, scale=-1.0).then_inc(sem("gate_step"), 1)
            his(B_IN2 + 6)
            act.wait_ge(sem("gate_step"), 2)
            act.activation(z2, z2, ACT.Ln, bias=E_ONE).then_inc(sem("gate_ln"), 1)
            his(B_IN2 + 7)
            act.wait_ge(sem("csum_ready"), 1)
            act.activation(e_pos, csum, ACT.Exp).then_inc(sem("gla_exp"), 1)
            act.activation(e_neg, csum, ACT.Exp, scale=-1.0).then_inc(sem("gla_exp"), 1)
            for n in range(NCH):
                last = csum[:, CHUNK * n + CHUNK - 1:CHUNK * n + CHUNK]
                act.activation(e_end[:, CHUNK * n:CHUNK * n + CHUNK], csum[:, CHUNK * n:CHUNK * n + CHUNK], ACT.Exp,
                               scale=-1.0, bias=last)
                ins = act.activation(decay[:, n:n + 1], last, ACT.Exp)
            ins.then_inc(sem("gla_exp"), 1)
            his(B_IN2 + 9)
            act.wait_ge(sem("bank_free"), M_IN2 + 7)
            act.activation(flat2(silu_o), flat2(proj2[:, 22:24, :]), ACT.Silu).then_inc(sem("silu_ready"), 1)
            act.wait_ge(sem("gla_turned"), 1)
            act.activation(flat2(v_gla), banks(2, 2)[0:CHUNK, :], ACT.Copy).then_inc(sem("gla_v"), 1)
            act.activation(flat2(kend_t), ps[0:CHUNK, 4, :], ACT.Copy).then_inc(sem("gla_v"), 1)
            his(B_IN2 + 12)
            act.wait_ge(sem("gla_out"), 1)
            act.activation(sq[:, 0:2 * NQ].rearrange("p (a b) -> p a b", a=2), ps[:, 2:4, 0:NQ], ACT.Square
                           ).then_inc(sem("gla_squares"), 1)
            act.activation(o_gla, ps[:, 2:4, 0:NQ], ACT.Copy).then_inc(sem("gla_o"), 1)
            his(B_IN2 + 13)
            act.wait_ge(sem("gla_sum"), 1)
            act.activation(acc_sb[:, 0:512], ps[:, 4, :], ACT.Sqrt, scale=1.0 / GDV, bias=E_MODEL).then_inc(sem("gla_root"), 1)
            his(B_IN2 + 25)
            soft(U_MOBA)
            his(B_IN2 + 27)
            act.wait_ge(sem("block_used"), B_OUT2)
            act.wait_ge(sem("mix_ready"), 2)
            act.activation(x_op[:, 0, 0:2 * NQ], flat2(conv_y), ACT.Copy).then_inc(sem("mix_hi"), 1)
            act.activation(x_op[:, 0, 6 * NQ:8 * NQ], flat2(y_gla), ACT.Copy).then_inc(sem("mix_hi"), 1)
            attention(U_MOBA, U_X, True)
            for j in range(KT):
                his(B_OUT2 + j + 3)
                act.wait_ge(sem("bank_free"), M_OUT2 + j + 1)
                squares(res[:, j, :], j, NQ)
            act.wait_ge(sem("block_used"), B_XQ)
            gained_hi(R_XATTN, "xattn", range(KT))
            root(R_XATTN, NQ)
            his(B_FFN + 2)
            attention(U_X, U_END)
            his(B_FFN + 2)
            for b in range(2):
                act.wait_ge(sem("bank_free"), M_XO + b + 1)
                gained_hi(R_FFN, "ffn2", range(4 * b, 4 * b + 4))
                his(B_FFN + 2 + b)
                squares(flat2(res[:, 4 * b:4 * b + 4, :]), 4 * b, NQ, 4)
            root(R_FFN, NQ)

            def pvar(name, per, k, p):
                return par[:, bass.ds(p.value(PARAMS[name][0] + k + per * p.first, per * p.stride), 1)]

            def taps(p):
                for half, buf in enumerate((conv_a, conv_g)):
                    act.wait_ge(sem("bank_free"), p.value(M_FFN + 2 * p.first + half + 1, 2 * p.stride))
                    if half == 0 and p.first >= 2:
                        act.wait_ge(sem("act_used"), p.value(NKEYS + p.first - 1))
                    act.activation(buf[:, p.mod(2), :], up_out[:, half, p.mod(2), :], ACT.Identity, scale=pvar("cw", 6, 3 * half + 2, p),
                                   bias=pvar("cb", 2, half, p)).then_inc(sem("tap_done"), 1)

            def silu(p):
                act.wait_ge(sem("conv_done"), p.value(2 * p.first + 1, 2 * p.stride))
                act.activation(act_a[:, p.mod(2), :], conv_a[:, p.mod(2), :], ACT.Silu).then_inc(sem("silu_done"), 1)

            def tile(p):
                n = At(B_FFN + 3 * p.first + 3, p.i, 3 * p.stride)
                hi(n)
                taps(p)
                hi(n.plus(1))
                silu(p)
                hi(n.plus(2))

            his(B_FFN + 3)
            tile(At(0))
            with act.Fori(0, (FT - 2) // 4) as i:
                for j in range(4):
                    tile(At(1 + j, i, 4))
            taps(At(FT - 1))
            silu(At(FT - 1))
            residual_squares(1)
            root(R_FINAL, NQ)
            for f in range(2):
                at = slice(4 * f * NQ, 4 * (f + 1) * NQ)
                act.wait_ge(sem("rms_xf"), normed(R_FINAL) + 4 * f + 4)
                act.dma_start(dram["out"][:, at], xf[:, at]).then_inc(sem("out_stored"), 16)
            act.wait_ge(sem("out_stored"), 32)

        @block.vector
        def _(dve):
            steps = [0]

            def step(ins):
                steps[0] += 1
                ins.then_inc(sem("dve_step"), 1)
                dve.wait_ge(sem("dve_step"), steps[0])

            def lo(n):
                dve.wait_ge(sem("hi_done"), n.value(taken(n.first)))
                s = n.mod(RING)
                dve.tensor_tensor(w_lo[:, s, :], raw[:, s, :], w_hi[:, s, :].bitcast(F32), ALU.subtract
                                  ).then_inc(sem("lo_dve"), 1)

            ahead = [0]

            def los(upto):
                while ahead[0] < min(upto, N_BLOCKS):
                    if lo_owner(ahead[0]) == "dve":
                        lo(At(ahead[0]))
                    ahead[0] += 1

            def norm(r, src, gain, T, operand=True):
                dve.wait_ge(sem("rms_root"), r + 1)
                step(dve.reciprocal(rb[:, 0:T], rt[:, 0:T]))

                def lower(k):
                    dve.wait_ge(sem("rms_hi"), KT * (operands(r) - 1) + k + 1)
                    dve.tensor_tensor(x_k(1, k, T), xf[:, k * T:(k + 1) * T], x_k(0, k, T).bitcast(F32), ALU.subtract
                                      ).then_inc(sem("x_even"), 1)

                for k in range(KT):
                    dve.scalar_tensor_tensor(out=xf[:, k * T:(k + 1) * T], in0=src[:, k, :], scalar=pcol(gain, k),
                                             in1=rb[:, 0:T], op0=ALU.mult, op1=ALU.mult).then_inc(sem("rms_xf"), 1)
                    if operand and k % 2:
                        lower(k - 1)

            def gained_lo(r, gain, tiles=range(KT)):
                for k in tiles:
                    dve.wait_ge(sem("rms_hi"), KT * (operands(r) - 1) + k + 1)
                    dve.scalar_tensor_tensor(out=x_k(1, k, NQ), in0=res[:, k, :], scalar=pcol(gain, k), in1=x_k(0, k, NQ).bitcast(F32),
                                             op0=ALU.mult, op1=ALU.subtract).then_inc(sem("x_odd" if k % 2 else "x_even"), 1)

            def inverse_root(r):
                dve.wait_ge(sem("rms_root"), r + 1)
                step(dve.reciprocal(rb[:, 0:NQ], rt[:, 0:NQ]))

            dve.wait_ge(sem("par_loaded"), 16)
            for c in range(4):
                dve.wait_ge(sem(f"h_loaded{c}"), 16)
            norm(R_ATTN, h_t, "attn", NK)
            dve.wait_ge(sem("rel_loaded"), 16)
            dve.tensor_copy(rel_rep, rel_in.unsqueeze(2).to_broadcast([BUCKETS, DH, P])).then_inc(sem("rel_ready"), 1)
            l0 = PARAMS["lam"][0]
            dve.tensor_tensor(lam[0:64, 0:2], par[0:64, l0:l0 + 4:2], par[0:64, l0 + 1:l0 + 4:2], ALU.mult
                              ).then_inc(sem("lam_ready"), 1)
            dve.wait_ge(sem("windows_zero"), 1)
            dve.memset(one_in[:, 7:8], 1.0)
            dve.memset(pair_in[:, 6:8], 1.0)
            for a in range(2):
                ins = dve.memset(two_in[64 * a:64 * a + 64, 6 + a:7 + a], 1.0)
            ins.then_inc(sem("windows_set"), 1)
            dve.wait_ge(sem("kept_loaded"), 16)
            for a, n in ((head_of, QK), (map_of, 64)):
                ins = dve.tensor_copy(a.rearrange("p (h n) -> p h n", h=8), ident[0:8, 0:8].unsqueeze(2).to_broadcast([8, 8, n]))
            ins.then_inc(sem("heads_set"), 1)
            los(B_IN + 4)
            dve.wait_ge(sem("rms_root"), R_MEM + 1)
            step(dve.reciprocal(mem_rb, mem_rt))
            for k in range(KT):
                ins = dve.scalar_tensor_tensor(out=mem_t[:, k, :], in0=mem_t[:, k, :], scalar=pcol("mem", k), in1=mem_rb,
                                               op0=ALU.mult, op1=ALU.mult)
            ins.then_inc(sem("rms_xf"), KT)

            def latent_norm(w):
                src, dst, n, gain = ((proj[:, 0:2, N_META:NK], cqn, NQ, "qn"), (proj[:, 2:4, :], ckvn, NK, "kvn"))[w]
                r = (rt, rb)[w][:, 0:n]
                dve.wait_ge(sem("lat_root"), w + 1)
                step(dve.reciprocal(r, r))
                for k in range(2):
                    ins = dve.scalar_tensor_tensor(out=dst[:, k, :], in0=src[:, k, :], scalar=pcol(gain, k), in1=r,
                                                   op0=ALU.mult, op1=ALU.mult)
                ins.then_inc(sem("lat_ready"), 1)

            latent_norm(0)
            los(B_IN + 6)
            latent_norm(1)
            los(B_IN + 8)
            dve.wait_ge(sem("bank_free"), M_IN + 5)
            dve.wait_ge(sem("cst_loaded"), 16)
            dve.wait_ge(sem("q_product"), 1)
            dve.tensor_tensor(rope_kc, rope_k, con("cos", QK, cst)[NOPE:QK, :], ALU.mult).then_inc(sem("rope_kc_ready"), 1)
            los(B_IN + 10)
            dve.wait_ge(sem("qk_turned"), 1)
            dve.wait_ge(sem("rope_cos"), 1)
            sin = con("sin", QK, cst)[:, N_META:NK].unsqueeze(1).to_broadcast([QK, HEADS, NQ])
            dve.tensor_tensor(q_mla, banks(4, 4)[0:QK, :].rearrange("p (h n) -> p h n", h=HEADS), sin, ALU.mult
                              ).then_inc(sem("qk_turned_read"), 1)
            los(B_IN + 12)
            dve.wait_ge(sem("qk_turned_read"), 1)
            dve.tensor_tensor(q_mla, q_mla, rope_a[:, :, 0:NQ], ALU.add).then_inc(sem("q_ready"), 1)
            dve.wait_ge(sem("qk_turned"), 2)
            dve.wait_ge(sem("rope_kc_ready"), 1)
            dve.tensor_tensor(rope_k, ps[NOPE:QK, 2, 0:NK], con("sin", QK, cst)[NOPE:QK, :], ALU.mult
                              ).then_inc(sem("qk_turned_read"), 1)
            dve.wait_ge(sem("qk_turned_read"), 2)
            dve.tensor_tensor(rope_k, rope_k, rope_kc, ALU.add).then_inc(sem("rope_k_ready"), 1)
            los(B_IN + 14)
            dve.wait_ge(sem("k_root"), 1)
            dve.reciprocal(rk[:, 0, :], rk[:, 0, :]).then_inc(sem("k_inverse"), 1)
            rq_flat = rq.rearrange("p w t h -> p (w t h)")
            dve.wait_ge(sem("q_root"), 1)
            dve.reciprocal(rq_flat, rq_flat).then_inc(sem("q_ready"), 1)

            def key_scale(w):
                at = slice(4 * w, 4 * w + 4)
                dve.wait_ge(sem("k_spread"), w + 1)
                dve.tensor_tensor(k_mla[0:NOPE, at, :], k_mla[0:NOPE, at, :], ps[0:NOPE, 4:8, 0:NK], ALU.mult)
                dve.tensor_tensor(k_mla[NOPE:QK, at, :], ps[NOPE:QK, 4:8, 0:NK],
                                  rope_k.unsqueeze(1).to_broadcast([ROPE, 4, NK]), ALU.mult).then_inc(sem("k_ready"), 1)

            dve.wait_ge(sem("k_raw"), 2)
            dve.wait_ge(sem("rope_k_ready"), 1)
            key_scale(0)
            dve.wait_ge(sem("k_root"), 2)
            dve.reciprocal(rk[:, 1, :], rk[:, 1, :]).then_inc(sem("k_inverse"), 1)
            los(B_IN + 16)
            key_scale(1)
            los(B_MEM)
            dve.wait_ge(sem("k_spread"), 3)
            dve.tensor_tensor(dkn, dkn, ps[:, 4:8, 0:NK], ALU.mult).then_inc(sem("k_ready"), 1)
            dve.wait_ge(sem("lam_exp"), 1)
            step(dve.tensor_tensor(lam[:, 6:7], lam[:, 5:6], lam[:, 4:5], ALU.subtract))
            step(dve.tensor_scalar(lam[:, 7:8], lam[:, 6:7], -LAMBDA_INIT, None, ALU.add))
            dve.wait_ge(sem("q_ready"), 2)

            def soft_in(u):
                x = units[u]
                n, b = x["keys"], 2 + 2 * (u % 2)
                s = scores_sb[:, u % 3, :, 0:n]
                src = ps[:, b:b + 2, 0:n]
                dve.wait_ge(sem("scores_done"), u + 1)
                if u >= 3:
                    dve.wait_ge(sem("probs_turned"), sum(1 for v in units[:u - 2] if v["out"] is not None))
                    if units[u - 3]["out"] is None:
                        dve.wait_ge(sem("probs_normed"), u - 1)
                h, m = x["head"], row_inv[:, u % 3, :]
                if x["kind"] == "mla":
                    mask = con("mask", at=cst).rearrange("p (t k) -> p t k", t=2)
                    for t in range(2):
                        ins = dve.tensor_tensor_reduce(s[:, t], src[:, t], mask[:, t], 1.0, -3.0e38, ALU.add, ALU.max, m[:, t:t + 1])
                    ins.then_inc(sem("scores_read"), 1)
                    dve.wait_ge(sem("scores_read"), u + 1)
                    dve.scalar_tensor_tensor(out=row_max[:, u % 3, :], in0=m, scalar=-1.0, in1=rq[:, 0, :, h], op0=ALU.mult,
                                             op1=ALU.mult).then_inc(sem("max_ready"), 1)
                    return
                if x["kind"] == "diff":
                    if u == U_DIFF:
                        dve.wait_ge(sem("bias_ready"), 1)
                    for t in range(2):
                        ins = dve.scalar_tensor_tensor(out=s[:, t], in0=src[:, t], scalar=rq[:, 1, t, 2 * h + x["map"]:2 * h + x["map"] + 1],
                                                       in1=bias[:, h, t], op0=ALU.mult, op1=ALU.add)
                elif x["kind"] == "moba":
                    rel = con("rel", at=cst2).rearrange("p (t k) -> p t k", t=2)
                    ins = dve.scalar_tensor_tensor(out=s, in0=rel, scalar=2.0 ** (-8.0 * (h + 1) / MH), in1=src,
                                                   op0=ALU.mult, op1=ALU.add)
                if x["kind"] == "xattn":
                    s = src
                else:
                    ins.then_inc(sem("scores_read"), 1)
                    dve.wait_ge(sem("scores_read"), u + 1)
                step(dve.tensor_reduce(m, s, AX.X, ALU.max))
                dve.tensor_scalar(row_max[:, u % 3, :], m, -1.0, None, ALU.mult).then_inc(sem("max_ready"), 1)

            def inverse(u):
                x, r = units[u], row_inv[:, u % 3, :]
                dve.wait_ge(sem("exp_done"), u + 1)
                ins = dve.reciprocal(r, row_sum[:, u % 3, :])
                if x["kind"] == "diff" and x["map"] == 1:
                    step(ins)
                    ins = dve.tensor_scalar(r, r, lam[:, 7:8], None, ALU.mult)
                ins.then_inc(sem("row_inverse"), 1)

            def combine(u):
                n = units[u]["keys"]
                dve.wait_ge(sem("row_inverse"), u + 1)
                dve.wait_ge(sem("probs_normed"), u)
                for t in range(2):
                    s = scores_sb[:, u % 3, t, 0:n]
                    ins = dve.scalar_tensor_tensor(out=s, in0=s, scalar=row_inv[:, u % 3, t:t + 1], in1=scores_sb[:, (u - 1) % 3, t, 0:n],
                                                   op0=ALU.mult, op1=ALU.add)
                ins.then_inc(sem("probs_normed"), 1)

            def finish(u):
                x, o = units[u], units[u]["out"]
                if o is None or x["kind"] == "diff":
                    return
                rows = slice(64 * (x["head"] % 2), 64 * (x["head"] % 2) + 64)
                k = out_tile(x["kind"], x["head"])
                dve.wait_ge(sem("y_hi"), o + 1)
                dve.tensor_tensor(x_k(1, k, NQ)[rows], ps[rows, out_bank(o), 0:NQ], x_k(0, k, NQ)[rows].bitcast(F32),
                                  ALU.subtract).then_inc(sem("y_ready"), 1)

            def attention(a, b, begun=False):
                before = None
                for s, p, o in walk(a, b):
                    if s is not None and not (begun and s == a):
                        soft_in(s)
                    if before is not None:
                        finish(before)
                    if p is not None:
                        inverse(p)
                        if units[p]["kind"] == "diff" and units[p]["map"] == 1:
                            combine(p)
                    before = o
                    if s == OUT_LO_AT:
                        los(B_OUT + 1)
                finish(before)

            soft_in(U_MLA)
            for t in range(3):
                rows = min(P, NK - P * t)
                dve.wait_ge(sem("dv_turned"), t + 1)
                dve.tensor_copy(v_diff[0:rows, t, :], ps[0:rows, 6 + t % 2, :]).then_inc(sem("dv_ready"), 1)
            attention(U_MLA, U_MOBA, True)
            dve.wait_ge(sem("sub_root"), 1)
            dve.reciprocal(sub_r, sub_r).then_inc(sem("sub_inverse"), 1)

            def sub_lower(h):
                dve.wait_ge(sem("sub_hi"), h + 1)
                dve.tensor_tensor(x_k(1, 4 + h, NQ), xf[:, h * NQ:(h + 1) * NQ], x_k(0, 4 + h, NQ).bitcast(F32), ALU.subtract
                                  ).then_inc(sem("y_ready"), 1)

            dve.wait_ge(sem("y_hi"), HEADS + DH)
            for h in range(DH):
                dve.wait_ge(sem("sub_spread"), h + 1)
                dve.scalar_tensor_tensor(out=xf[:, h * NQ:(h + 1) * NQ], in0=o_diff[:, h, :], scalar=pcol("subln"),
                                         in1=ps[:, 2 + h, 0:NQ], op0=ALU.mult, op1=ALU.mult).then_inc(sem("sub_ready"), 1)
                if h:
                    sub_lower(h - 1)
            sub_lower(DH - 1)

            def add_residual(n, m, dst, src):
                dve.wait_ge(sem("block_used"), n + 1)
                dve.tensor_tensor(dst, ps[:, m % 2, 0:NQ], src, ALU.add).then_inc(sem("bank_free"), 1)

            for k in range(KT):
                los(min(B_OUT + k + 3, B_QUERY))
                add_residual(B_OUT + k, M_OUT + k, res[:, k, :], h_t[:, k, N_META:NK])
            dve.wait_ge(sem("bank_free"), M_QUERY)
            norm(R_PEER, res, "ffn", NQ)

            def top16(src, rest_, vals, idx):
                for half in range(2):
                    at = slice(8 * half, 8 * half + 8)
                    for t in range(2):
                        ins = dve.max(vals(t)[:, at], src(t) if half == 0 else rest_(t))
                    step(ins)
                    for t in range(2):
                        ins = dve.max_index(idx(t)[:, at].bitcast(U32), vals(t)[:, at], src(t) if half == 0 else rest_(t))
                    if half == 0:
                        for t in range(2):
                            ins = dve.match_replace(rest_(t), vals(t)[:, at], src(t), -3.0e38)
                        step(ins)
                return ins

            for j in range(2 * PH):
                dve.wait_ge(sem("key_scores"), j + 1)
                top16(lambda t: ps[:, 2 + j % 2, NKEYS * t:NKEYS * (t + 1)], lambda t: rest[:, t, :],
                      lambda t: top_v[:, t, j, :], lambda t: top_i[:, t, j, :]).then_inc(sem("key_scores_read"), 1)
                if j % 2:
                    h = j // 2
                    dve.wait_ge(sem("key_scores_read"), j + 1)
                    for t in range(2):
                        ins = dve.tensor_tensor(cand[:, t, :].rearrange("p (a b) -> p a b", a=TOPK),
                                                top_v[:, t, j - 1, :].unsqueeze(2).to_broadcast([P, TOPK, TOPK]),
                                                top_v[:, t, j, :].unsqueeze(1).to_broadcast([P, TOPK, TOPK]), ALU.add)
                    step(ins)
                    step(top16(lambda t: cand[:, t, :], lambda t: cand_rest[:, t, :],
                               lambda t: best[:, t, h, :], lambda t: flat[:, t, h, :]))
            dve.tensor_tensor(soft_hk, best_hk, best_hk[:, :, 0:1].to_broadcast([P, 2 * PH, TOPK]), ALU.subtract
                              ).then_inc(sem("soft_in"), 1)
            step(dve.tensor_scalar(ab_u0, flat_u, 4, None, ALU.logical_shift_right))
            step(dve.tensor_scalar(ab_u1, flat_u, 15, None, ALU.bitwise_and))
            step(dve.tensor_copy(ab_f_flat, ab_u_flat))
            step(dve.tensor_copy(top_f.rearrange("p a b c -> p (a b c)"), top_i.rearrange("p a b c -> p (a b c)").bitcast(U32)))
            iota16 = con("iota")[:, 0:TOPK].unsqueeze(1).to_broadcast([P, PH * TOPK, TOPK])
            for half in range(2):
                for t in range(2):
                    hits = hit.rearrange("p a b c -> p (a b) c")
                    step(dve.tensor_tensor(hits, ab_f[:, half, t].rearrange("p a b -> p (a b)").unsqueeze(2).to_broadcast(
                        [P, PH * TOPK, TOPK]), iota16, ALU.is_equal))
                    step(dve.tensor_tensor(hit, hit, top_f[:, t, half:2 * PH:2, :].unsqueeze(2).to_broadcast(
                        [P, PH, TOPK, TOPK]), ALU.mult))
                    ins = dve.tensor_reduce(expert[:, half, t].rearrange("p a b -> p (a b)"), hits, AX.X, ALU.add)
                    step(ins)
            dve.wait_ge(sem("soft_exp"), 1)
            step(dve.tensor_reduce(soft_s.rearrange("p a b -> p (a b)"), soft_hk, AX.X, ALU.add))
            step(dve.reciprocal(soft_s.rearrange("p a b -> p (a b)"), soft_s.rearrange("p a b -> p (a b)")))
            dve.tensor_tensor(soft_hk, soft_hk, soft_s.rearrange("p a b -> p (a b)").unsqueeze(2).to_broadcast(
                [P, 2 * PH, TOPK]), ALU.mult).then_inc(sem("route_ready"), 1)
            dve.wait_ge(sem("route_t_ready"), 3)

            def one_hot(g, j, tok):
                dve.tensor_scalar(one1[:, g, j, :], con("iota"), route_t[:, 0, tok], None, ALU.is_equal)
                return dve.tensor_scalar(one2[:, g, j, :], con("iota"), route_t[:, 1, tok], route_t[:, 2, tok],
                                         ALU.is_equal, ALU.mult)

            for g in range(2):
                for j in range(4):
                    ins = one_hot(g, j, slice(4 * g + j, 4 * g + j + 1))
                ins.then_inc(sem("one_hot_ready"), 1)
            with dve.Fori(1, NQ // 8) as i:
                for g in range(2):
                    dve.wait_ge(sem("g_product"), 2 * i + (g - 1))
                    for j in range(4):
                        ins = one_hot(g, j, bass.ds(8 * i + (4 * g + j), 1))
                    ins.then_inc(sem("one_hot_ready"), 1)

            def split(c, a, chunk):
                b = c.mod(2)
                dve.tensor_tensor(hf[:, b, :], a, G[:, :, bass.ds(chunk.value(), 1)].rearrange("p t e -> p (t e)"),
                                  ALU.mult).then_inc(sem("act_used"), 1)
                dve.wait_ge(sem("act_used"), c.plus(1).value())
                if c.first >= 2:
                    n = B_V + c.first - 1 if c.first < EARLY + 2 else B_PEER + 2 * (c.first - EARLY) - 1
                    dve.wait_ge(sem("block_used"), c.value(n, c.stride if c.first < EARLY else 2 * c.stride))
                dve.tensor_copy(h_op[:, b, 0, :], hf[:, b, :]).then_inc(sem("act_hi"), 1)
                dve.wait_ge(sem("act_hi"), c.plus(1).value())
                dve.tensor_tensor(h_op[:, b, 1, :], hf[:, b, :], h_op[:, b, 0, :].bitcast(F32), ALU.subtract
                                  ).then_inc(sem("acts_ready"), 1)

            def early(c):
                if c.first < RING:
                    split(c, a_out[:, c.mod(RING), :], c.plus(EARLY - RING))
                else:
                    dve.wait_ge(sem(f"early_loaded{c.mod(RING)}"), c.div(RING) * 16)
                    split(c, a_in[:, c.mod(RING), :], c.plus(-RING))
                n = At(B_V + 2 + c.first, c.i, c.stride)
                if lo_owner(n.first) == "dve":
                    lo(n)

            def chunk(d):
                dve.wait_ge(sem("gelu_done"), d.plus(1).value())
                split(d.plus(EARLY), ge[:, d.mod(2), :], d.plus(EARLY))

            los(B_V + 2)
            dve.wait_ge(sem("g_ready"), NQ // 4)
            for c in range(RING):
                dve.wait_ge(sem("bank_free"), M_PEER - RING + 1 + c)
                early(At(c))
            with dve.Fori(0, EARLY // RING - 1) as i:
                for j in range(RING):
                    early(At(RING + j, i, RING))
            ahead[0] = B_PEER + 2
            los(B_PEER + 3)
            for d in range(2):
                chunk(At(d))
                lo(At(B_PEER + 4 + 2 * d))
            with dve.Fori(0, (NKEYS - EARLY - 4) // 2) as i:
                for d in range(2):
                    chunk(At(2 + d, i, 2))
                    lo(At(B_PEER + 8 + 2 * d, i, 4))
            ahead[0] = B_IN2 - 1
            chunk(At(NKEYS - EARLY - 2))
            los(B_IN2)
            chunk(At(NKEYS - EARLY - 1))

            def add_sum(r):
                for b in range(4):
                    if b < 3:
                        dve.wait_ge(sem("sum_ready"), 3 * r + b + 1)
                    else:
                        dve.wait_ge(sem("block_used"), (B_IN2, N_BLOCKS)[r])
                    two = flat2(res[:, 2 * b:2 * b + 2, :])
                    dve.tensor_tensor(two, ps[:, 4 + b, :], two, ALU.add).then_inc(sem("res_ready"), 1)
                    if r == 0 and b:
                        gained_lo(R_MIX, "mix", range(2 * b - 2, 2 * b))

            los(B_IN2 + 2)
            add_sum(0)
            gained_lo(R_MIX, "mix", range(KT - 2, KT))
            inverse_root(R_MIX)

            def evacuate_in2(j):
                while at_in2[0] <= j:
                    k = at_in2[0]
                    los(B_IN2 + k + 3)
                    tile = IN2_ORDER[k]
                    dve.wait_ge(sem("block_used"), B_IN2 + k + 1)
                    dve.scalar_tensor_tensor(out=proj2[:, tile, :], in0=ps[:, (M_IN2 + k) % 2, 0:NQ],
                                             scalar=0.125 if 6 <= tile < 10 else 1.0, in1=rb[:, 0:NQ], op0=ALU.mult, op1=ALU.mult
                                             ).then_inc(sem("bank_free"), 1)
                    at_in2[0] += 1

            at_in2 = [0]
            evacuate_in2(3)
            dve.wait_ge(sem("gate_ln"), 1)
            step(dve.tensor_scalar(z, z, 0.0, None, ALU.min))
            step(dve.tensor_tensor(log_a, z, z2, ALU.subtract))
            step(dve.tensor_scalar(log_a, log_a, 1.0 / 16, None, ALU.mult))
            for n in range(NCH):
                c = slice(CHUNK * n, CHUNK * n + CHUNK)
                ins = dve.tensor_tensor_scan(csum[:, c], ones[:, 0:CHUNK], log_a[:, c], 0.0, ALU.mult, ALU.add)
            ins.then_inc(sem("csum_ready"), 1)
            evacuate_in2(4)
            dve.wait_ge(sem("gla_exp"), 2)
            dve.wait_ge(sem("bank_free"), M_IN2 + 3)
            dve.scalar_tensor_tensor(out=qd, in0=proj2[:, 18, :], scalar=GDK ** -0.5, in1=e_pos, op0=ALU.mult, op1=ALU.mult)
            dve.tensor_tensor(kd, proj2[:, 19, :], e_neg, ALU.mult).then_inc(sem("gla_qk"), 1)
            dve.wait_ge(sem("gla_exp"), 3)
            dve.tensor_tensor(e_end, e_end, proj2[:, 19, :], ALU.mult).then_inc(sem("gla_end"), 1)
            step(dve.memset(state[:, 0, :], 0.0))
            evacuate_in2(7)
            dve.wait_ge(sem("gla_scores"), 1)
            dve.wait_ge(sem("cst2_loaded"), 32)
            dve.tensor_tensor(a_gla.rearrange("p h n c -> p h (n c)").rearrange("p h (n c) -> p h n c", n=NCH),
                              ps[0:CHUNK, 4:8, 0:NQ].rearrange("p h (n c) -> p h n c", n=NCH),
                              con("gmask", CHUNK, cst2).unsqueeze(1).unsqueeze(1).to_broadcast([CHUNK, GH, NCH, CHUNK]),
                              ALU.mult).then_inc(sem("gla_a"), 1)
            for n in range(NCH - 1):
                dve.wait_ge(sem("gla_update"), n + 1)
                step(dve.tensor_tensor(upd[:, n, :], ps[:, 2 + n % 2, 0:256], con("gblk", at=cst2), ALU.mult))
                ins = dve.scalar_tensor_tensor(out=state[:, n + 1, :], in0=state[:, n, :], scalar=decay[:, n:n + 1],
                                               in1=upd[:, n, :], op0=ALU.mult, op1=ALU.add)
                ins.then_inc(sem("gla_state"), 1)
                dve.wait_ge(sem("gla_state"), n + 1)
                if n == 1:
                    evacuate_in2(8)
            evacuate_in2(11)
            for t in range(2):
                dve.wait_ge(sem("mv_turned"), t + 1)
                dve.tensor_copy(v_moba[:, t, :], ps[:, 6 + t, :]).then_inc(sem("mv_ready"), 1)
            evacuate_in2(12)
            dve.wait_ge(sem("gla_root"), 1)
            for t in range(2):
                step(dve.reciprocal(acc_sb[:, NQ * t:NQ * (t + 1)], acc_sb[:, NQ * t:NQ * (t + 1)]))
                evacuate_in2(13 + t)
            dve.wait_ge(sem("gla_o"), 1)
            step(dve.scalar_tensor_tensor(out=flat2(y_gla), in0=flat2(o_gla), scalar=pcol("gla"), in1=acc_sb[:, 0:512],
                                          op0=ALU.mult, op1=ALU.mult))
            dve.wait_ge(sem("silu_ready"), 1)
            dve.tensor_tensor(flat2(y_gla), flat2(y_gla), flat2(silu_o), ALU.mult).then_inc(sem("mix_ready"), 1)
            evacuate_in2(16)
            dve.wait_ge(sem("bank_free"), M_IN2 + 17)
            step(dve.tensor_tensor(flat2(conv_u), flat2(proj2[:, 2:4, :]), flat2(proj2[:, 4:6, :]), ALU.mult))
            for t in range(2):
                w = [pcol("scw", 3 * t + j) for j in range(3)]
                step(dve.tensor_scalar(conv_y[:, t, :], conv_u[:, t, :], w[2], pcol("scb", t), ALU.mult, ALU.add))
                for back in (1, 2):
                    step(dve.scalar_tensor_tensor(out=conv_y[:, t, back:NQ], in0=conv_u[:, t, 0:NQ - back], scalar=w[2 - back],
                                                  in1=conv_y[:, t, back:NQ], op0=ALU.mult, op1=ALU.add))
                evacuate_in2(17 + t)
            dve.tensor_tensor(flat2(conv_y), flat2(conv_y), flat2(proj2[:, 0:2, :]), ALU.mult).then_inc(sem("mix_ready"), 1)
            evacuate_in2(21)
            soft_in(U_MOBA)
            evacuate_in2(24)
            los(B_OUT2 + 2)
            for w, (src, a) in enumerate(((conv_y, 0), (y_gla, 6))):
                dve.wait_ge(sem("mix_hi"), w + 1)
                dve.tensor_tensor(x_op[:, 1, a * NQ:(a + 2) * NQ], flat2(src), x_op[:, 0, a * NQ:(a + 2) * NQ].bitcast(F32),
                                  ALU.subtract).then_inc(sem("mix_lo"), 1)
            attention(U_MOBA, U_X, True)
            for k in range(KT):
                los(B_OUT2 + k + 3)
                add_residual(B_OUT2 + k, M_OUT2 + k, res[:, k, :], res[:, k, :])
            dve.wait_ge(sem("bank_free"), M_XQ)
            gained_lo(R_XATTN, "xattn")
            los(B_XQ + 2)
            inverse_root(R_XATTN)
            for j in range(2):
                dve.wait_ge(sem("block_used"), B_XQ + j + 1)
                dve.scalar_tensor_tensor(out=q_x[:, j, :], in0=ps[:, (M_XQ + j) % 2, 0:NQ], scalar=0.125, in1=rb[:, 0:NQ],
                                         op0=ALU.mult, op1=ALU.mult).then_inc(sem("bank_free"), 1)
                los(B_XQ + j + 3)
            attention(U_X, U_END)
            for b in range(2):
                dve.wait_ge(sem("block_used"), B_XO + b + 1)
                four = flat2(res[:, 4 * b:4 * b + 4, :])
                dve.tensor_tensor(four, banks(2 + 2 * b, 2), four, ALU.add).then_inc(sem("bank_free"), 1)
                los(B_FFN + 1)
                dve.wait_ge(sem("bank_free"), M_XO + b + 1)
                gained_lo(R_FFN, "ffn2", range(4 * b, 4 * b + 4))
            los(B_FFN + 2)
            inverse_root(R_FFN)

            def scale(p, half):
                done = B_FFN + 1 + half if p.first == 0 else B_FFN + 3 * p.first + half
                dve.wait_ge(sem("block_used"), p.value(done, 3 * p.stride))
                dve.tensor_tensor(up_out[:, half, p.mod(2), :], ps[:, half, 0:NQ], rb[:, 0:NQ], ALU.mult
                                  ).then_inc(sem("bank_free"), 1)

            def conv(p):
                for half, buf in enumerate((conv_a, conv_g)):
                    dve.wait_ge(sem("tap_done"), p.value(2 * p.first + half + 1, 2 * p.stride))
                    for back, done in ((1, "conv_step"), (2, "conv_done")):
                        a = PARAMS["cw"][0] + 3 * half + 2 - back
                        dve.scalar_tensor_tensor(out=buf[:, p.mod(2), back:NQ], in0=up_out[:, half, p.mod(2), 0:NQ - back],
                                                 scalar=par[:, bass.ds(p.value(a + 6 * p.first, 6 * p.stride), 1)],
                                                 in1=buf[:, p.mod(2), back:NQ], op0=ALU.mult, op1=ALU.add
                                                 ).then_inc(sem(done), 1)
                        if back == 1:
                            dve.wait_ge(sem("conv_step"), p.value(2 * p.first + half + 1, 2 * p.stride))

            def gate(p):
                b = p.mod(2)
                dve.wait_ge(sem("conv_done"), p.value(2 * p.first + 2, 2 * p.stride))
                dve.wait_ge(sem("silu_done"), p.plus(1).value())
                dve.tensor_tensor(hf[:, b, :], act_a[:, b, :], conv_g[:, b, :], ALU.mult).then_inc(sem("act_used"), 1)
                dve.wait_ge(sem("act_used"), p.value(NKEYS + p.first + 1))
                if p.first >= 2:
                    dve.wait_ge(sem("block_used"), p.value(B_FFN + 3 * (p.first - 2) + 5, 3 * p.stride))
                dve.tensor_copy(h_op[:, b, 0, :], hf[:, b, :]).then_inc(sem("act_hi"), 1)
                dve.wait_ge(sem("act_hi"), p.value(NKEYS + p.first + 1))
                dve.tensor_tensor(h_op[:, b, 1, :], hf[:, b, :], h_op[:, b, 0, :].bitcast(F32), ALU.subtract
                                  ).then_inc(sem("acts_ready"), 1)

            def tile(p):
                n = At(B_FFN + 3 * p.first + 3, p.i, 3 * p.stride)
                scale(p, 0)
                if n.mod(2):
                    lo(n)
                scale(p, 1)
                conv(p)
                if n.plus(1).mod(2):
                    lo(n.plus(1))
                gate(p)
                if n.plus(2).mod(2):
                    lo(n.plus(2))

            los(B_FFN + 3)
            tile(At(0))
            with dve.Fori(0, (FT - 2) // 4) as i:
                for j in range(4):
                    tile(At(1 + j, i, 4))
            for half in range(2):
                scale(At(FT - 1), half)
            conv(At(FT - 1))
            gate(At(FT - 1))
            add_sum(1)
            norm(R_FINAL, res, "final", NQ, operand=False)

        @block.tensor
        def _(pe):
            def parts(s, wa, wb, k_hi, k_lo):
                return ((w_hi[:, s, wa:wb], k_hi), (w_hi[:, s, wa:wb], k_lo), (w_lo[:, s, wa:wb], k_hi))

            def arrived(n):
                pe.wait_ge(*rest_taken(n))

            def project(n, m_bank, T=NQ, free=None, ready=None, tiles=range(KT), last=KT - 1):
                if 0 in tiles:
                    arrived(n)
                    if free is not None:
                        pe.wait_ge(*free)
                for k in tiles:
                    if ready is not None and ready(k) is not None:
                        pe.wait_ge(*ready(k))
                    for j, (w, x) in enumerate(parts(n.mod(RING), k * P, k * P + P, x_k(0, k, T), x_k(1, k, T))):
                        mm = pe.matmul(ps[:, m_bank, 0:T], w, x, start=(k == 0 and j == 0), stop=(k == last and j == 2))
                if last in tiles:
                    mm.then_inc(sem("block_used"), 1)

            def bank_free(m):
                return (sem("bank_free"), m - 1) if m >= 2 else None

            def projections(n, m, count, T=NQ, ready=None):
                for j in range(count):
                    project(At(n + j), (m + j) % 2, T, bank_free(m + j), ready if j == 0 else None)

            def norm_sum(r, k, T, bank=2):
                pe.wait_ge(sem("rms_squares"), KT * r + k + 1)
                mm = pe.matmul(ps[:, bank, 0:T], ones[:, :], sq[:, k * T:(k + 1) * T], start=(k == 0), stop=(k == KT - 1))
                if k == KT - 1:
                    mm.then_inc(sem("rms_sum"), 1)

            def norm(r, T, bank=2):
                for k in range(KT):
                    norm_sum(r, k, T, bank)

            def operand(r):
                return lambda k: (sem("x_odd" if k % 2 else "x_even"), KT // 2 * (operands(r) - 1) + k // 2 + 1)

            def mixed(n, m, r, begun):
                projections(n + begun, m + begun, KT - begun)
                pe.wait_ge(sem("squares_added"), KT - 2 if r == R_PEER else 2 * (KT - 2))
                pe.matmul(ps[:, 2, 0:NQ], ones[:, :], sq[:, 0:NQ], start=True, stop=False)
                pe.wait_ge(sem("rms_squares"), KT * (r + 1))
                pe.matmul(ps[:, 2, 0:NQ], ones[:, :], sq[:, (KT - 1) * NQ:KT * NQ], start=False, stop=True
                          ).then_inc(sem("rms_sum"), 1)

            def spread(b, stationary, src, n, rows=P):
                for a in range(0, n, 512):
                    e = min(n, a + 512)
                    mm = pe.matmul(ps[0:rows, b + a // 512, 0:e - a], stationary, src[:, a:e], start=True, stop=True)
                return mm

            pe.wait_ge(sem("ones_set"), 1)
            norm(R_ATTN, NK)

            def project_in(j):
                projections(B_IN + j, M_IN + j, 1, NK, operand(R_ATTN) if j == 0 else None)

            def relative_line(h):
                if h:
                    pe.wait_ge(sem("line_ready"), h)
                for a, e, b in ((0, LINE // 2, 4), (LINE // 2, LINE, 5)):
                    mm = pe.matmul(ps[:, b, 0:e - a], rel_rep[:, h, :], con("bucket", BUCKETS, cst)[:, a:e], start=True, stop=True)
                mm.then_inc(sem("line_done"), 1)

            def latent_sum(w):
                n = (NQ, NK)[w]
                pe.wait_ge(sem("lat_squares"), w + 1)
                for k in range(2):
                    a = w * 2 * NQ + k * n
                    mm = pe.matmul(ps[:, 2 + w, 0:n], ones[:, :], lat_sq[:, a:a + n], start=(k == 0), stop=(k == 1))
                mm.then_inc(sem("lat_sum"), 1)

            def values(t):
                rows = min(P, NK - P * t)
                if t == 2:
                    pe.wait_ge(sem("v_ready"), 1)
                for k in range(2):
                    mm = pe.matmul(ps[0:rows, 2 + t % 2, :], ckvn[:, k, P * t:P * t + rows], w_ukv[:, k, 512:1024],
                                   start=(k == 0), stop=(k == 1))
                mm.then_inc(sem("v_product"), 1)

            def keys(w):
                for h in range(4):
                    for k in range(2):
                        a = NOPE * (4 * w + h)
                        mm = pe.matmul(ps[0:NOPE, 4 + h, 0:NK], w_ukv[:, k, a:a + NOPE], ckvn[:, k, :], start=(k == 0), stop=(k == 1))
                mm.then_inc(sem("k_product"), 1)

            def key_spread(w):
                for h in range(4):
                    a = QK * (4 * w + h)
                    mm = pe.matmul(ps[0:QK, 4 + h, 0:NK], head_of[:, a:a + QK], rk[:, 0, :], start=True, stop=True)
                mm.then_inc(sem("k_spread"), 1)

            project_in(0)
            pe.wait_ge(sem("rel_ready"), 1)
            pe.wait_ge(sem("cst_loaded"), 16)
            relative_line(0)
            project_in(1)
            relative_line(1)
            norm(R_MEM, NQ, bank=3)
            project_in(2)
            relative_line(2)
            latent_sum(0)
            project_in(3)
            relative_line(3)
            project_in(4)
            pe.wait_ge(sem("rms_root"), R_MEM + 1)
            latent_sum(1)
            pe.wait_ge(sem("wu_loaded"), 32)
            pe.wait_ge(sem("lat_ready"), 1)
            pe.wait_ge(sem("line_ready"), DH)
            for h in range(HEADS):
                for k in range(2):
                    mm = pe.matmul(ps[0:QK, 4 + h // 2, (h % 2) * NQ:(h % 2 + 1) * NQ], w_uq[:, k, QK * h:QK * h + QK],
                                   cqn[:, k, :], start=(k == 0), stop=(k == 1))
            mm.then_inc(sem("q_product"), 1)
            project_in(5)
            project_in(6)
            pe.wait_ge(sem("lat_ready"), 2)
            values(0)
            values(1)
            project_in(7)
            pe.wait_ge(sem("q_squares"), 1)
            spread(4, con("rot", QK, cst), flat2(q_mla), HEADS * NQ, QK).then_inc(sem("qk_turned"), 1)
            project_in(8)
            values(2)
            project_in(9)
            pe.wait_ge(sem("qk_turned_read"), 1)
            keys(0)
            project_in(10)
            pe.wait_ge(sem("k_raw"), 1)
            keys(1)
            project_in(11)
            pe.wait_ge(sem("v_ready"), 3)
            pe.matmul(ps[0:QK, 2, 0:NK], con("rot", QK, cst)[NOPE:QK], rope_k, start=True, stop=True).then_inc(sem("qk_turned"), 1)
            pe.wait_ge(sem("k_raw"), 2)
            pe.wait_ge(sem("windows_set"), 1)
            pe.matmul(ps[0:8, 3, 0:NK], ones[NOPE:QK, 0:8], rope_sq, start=True, stop=False)
            for h in range(HEADS):
                mm = pe.matmul(ps[0:8, 3, 0:NK], one_in[0:NOPE, 7 - h:15 - h], sq[0:NOPE, h * NK:(h + 1) * NK],
                               start=False, stop=(h == HEADS - 1))
            mm.then_inc(sem("k_sum"), 1)
            project_in(12)
            pe.wait_ge(sem("qk_turned_read"), 2)
            pe.wait_ge(sem("bank_free"), M_IN + 9)
            for t in range(2):
                for h in range(HEADS):
                    a = h * NQ + P * t
                    pe.matmul(ps[:, 2, 8 * t + h:8 * t + h + 1], xf[0:QK, a:a + P], ones[0:QK, 0:1], start=True, stop=True)
                for h in range(DH):
                    a = 16 + 8 * t + 2 * h
                    mm = pe.matmul(ps[:, 2, a:a + 2], dq_sq[:, h, P * t:P * t + P], two_in[:, 6:8], start=True, stop=True)
            mm.then_inc(sem("q_sum"), 1)
            project_in(13)
            pe.wait_ge(sem("heads_set"), 1)
            pe.wait_ge(sem("k_inverse"), 1)
            key_spread(0)
            pe.wait_ge(sem("k_root"), 1)
            pe.wait_ge(sem("bank_free"), M_IN + 13)
            for h in range(DH):
                mm = pe.matmul(ps[0:8, 3, 0:NK], two_in[:, 6 - 2 * h:14 - 2 * h], dk_sq[:, h, :], start=(h == 0), stop=(h == DH - 1))
            mm.then_inc(sem("k_sum"), 1)
            project_in(14)
            pe.wait_ge(sem("k_ready"), 1)
            key_spread(1)
            project_in(15)
            pe.wait_ge(sem("k_inverse"), 2)
            pe.wait_ge(sem("k_ready"), 2)
            for h in range(DH):
                mm = pe.matmul(ps[:, 4 + h, 0:NK], map_of[:, P * h:P * h + P], rk[:, 1, :], start=True, stop=True)
            mm.then_inc(sem("k_spread"), 1)
            pe.wait_ge(sem("lam_ready"), 1)
            pe.wait_ge(sem("q_root"), 1)
            pe.matmul(ps[:, 2, 0:2], ones[0:64, :], lam[0:64, 0:2], start=True, stop=True).then_inc(sem("lam_sum"), 1)
            project_in(16)
            pe.wait_ge(sem("q_ready"), 1)
            pe.wait_ge(sem("k_ready"), 2)
            pe.wait_ge(sem("lam_exp"), 1)

            def memory(j):
                if j < 4:
                    n = B_MEM + j
                    pe.wait_ge(sem(f"raw_loaded{n % RING}"), 16 * (n // RING) + 16)
                    pe.wait_ge(sem("rms_xf"), KT * (R_MEM + 1))
                    if j and j < 3:
                        pe.wait_ge(sem("memory_out"), j)
                    for k in range(KT):
                        mm = pe.matmul(ps[:, memory_bank(j), 0:NQ], raw[:, n % RING, k * P:k * P + P], mem_t[:, k, :],
                                       start=(k == 0), stop=(k == KT - 1))
                    mm.then_inc(sem("block_used"), 1)
                else:
                    pe.wait_ge(sem("memory_out"), 4)
                    for t in range(2):
                        for f in range(2):
                            a = (2 * t + f) * P
                            mm = pe.transpose(ps[:, memory_bank(j), a:a + P], v_mem_t[:, f, t * P:t * P + P], ident)
                    mm.then_inc(sem("v_mem_turned"), 1)

            def scores(u):
                x = units[u]
                h, n, b = x["head"], x["keys"], 2 + 2 * (u % 2)
                if u >= 2:
                    pe.wait_ge(sem("exp_done" if units[u - 2]["kind"] == "xattn" else "scores_read"), u - 1)
                for t in range(2):
                    c = slice(P * t, P * t + P)
                    half = slice(64 * (h % 2), 64 * (h % 2) + 64)
                    if x["kind"] == "mla":
                        q, k = q_mla[:, h, c], k_mla[:, h, :]
                    elif x["kind"] == "diff":
                        half = slice(64 * x["map"], 64 * x["map"] + 64)
                        q, k = dqn[half, h, c], dkn[half, h, :]
                    elif x["kind"] == "moba":
                        q, k = proj2[half, 6 + h // 2, c], proj2[half, 10 + h // 2, :]
                    else:
                        q, k = q_x[half, h // 2, c], kv_x[half, h // 2, :]
                    mm = pe.matmul(ps[:, b + t, 0:n], q, k, start=True, stop=True)
                mm.then_inc(sem("scores_done"), 1)

            def outputs_out(o):
                pe.wait_ge(sem("y_hi"), o - 1)
                pe.wait_ge(sem("y_ready"), outputs_read(o))

            def turn(u):
                o, n = units[u]["out"], units[u]["keys"]
                if o is None:
                    return
                pe.wait_ge(sem("probs_normed"), u + 1)
                if o:
                    pe.wait_ge(sem("probs_ready"), o)
                if o >= 2 and n > NQ:
                    outputs_out(o)
                for t in range(2):
                    for j in range(2):
                        mm = pe.transpose(ps[:, 6, j * NQ + t * P:j * NQ + t * P + P], scores_sb[:, u % 3, t, j * P:j * P + P], ident)
                    if n > NQ:
                        mm = pe.transpose(ps[0:N_META, out_bank(o), NQ + t * P:NQ + t * P + P], scores_sb[:, u % 3, t, NQ:n], ident)
                mm.then_inc(sem("probs_turned"), 1)

            def weigh(u):
                x = units[u]
                o, h, n = x["out"], x["head"], x["keys"]
                if o is None:
                    return
                pe.wait_ge(sem("probs_ready"), o + 1)
                if o >= 2:
                    outputs_out(o)
                rows = slice(0, P) if x["kind"] == "diff" else slice(64 * (h % 2), 64 * (h % 2) + 64)
                tiles = 3 if n > NQ else 2
                for t in range(tiles):
                    k = min(P, n - P * t)
                    if x["kind"] == "mla":
                        v = v_mla[0:k, t, 64 * h:64 * h + 64]
                    elif x["kind"] == "diff":
                        v = v_diff[0:k, t, P * h:P * h + P]
                    elif x["kind"] == "moba":
                        v = v_moba[0:k, t, 64 * h:64 * h + 64]
                    else:
                        v = kv_x[0:k, 2 + t, 64 * h:64 * h + 64]
                    mm = pe.matmul(ps[rows, out_bank(o), 0:NQ], v, probs_t[0:k, o % 2, t, :], start=(t == 0), stop=(t == tiles - 1))
                mm.then_inc(sem("out_done"), 1)

            def sub_sum(h):
                pe.wait_ge(sem("sub_squares"), h + 1)
                mm = pe.matmul(ps[0:8, 0, 0:NQ], pair_in[:, 6 - 2 * h:14 - 2 * h], sq[:, h * NQ:(h + 1) * NQ],
                               start=(h == 0), stop=(h == DH - 1))
                if h == DH - 1:
                    mm.then_inc(sem("sub_sum"), 1)

            def attention(a, b, begun=False, fill=None):
                if not begun:
                    scores(a)
                for s, p, o in walk(a, b):
                    if s is not None and s + 1 < b:
                        scores(s + 1)
                    if s is None and fill is not None:
                        fill(0 if p is not None else 1)
                    if o is not None:
                        weigh(o)
                        if units[o]["kind"] == "diff" and units[o]["out"] is not None and units[o]["head"]:
                            sub_sum(units[o]["head"] - 1)
                    if p is not None:
                        turn(p)
                    if s in MEMORY_AT:
                        memory(MEMORY_AT.index(s))

            scores(U_MLA)
            pe.wait_ge(sem("bank_free"), M_OUT)
            pe.wait_ge(sem("k_ready"), 3)
            for t in range(3):
                rows = min(P, NK - P * t)
                if t == 2:
                    pe.wait_ge(sem("dv_ready"), 1)
                for h in range(DH):
                    mm = pe.transpose(ps[0:rows, 6 + t % 2, h * P:h * P + P], proj[:, 5 + h, P * t:P * t + rows], ident)
                mm.then_inc(sem("dv_turned"), 1)
            pe.wait_ge(sem("dv_ready"), 3)
            attention(U_MLA, U_MOBA, True)
            sub_sum(DH - 1)
            memory(3)
            pe.wait_ge(sem("sub_inverse"), 1)
            for h in range(DH):
                pe.matmul(ps[:, 2 + h, 0:NQ], map_of[:, P * h:P * h + P], sub_r, start=True, stop=True).then_inc(sem("sub_spread"), 1)

            def heads_out(k):
                return (sem("y_ready"), 2 * k + 2 if k < HEADS // 2 else HEADS // 2 + k + 1)

            pe.wait_ge(sem("y_ready"), HEADS)
            for half in (range(KT // 2), range(KT // 2, KT)):
                for j in range(2):
                    project(At(B_OUT + j), (M_OUT + j) % 2, NQ, (sem("bank_free"), M_OUT), heads_out if j == 0 else None, half)
            mixed(B_OUT, M_OUT, R_PEER, 2)
            memory(4)
            def key_scores(j):
                pe.wait_ge(sem("sub_keys_loaded"), 16)
                pe.wait_ge(sem("bank_free"), M_QUERY + 2 * j + 1)
                if j >= 2:
                    pe.wait_ge(sem("key_scores_read"), j - 1)
                for t in range(2):
                    mm = pe.matmul(ps[:, 2 + j % 2, NKEYS * t:NKEYS * (t + 1)], q_peer[:, j, P * t:P * t + P], sub_keys[:, j, :],
                                   start=True, stop=True)
                mm.then_inc(sem("key_scores"), 1)

            for j in range(2 * PH):
                for w in range(2 * j, 2 * j + 2):
                    projections(B_QUERY + w, M_QUERY + w, 1, NQ, operand(R_PEER) if w == 0 else None)
                key_scores(j)
            last = B_BESIDE - B_EARLY - 1
            projections(B_EARLY, M_QUERY + 4 * PH, last)
            pe.wait_ge(sem("route_ready"), 1)
            for w in range(3):
                for t in range(2):
                    src = (expert[:, w, t] if w < 2 else soft[:, t]).rearrange("p a b -> p (a b)")
                    mm = pe.transpose(ps[:, 2 + w, P * t:P * t + P], src, ident)
                mm.then_inc(sem("route_turned"), 1)
            projections(B_EARLY + last, M_QUERY + 4 * PH + last, 1)
            pe.wait_ge(sem("route_t_ready"), 3)

            def beside(i, first=False):
                for j in range(RING):
                    for g in range(2 * j, 2 * j + 2):
                        pe.wait_ge(sem("one_hot_ready"), At(g + 1, i, 8).value())
                        if not first or g >= 2:
                            pe.wait_ge(sem("g_ready"), At(g - 1, i, 8).value())
                        for k in range(4):
                            mm = pe.matmul(ps[:, 2 + g % 2, P * k:P * k + P], one1[:, g % 2, k, :], one2[:, g % 2, k, :],
                                           start=True, stop=True)
                        mm.then_inc(sem("g_product"), 1)
                    m = At(M_PEER - EARLY_G + j, i, RING)
                    project(At(B_BESIDE + j, i, RING), m.mod(2), NQ, (sem("bank_free"), m.plus(-1).value()))

            beside(0, True)
            with pe.Fori(1, EARLY_G // RING) as i:
                beside(i)

            def expand(n, b, first, last):
                s = n.mod(RING)
                for k in range(KT):
                    out = ps[:, 4 + k // 2, (k % 2) * NQ:(k % 2 + 1) * NQ]
                    for j, (w, x) in enumerate(parts(s, P * k, P * k + P, h_op[:, b, 0, :], h_op[:, b, 1, :])):
                        mm = pe.matmul(out, w, x, start=(first and j == 0 and k % 2 == 0), stop=(last and j == 2),
                                       skip_group_check=True)
                    if last and k % 2 and k < KT - 1:
                        mm.then_inc(sem("sum_ready"), 1)
                mm.then_inc(sem("block_used"), 1)

            def early(c):
                n = At(B_V + c.first, c.i, c.stride)
                arrived(n)
                pe.wait_ge(sem("acts_ready"), c.plus(1).value())
                expand(n, c.mod(2), c.first == 0, False)

            def chunk(d):
                n = At(B_PEER + 1 + 2 * d.first, d.i, 2 * d.stride)
                project(n, (d.first + 1) % 2, NQ, (sem("gelu_done"), d.value()) if d.first else None)
                arrived(n.plus(1))
                pe.wait_ge(sem("acts_ready"), d.plus(EARLY + 1).value())
                expand(n.plus(1), d.mod(2), False, False)

            for c in range(RING):
                early(At(c))
            with pe.Fori(0, EARLY // RING - 1) as i:
                for j in range(RING):
                    early(At(RING + j, i, RING))
            pe.wait_ge(sem("bank_free"), M_PEER)
            project(At(B_PEER), 0, NQ)
            for d in range(2):
                chunk(At(d))
            with pe.Fori(0, (NKEYS - EARLY - 4) // 2) as i:
                for d in range(2):
                    chunk(At(2 + d, i, 2))
            chunk(At(NKEYS - EARLY - 2))
            arrived(At(B_IN2 - 1))
            pe.wait_ge(sem("acts_ready"), NKEYS)
            expand(At(B_IN2 - 1), (NKEYS - 1) % 2, False, True)


            def project_in2(j, count=1):
                projections(B_IN2 + j, M_IN2 + j, count, NQ, operand(R_MIX) if j == 0 else None)

            project_in2(0)
            norm(R_MIX, NQ)
            project_in2(1)
            pe.wait_ge(sem("bank_free"), M_IN2 + 1)
            pe.wait_ge(sem("cst2_loaded"), 32)
            pe.matmul(ps[:, 2, 0:NQ], w_gate, proj2[0:16, 24, :], start=True, stop=True).then_inc(sem("gate_product"), 1)
            project_in2(2, 5)
            pe.wait_ge(sem("gate_z"), 1)
            pe.wait_ge(sem("bank_free"), M_IN2 + 5)
            pe.wait_ge(sem("gla_end"), 1)
            for n in range(NCH):
                c = slice(CHUNK * n, CHUNK * n + CHUNK)
                for f in range(2):
                    pe.transpose(banks(2, 2)[0:CHUNK, n * 256 + f * P:n * 256 + f * P + P], proj2[:, 20 + f, c], ident)
                mm = pe.transpose(ps[0:CHUNK, 4, n * P:n * P + P], e_end[:, c], ident)
            mm.then_inc(sem("gla_turned"), 1)
            project_in2(7)
            pe.wait_ge(sem("gla_v"), 2)
            pe.wait_ge(sem("gla_qk"), 1)
            for h in range(GH):
                r = slice(GDK * h, GDK * h + GDK)
                for n in range(NCH):
                    c = slice(CHUNK * n, CHUNK * n + CHUNK)
                    mm = pe.matmul(ps[0:CHUNK, 4 + h, c], kd[r, c], qd[r, c], start=True, stop=True)
            mm.then_inc(sem("gla_scores"), 1)

            def state_update(n):
                pe.matmul(ps[:, 2 + n % 2, 0:256], kend_t[:, n, :], v_gla[:, n, :], start=True, stop=True
                          ).then_inc(sem("gla_update"), 1)

            state_update(0)
            state_update(1)
            project_in2(8)
            pe.wait_ge(sem("gla_state"), 1)
            state_update(2)
            project_in2(9)
            pe.wait_ge(sem("gla_a"), 1)
            pe.wait_ge(sem("gla_state"), NCH - 1)
            for f in range(2):
                for n in range(NCH):
                    c = slice(CHUNK * n, CHUNK * n + CHUNK)
                    pe.matmul(ps[:, 2 + f, c], state[:, n, P * f:P * f + P], qd[:, c], start=True, stop=False,
                              skip_group_check=True)
                    for e in range(2):
                        h = 2 * f + e
                        mm = pe.matmul(ps[GDV * e:GDV * e + GDV, 2 + f, c], v_gla[:, n, GDV * h:GDV * h + GDV],
                                       a_gla[:, h, n, :], start=False, stop=True, skip_group_check=True)
            mm.then_inc(sem("gla_out"), 1)
            project_in2(10)
            pe.wait_ge(sem("gla_squares"), 1)
            spread(4, con("blk64", at=cst2), sq, 2 * NQ).then_inc(sem("gla_sum"), 1)
            project_in2(11)
            pe.wait_ge(sem("bank_free"), M_IN2 + 11)
            for t in range(2):
                for f in range(4):
                    mm = pe.transpose(ps[:, 6 + t, f * P:f * P + P], proj2[:, 14 + f, P * t:P * t + P], ident)
                mm.then_inc(sem("mv_turned"), 1)
            project_in2(12, 10)
            pe.wait_ge(sem("gla_o"), 1)
            pe.wait_ge(sem("gla_root"), 1)
            pe.wait_ge(sem("bank_free"), M_IN2 + 19)
            scores(U_MOBA)
            project_in2(22, 3)
            pe.wait_ge(sem("bank_free"), M_OUT2)
            pe.wait_ge(sem("mv_ready"), 2)

            def first_out2(part):
                pe.wait_ge(sem("mix_lo"), part + 1)
                project(At(B_OUT2), M_OUT2 % 2, tiles=(range(0, 2), range(6, 8))[part], last=None)

            assert M_OUT2 % 2 == 0
            attention(U_MOBA, U_X, True, first_out2)
            pe.wait_ge(sem("y_ready"), HEADS + DH + MH)
            project(At(B_OUT2), M_OUT2 % 2, tiles=range(2, 6), last=5)
            mixed(B_OUT2, M_OUT2, R_XATTN, 1)
            projections(B_XQ, M_XQ, 2, NQ, operand(R_XATTN))
            pe.wait_ge(sem("bank_free"), M_XO)
            pe.wait_ge(sem("kv_back"), 16)

            def cross_out(b, k, tiles=range(4)):
                n = At(B_XO + b)
                if k == 0:
                    arrived(n)
                for f in tiles:
                    a = (2 * f + k) * P
                    for j, (w, x) in enumerate(parts(n.mod(RING), a, a + P, x_k(0, KT - 2 + k, NQ), x_k(1, KT - 2 + k, NQ))):
                        mm = pe.matmul(ps[:, 2 + 2 * b + f // 2, (f % 2) * NQ:(f % 2 + 1) * NQ], w, x,
                                       start=(k == 0 and j == 0 and f % 2 == 0), stop=(k == 1 and j == 2), skip_group_check=True)
                if k == 1:
                    mm.then_inc(sem("block_used"), 1)

            def first_heads(part):
                pe.wait_ge(sem("y_ready"), HEADS + DH + MH + 2)
                cross_out(0, 0, range(2 * part, 2 * part + 2))

            attention(U_X, U_END, False, first_heads)
            cross_out(1, 0)
            pe.wait_ge(sem("y_ready"), HEADS + DH + MH + XH)
            for b in range(2):
                cross_out(b, 1)

            def up(p, n):
                for half in range(2):
                    free = (sem("bank_free"), p.value(M_FFN + 2 * p.first - 1 + half, 2 * p.stride)) if p.first else None
                    if p.first == 0 and half == 0:
                        for tiles in (range(KT // 2), range(KT // 2, KT)):
                            project(n, 0, NQ, None, operand(R_FFN), tiles)
                            for k in tiles:
                                norm_sum(R_FFN, k, NQ)
                    else:
                        project(n.plus(half), half, NQ, free)

            def down(p, n, last=False):
                arrived(n)
                pe.wait_ge(sem("acts_ready"), p.value(NKEYS + p.first + 1))
                expand(n, p.mod(2), p.first == 0, last)

            def tile(p):
                n = At(B_FFN + 2 + 3 * p.first, p.i, 3 * p.stride)
                up(p.plus(1), n)
                down(p, n.plus(2))

            up(At(0), At(B_FFN))
            tile(At(0))
            with pe.Fori(0, (FT - 2) // 4) as i:
                for j in range(4):
                    tile(At(1 + j, i, 4))
            down(At(FT - 1), At(N_BLOCKS - 1), last=True)
            norm(R_FINAL, NQ)


def constants():
    c = np.zeros((P, N_CONSTS), np.float32)

    def put(name, a):
        c[:a.shape[0], CONSTS[name][0]:CONSTS[name][0] + a.shape[1]] = a

    put("ident", np.eye(P, dtype=np.float32))
    put("blk64", np.kron(np.eye(2), np.ones((64, 64))))
    put("iota", np.tile(np.arange(P), (P, 1)))
    half = ROPE // 2
    rot = np.zeros((QK, QK))
    for j in range(half):
        rot[NOPE + half + j, NOPE + j] = -1.0
        rot[NOPE + j, NOPE + half + j] = 1.0
    put("rot", rot)
    freq = np.float32(10000.0) ** (-np.arange(half, dtype=np.float32) / np.float32(half))
    angle = np.arange(NK, dtype=np.float32)[:, None] * freq[None, :]
    cos, sin = np.ones((QK, NK)), np.zeros((QK, NK))
    for j in range(2):
        cos[NOPE + half * j:NOPE + half * (j + 1)] = np.cos(angle).T
        sin[NOPE + half * j:NOPE + half * (j + 1)] = np.sin(angle).T
    put("cos", cos)
    put("sin", sin)
    p = np.arange(P)[:, None, None]
    t = np.arange(2)[None, :, None]
    d = N_META + P * t + p - np.arange(NK)[None, None, :]
    put("mask", np.where(d >= 0, 0.0, NEG).reshape(P, -1))
    n = np.maximum(FAR - np.arange(LINE), 0)
    exact = BUCKETS // 2
    large = exact + (np.log(np.maximum(n, 1).astype(np.float32) / np.float32(exact))
                     / np.float32(math.log(MAX_DIST / exact)) * np.float32(BUCKETS - exact)).astype(np.int32)
    bucket = np.where(n < exact, n, np.minimum(large, BUCKETS - 1))
    put("bucket", (bucket[None, :] == np.arange(BUCKETS)[:, None]).astype(np.float32))
    d = P * t + p - np.arange(NQ)[None, None, :]
    put("rel", np.where(d >= 0, -d, -1e32).reshape(P, -1))
    put("gmask", (np.arange(CHUNK)[:, None] <= np.arange(CHUNK)[None, :]).astype(np.float32))
    put("gblk", (np.arange(P)[:, None] // GDK == np.arange(256)[None, :] // GDV).astype(np.float32))
    return c


def layout(a):
    def lay(name):
        return np.asarray(a[name], np.float32)

    def tiles(w):
        return w.reshape(KT, P, -1, P).transpose(2, 1, 0, 3).reshape(-1, P, D)

    def pad(w, rows, cols):
        out = np.zeros((rows, cols), np.float32)
        out[:w.shape[0], :w.shape[1]] = w
        return out

    def feature_major(x):
        return np.ascontiguousarray(x.T.reshape(KT, P, -1).transpose(1, 0, 2).reshape(P, -1))

    w_in = lay("w_in")[0]
    rope = np.zeros((D, P), np.float32)
    rope[:, NOPE:QK] = w_in[:, 512:544]
    u = lay("peer_u")[0].reshape(NKEYS, NKEYS, KT, P).transpose(1, 3, 2, 0).reshape(NKEYS, P, D)
    v = lay("peer_v")[0].reshape(NKEYS, NKEYS, D).transpose(1, 0, 2)
    up = lay("ffn_w_up_2")[0]
    up_a, up_g = (tiles(pad(up[:, FF * j:FF * (j + 1)], D, FT * P)) for j in range(2))
    down = pad(lay("ffn_w_down_2")[0], FT * P, D).reshape(FT, P, D)
    wo = lay("xattn_wo_2")[0].reshape(2, P, 2, 4, P).transpose(2, 1, 3, 0, 4).reshape(2, P, D)
    query = tiles(lay("peer_w_query")[0])
    early = [w for j in range(2 * PH) for w in (query[j], u[j])] + list(u[2 * PH:EARLY]) + list(v[EARLY - RING:EARLY]) + list(v[:EARLY - RING])
    peer = [u[EARLY]] + [w for c in range(EARLY, NKEYS - 1) for w in (u[c + 1], v[c])] + [v[-1]]
    ffn = [up_a[0], up_g[0]] + [w for t in range(FT - 1) for w in (up_a[t + 1], up_g[t + 1], down[t])] + [down[-1]]
    blocks = np.empty((N_BLOCKS, P, D), np.float32)
    at = 0
    for group in (tiles(np.concatenate([w_in[:, :512], rope, w_in[:, 544:]], axis=1)), tiles(lay("xattn_wkv_2")[0]),
                  tiles(lay("w_out")[0]), early, peer, tiles(pad(lay("w_in_2")[0], D, 25 * P))[IN2_ORDER],
                  tiles(lay("w_out_2")[0]), tiles(lay("xattn_wq_2")[0]), wo, ffn):
        for w in group:
            blocks[at] = w
            at += 1
    assert at == N_BLOCKS

    params = np.zeros((P, N_PARAMS), np.float32)

    def put(name, v, k=0, twice=False):
        v = np.concatenate([v, v]) if twice else v
        n = -(-v.size // P)
        cols = np.zeros(n * P, np.float32)
        cols[:v.size] = v
        params[:, PARAMS[name][0] + k:PARAMS[name][0] + k + n] = cols.reshape(n, P).T

    for name, source in (("attn", "attn_norm"), ("qn", "mla_q_norm"), ("kvn", "mla_kv_norm"), ("qkq", "mla_qk_norm_q"),
                         ("qkk", "mla_qk_norm_k"), ("subln", "diff_subln"), ("ffn", "ffn_norm"), ("mix", "norm_mix_g_2"),
                         ("scb", "sc_conv_b_2"), ("gate_b", "gla_b_gate_2"), ("xattn", "norm_xattn_g_2"),
                         ("mem", "norm_mem_g_2"), ("ffn2", "norm_ffn_g_2")):
        put(name, lay(source)[0])
    put("final", lay("final_norm_g_2"))
    for name, source in (("dq", "diff_q_norm"), ("dk", "diff_k_norm"), ("gla", "gla_norm_g_2")):
        put(name, lay(source)[0], twice=True)
    for k, source in enumerate(("diff_lambda_q1", "diff_lambda_k1", "diff_lambda_q2", "diff_lambda_k2")):
        put("lam", lay(source)[0], k)
    for t in range(2):
        for j in range(3):
            put("scw", lay("sc_conv_w_2")[0, j, P * t:P * t + P], 3 * t + j)
    cw, cb = lay("ffn_conv_w_2")[0], lay("ffn_conv_b_2")[0]
    for half in range(2):
        for t in range(FT):
            f = slice(FF * half + P * t, FF * half + min(P * t + P, FF))
            put("cb", cb[f], 2 * t + half)
            for j in range(3):
                put("cw", cw[j, f], 6 * t + 3 * half + j)

    ukv = lay("mla_w_ukv")[0].reshape(2, P, HEADS, 2, 64).transpose(1, 0, 3, 2, 4).reshape(P, -1)
    return {
        "blocks": blocks,
        "params": params,
        "consts": constants(),
        "h_t": feature_major(np.concatenate([lay("meta_tokens"), lay("x")[0]], axis=0)),
        "mem_t": feature_major(lay("mem_2")[0]),
        "rel_bias": lay("rel_bias"),
        "w_uq": np.ascontiguousarray(lay("mla_w_uq")[0].reshape(2, P, -1).transpose(1, 0, 2).reshape(P, -1)),
        "w_ukv": np.ascontiguousarray(ukv),
        "sub_keys": np.ascontiguousarray(lay("peer_sub_keys")[0].transpose(3, 0, 1, 2).reshape(P, -1)),
        "w_gate": lay("gla_w_gate_2")[0],
    }


def kernel(**inputs):
    import concourse.bacc as bacc
    from concourse.bass_utils import run_bass_kernel_spmd

    nc = bacc.Bacc("TRN2", target_bir_lowering=False, num_devices=1, dynamic_dma_scratch_size=1024)
    arrays = layout(inputs)
    dram = {name: nc.dram_tensor(name, a.shape, F32, kind="ExternalInput").ap() for name, a in arrays.items()}
    dram["out"] = nc.dram_tensor("out", (P, KT * NQ), F32, kind="ExternalOutput").ap()
    build(nc, dram)
    out = run_bass_kernel_spmd(nc, [arrays], core_ids=[0]).results[0]["out"]
    return np.ascontiguousarray(out.reshape(P, KT, NQ).transpose(2, 1, 0).reshape(1, NQ, D))
```
